# Optimizing a Trainium2 kernel written in Bass

```python
import math
import jax, jax.numpy as jnp
from jax import lax
import numpy as np

D_MODEL = 1024
BATCH = 1
SEQ = 256
DEPTH = 2

N_META = 16
D_RNN = D_MODEL
LRU_HEADS = 16
LRU_HEAD_DIM = D_RNN // LRU_HEADS
CONV_A = 4
LRU_C = 8.0
D_CONV = D_MODEL
CONV_B = 3
N_GROUPS = 4
EXPERTS_PER_GROUP = 8
N_EXPERTS = N_GROUPS * EXPERTS_PER_GROUP
TOP_K = 2
D_EXPERT = D_MODEL // 2
BLK = 128
N_MIXERS = 2
N_A_LAYERS = (DEPTH + 1) // 2
N_B_LAYERS = DEPTH // 2
ALPHA = (2.0 * DEPTH) ** 0.25
BETA = (8.0 * DEPTH) ** -0.25
LN_EPS = 1e-5


def layer_norm(x, g, b):
    xf = x.astype(jnp.float32)
    mu = jnp.mean(xf, axis=-1, keepdims=True)
    var = jnp.mean(jnp.square(xf - mu), axis=-1, keepdims=True)
    y = (xf - mu) * lax.rsqrt(var + LN_EPS) * g.astype(jnp.float32) + b.astype(jnp.float32)
    return y.astype(x.dtype)

def causal_depthwise_conv(x, w):
    K, C = w.shape
    return lax.conv_general_dilated(
        x, w[:, None, :].astype(x.dtype), window_strides=(1,), padding=[(K - 1, 0)],
        dimension_numbers=("NWC", "WIO", "NWC"), feature_group_count=C)

def _linear_recurrence_combine(c1, c2):
    a1, b1 = c1
    a2, b2 = c2
    return a1 * a2, a2 * b1 + b2

def rglru_mixer(h, w_in, conv_w, conv_b, w_a, b_a, w_i, b_i, lam, w_out):
    Bsz, S, _ = h.shape
    u = h @ w_in
    y_br = jax.nn.gelu(u[..., :D_RNN])
    xc = causal_depthwise_conv(u[..., D_RNN:], conv_w) + conv_b
    xh = xc.reshape(Bsz, S, LRU_HEADS, LRU_HEAD_DIM)
    r = jax.nn.sigmoid(jnp.einsum("bshd,hde->bshe", xh, w_a).reshape(Bsz, S, D_RNN) + b_a)
    gi = jax.nn.sigmoid(jnp.einsum("bshd,hde->bshe", xh, w_i).reshape(Bsz, S, D_RNN) + b_i)
    log_a = -LRU_C * r.astype(jnp.float32) * jax.nn.softplus(-lam.astype(jnp.float32))
    a = jnp.exp(log_a)
    mult = jnp.sqrt(-jnp.expm1(2.0 * log_a))
    b = mult * (gi * xc).astype(jnp.float32)
    _, hs = lax.associative_scan(_linear_recurrence_combine, (a, b), axis=1)
    return (hs.astype(h.dtype) * y_br) @ w_out

def shortconv_mixer(h, w_in, conv_w, w_out):
    u = h @ w_in
    bg = u[..., :D_CONV]
    cg = u[..., D_CONV:2 * D_CONV]
    v = u[..., 2 * D_CONV:]
    zc = causal_depthwise_conv(cg * v, conv_w)
    return (bg * zc) @ w_out

def hierarchical_moe(h, w_group, b_group, w_expert, b_expert, w_gate, w_up, w_down):
    Bsz, S, D = h.shape
    x2 = h.reshape(Bsz * S, D)
    T = x2.shape[0]
    xf = x2.astype(jnp.float32)
    glog = xf @ w_group.astype(jnp.float32) + b_group.astype(jnp.float32)
    gprob = jax.nn.softmax(glog, axis=-1)
    g = jnp.argmax(glog, axis=-1)
    pg = jnp.take_along_axis(gprob, g[:, None], axis=1)
    elog = (xf @ w_expert.astype(jnp.float32)).reshape(T, N_GROUPS, EXPERTS_PER_GROUP) + b_expert.astype(jnp.float32)
    elog_g = jnp.take_along_axis(elog, g[:, None, None], axis=1)[:, 0]
    vals, loc = lax.top_k(elog_g, TOP_K)
    gates = pg * jax.nn.softmax(vals, axis=-1)
    eid = g[:, None] * EXPERTS_PER_GROUP + loc
    A = T * TOP_K
    eid_f = eid.reshape(-1)
    tok_f = jnp.repeat(jnp.arange(T, dtype=jnp.int32), TOP_K)
    gate_f = gates.reshape(-1)
    order = jnp.argsort(eid_f)
    eid_s = eid_f[order]
    tok_s = tok_f[order]
    gate_s = gate_f[order]
    counts = jnp.bincount(eid_f, length=N_EXPERTS)
    start = jnp.cumsum(counts) - counts
    padded = (counts + BLK - 1) // BLK * BLK
    pend = jnp.cumsum(padded)
    pstart = pend - padded
    rank = jnp.arange(A, dtype=jnp.int32) - start[eid_s]
    dest = pstart[eid_s] + rank
    n_blocks = (A + N_EXPERTS * (BLK - 1) + BLK - 1) // BLK
    P = n_blocks * BLK
    slot_tok = jnp.full((P,), T, dtype=jnp.int32).at[dest].set(tok_s)
    slot_gate = jnp.zeros((P,), jnp.float32).at[dest].set(gate_s)
    block_expert = jnp.clip(jnp.searchsorted(pend, jnp.arange(n_blocks) * BLK, side="right"), 0, N_EXPERTS - 1)
    xpad = jnp.concatenate([x2, jnp.zeros((1, D), x2.dtype)], axis=0)
    xs = xpad[slot_tok].reshape(n_blocks, BLK, D)

    def expert_block(args):
        xb, e = args
        hb = jax.nn.silu(xb @ w_gate[e]) * (xb @ w_up[e])
        return hb @ w_down[e]

    ys = lax.map(expert_block, (xs, block_expert)).reshape(P, D)
    y = jnp.zeros((T + 1, D), x2.dtype).at[slot_tok].add(ys * slot_gate[:, None].astype(ys.dtype))
    return y[:T].reshape(Bsz, S, D)

def first_inputs(seed: int = 0) -> dict:
    key = jax.random.key(seed)
    ks = jax.random.split(key, 24)

    def nrm(k, shape, scale):
        return jax.random.normal(k, shape, jnp.float32) * scale

    u = jax.random.uniform(ks[10], (N_A_LAYERS, D_RNN), jnp.float32, 0.9, 0.999)
    a0 = u ** (1.0 / LRU_C)
    lru_lambda = jnp.log(a0) - jnp.log1p(-a0)
    return {
        "x": nrm(ks[0], (BATCH, SEQ, D_MODEL), 1.0),
        "meta_tokens": nrm(ks[1], (N_META, D_MODEL), 1.0),
        "lru_w_in": nrm(ks[2], (N_A_LAYERS, D_MODEL, 2 * D_RNN), D_MODEL ** -0.5),
        "lru_conv_w": nrm(ks[3], (N_A_LAYERS, CONV_A, D_RNN), CONV_A ** -0.5),
        "lru_conv_b": nrm(ks[4], (N_A_LAYERS, D_RNN), 0.01),
        "lru_w_a": nrm(ks[5], (N_A_LAYERS, LRU_HEADS, LRU_HEAD_DIM, LRU_HEAD_DIM), LRU_HEAD_DIM ** -0.5),
        "lru_b_a": nrm(ks[6], (N_A_LAYERS, D_RNN), 0.01),
        "lru_w_i": nrm(ks[7], (N_A_LAYERS, LRU_HEADS, LRU_HEAD_DIM, LRU_HEAD_DIM), LRU_HEAD_DIM ** -0.5),
        "lru_b_i": nrm(ks[8], (N_A_LAYERS, D_RNN), 0.01),
        "lru_lambda": lru_lambda,
        "lru_w_out": nrm(ks[9], (N_A_LAYERS, D_RNN, D_MODEL), BETA * D_RNN ** -0.5),
        "sc_w_in": nrm(ks[11], (N_B_LAYERS, D_MODEL, 3 * D_CONV), D_MODEL ** -0.5),
        "sc_conv_w": nrm(ks[12], (N_B_LAYERS, CONV_B, D_CONV), CONV_B ** -0.5),
        "sc_w_out": nrm(ks[13], (N_B_LAYERS, D_CONV, D_MODEL), BETA * D_CONV ** -0.5),
        "moe_w_group": nrm(ks[14], (DEPTH, D_MODEL, N_GROUPS), D_MODEL ** -0.5),
        "moe_b_group": nrm(ks[15], (DEPTH, N_GROUPS), 0.01),
        "moe_w_expert": nrm(ks[16], (DEPTH, D_MODEL, N_EXPERTS), D_MODEL ** -0.5),
        "moe_b_expert": nrm(ks[17], (DEPTH, N_GROUPS, EXPERTS_PER_GROUP), 0.01),
        "moe_w_gate": nrm(ks[18], (DEPTH, N_EXPERTS, D_MODEL, D_EXPERT), D_MODEL ** -0.5),
        "moe_w_up": nrm(ks[19], (DEPTH, N_EXPERTS, D_MODEL, D_EXPERT), D_MODEL ** -0.5),
        "moe_w_down": nrm(ks[20], (DEPTH, N_EXPERTS, D_EXPERT, D_MODEL), BETA * D_EXPERT ** -0.5),
        "ln_g": 1.0 + nrm(ks[21], (DEPTH, 2, D_MODEL), 0.02),
        "ln_b": nrm(ks[22], (DEPTH, 2, D_MODEL), 0.02),
    }

def first_block(x, meta_tokens, lru_w_in, lru_conv_w, lru_conv_b, lru_w_a, lru_b_a, lru_w_i, lru_b_i,
              lru_lambda, lru_w_out, sc_w_in, sc_conv_w, sc_w_out, moe_w_group, moe_b_group,
              moe_w_expert, moe_b_expert, moe_w_gate, moe_w_up, moe_w_down, ln_g, ln_b):
    Bsz = x.shape[0]
    meta = jnp.broadcast_to(meta_tokens.astype(x.dtype)[None], (Bsz, N_META, D_MODEL))
    h = jnp.concatenate([meta, x], axis=1)
    for i in range(DEPTH):
        j = i // N_MIXERS
        if i % N_MIXERS == 0:
            mixed = rglru_mixer(h, lru_w_in[j], lru_conv_w[j], lru_conv_b[j], lru_w_a[j], lru_b_a[j],
                                lru_w_i[j], lru_b_i[j], lru_lambda[j], lru_w_out[j])
        else:
            mixed = shortconv_mixer(h, sc_w_in[j], sc_conv_w[j], sc_w_out[j])
        h = layer_norm(ALPHA * h + mixed, ln_g[i, 0], ln_b[i, 0])
        ffn = hierarchical_moe(h, moe_w_group[i], moe_b_group[i], moe_w_expert[i], moe_b_expert[i],
                               moe_w_gate[i], moe_w_up[i], moe_w_down[i])
        h = layer_norm(ALPHA * h + ffn, ln_g[i, 1], ln_b[i, 1])
    return h[:, N_META:]


SSM_GROUP = 16
N_GROUPS_2 = D_MODEL // SSM_GROUP
SSM_STATE = 64
DT_MIN = 1e-3
DT_MAX = 1e-1
N_HEADS = 8
QK_NOPE = 128
QK_ROPE = 64
V_HEAD = 128
Q_LORA = 384
KV_LORA = 256
ROPE_THETA = 10000.0
Q_BLOCK = 128
SM_SCALE = (QK_NOPE + QK_ROPE) ** -0.5
NEG_INF = -1e30
D_FF = 4 * D_MODEL
N_A_LAYERS_2 = DEPTH // 2
N_B_LAYERS_2 = DEPTH - N_A_LAYERS_2
DN_ALPHA = (2 * DEPTH) ** 0.25
DN_BETA = (8 * DEPTH) ** -0.25
RMS_EPS = 1e-6


def layer_norm_2(x, g, b):
    xf = x.astype(jnp.float32)
    mu = jnp.mean(xf, axis=-1, keepdims=True)
    var = jnp.mean(jnp.square(xf - mu), axis=-1, keepdims=True)
    y = (xf - mu) * lax.rsqrt(var + LN_EPS) * g.astype(jnp.float32) + b.astype(jnp.float32)
    return y.astype(x.dtype)

def rms_norm(x, g):
    xf = x.astype(jnp.float32)
    y = xf * lax.rsqrt(jnp.mean(jnp.square(xf), axis=-1, keepdims=True) + RMS_EPS) * g.astype(jnp.float32)
    return y.astype(x.dtype)

def rope_tables(positions):
    half = QK_ROPE // 2
    inv_freq = ROPE_THETA ** (-jnp.arange(half, dtype=jnp.float32) / half)
    ang = positions.astype(jnp.float32)[..., None] * inv_freq
    return jnp.cos(ang), jnp.sin(ang)

def apply_rope(x, cos, sin):
    x1, x2 = jnp.split(x.astype(jnp.float32), 2, axis=-1)
    return jnp.concatenate([x1 * cos - x2 * sin, x1 * sin + x2 * cos], axis=-1).astype(x.dtype)

def _complex_linear_combine(left, right):
    ar_l, ai_l, hr_l, hi_l = left
    ar_r, ai_r, hr_r, hi_r = right
    return (ar_r * ar_l - ai_r * ai_l,
            ar_r * ai_l + ai_r * ar_l,
            ar_r * hr_l - ai_r * hi_l + hr_r,
            ar_r * hi_l + ai_r * hr_l + hi_r)

def s5_mixer(x, lam_re, lam_im, log_dt, b_re, b_im, c_re, c_im, d_skip, w_glu, w_out):
    f32 = jnp.float32
    bsz, seq, _ = x.shape
    u = x.astype(f32).reshape(bsz, seq, N_GROUPS_2, SSM_GROUP)
    lr = lam_re.astype(f32)
    li = lam_im.astype(f32)
    dt = jnp.exp(log_dt.astype(f32))[:, None]
    mag = jnp.exp(lr * dt)
    a_re = mag * jnp.cos(li * dt)
    a_im = mag * jnp.sin(li * dt)
    inv_den = 1.0 / (lr * lr + li * li)
    coef_re = ((a_re - 1.0) * lr + a_im * li) * inv_den
    coef_im = (a_im * lr - (a_re - 1.0) * li) * inv_den
    br = b_re.astype(f32)
    bi = b_im.astype(f32)
    bb_re = coef_re[..., None] * br - coef_im[..., None] * bi
    bb_im = coef_re[..., None] * bi + coef_im[..., None] * br
    bu_re = jnp.einsum('bsgc,gpc->bsgp', u, bb_re)
    bu_im = jnp.einsum('bsgc,gpc->bsgp', u, bb_im)
    shape_a = (1, seq, N_GROUPS_2, SSM_STATE)
    a_re_t = jnp.broadcast_to(a_re, shape_a)
    a_im_t = jnp.broadcast_to(a_im, shape_a)
    _, _, h_re, h_im = lax.associative_scan(
        _complex_linear_combine, (a_re_t, a_im_t, bu_re, bu_im), axis=1)
    y = (jnp.einsum('bsgp,gcp->bsgc', h_re, c_re.astype(f32))
         - jnp.einsum('bsgp,gcp->bsgc', h_im, c_im.astype(f32)))
    y = y + d_skip.astype(f32).reshape(N_GROUPS_2, SSM_GROUP) * u
    y = jax.nn.gelu(y.reshape(bsz, seq, D_MODEL)).astype(x.dtype)
    val, gate = jnp.split(y @ w_glu, 2, axis=-1)
    return (val * jax.nn.sigmoid(gate)) @ w_out

def mla_shared_kv(h, kv_w_a, kv_norm_g, kv_w_b, cos, sin):
    bsz, seq, _ = h.shape
    c_kv, k_rope = jnp.split(h @ kv_w_a, [KV_LORA], axis=-1)
    c_kv = rms_norm(c_kv, kv_norm_g)
    k_rope = apply_rope(k_rope, cos, sin)
    kv = (c_kv @ kv_w_b).reshape(bsz, seq, N_HEADS, QK_NOPE + V_HEAD)
    k_nope, v = jnp.split(kv, [QK_NOPE], axis=-1)
    return k_nope, k_rope, v

def mla_mixer(h, q_w_a, q_norm_g, q_w_b, w_o, k_nope, k_rope, v, cos, sin):
    bsz, seq, _ = h.shape
    c_q = rms_norm(h @ q_w_a, q_norm_g)
    q = (c_q @ q_w_b).reshape(bsz, seq, N_HEADS, QK_NOPE + QK_ROPE)
    q_nope, q_rope = jnp.split(q, [QK_NOPE], axis=-1)
    q_rope = apply_rope(q_rope, cos[:, :, None, :], sin[:, :, None, :])
    n_blocks = seq // Q_BLOCK

    def to_blocks(t):
        return t.reshape(bsz, n_blocks, Q_BLOCK, *t.shape[2:]).swapaxes(0, 1)

    key_pos = jnp.arange(seq)

    def attend_block(args):
        blk, qn, qr = args
        s = (jnp.einsum('bqhd,bkhd->bhqk', qn, k_nope, preferred_element_type=jnp.float32)
             + jnp.einsum('bqhr,bkr->bhqk', qr, k_rope, preferred_element_type=jnp.float32)) * SM_SCALE
        q_pos = blk * Q_BLOCK + jnp.arange(Q_BLOCK)
        s = jnp.where(key_pos[None, :] <= q_pos[:, None], s, NEG_INF)
        p = jax.nn.softmax(s, axis=-1).astype(v.dtype)
        return jnp.einsum('bhqk,bkhd->bqhd', p, v)

    o = lax.map(attend_block, (jnp.arange(n_blocks), to_blocks(q_nope), to_blocks(q_rope)))
    o = o.swapaxes(0, 1).reshape(bsz, seq, N_HEADS * V_HEAD)
    return o @ w_o

def sq_relu_mlp(h, w1, w2):
    return jnp.square(jax.nn.relu(h @ w1)) @ w2

def second_inputs(seed: int = 0) -> dict:
    key = jax.random.key(seed)
    k = jax.random.split(key, 24)
    f32 = jnp.float32

    def nrm(i, shape, scale):
        return jax.random.normal(k[i], shape, f32) * scale

    n_idx = jnp.arange(SSM_STATE, dtype=f32)
    return {
        'x': nrm(0, (BATCH, SEQ, D_MODEL), 1.0),
        'positions': jnp.broadcast_to(jnp.arange(SEQ, dtype=jnp.int32), (BATCH, SEQ)),
        'ln_mix_g': 1.0 + nrm(1, (DEPTH, D_MODEL), 0.02),
        'ln_mix_b': nrm(2, (DEPTH, D_MODEL), 0.02),
        'ln_ffn_g': 1.0 + nrm(3, (DEPTH, D_MODEL), 0.02),
        'ln_ffn_b': nrm(4, (DEPTH, D_MODEL), 0.02),
        'w_ff1': nrm(5, (DEPTH, D_MODEL, D_FF), D_MODEL ** -0.5),
        'w_ff2': nrm(6, (DEPTH, D_FF, D_MODEL), D_FF ** -0.5 * DN_BETA),
        'ssm_lam_re': -0.5 + nrm(7, (N_A_LAYERS_2, N_GROUPS_2, SSM_STATE), 0.01),
        'ssm_lam_im': math.pi * n_idx + nrm(8, (N_A_LAYERS_2, N_GROUPS_2, SSM_STATE), 0.01),
        'ssm_log_dt': jax.random.uniform(k[9], (N_A_LAYERS_2, N_GROUPS_2), f32, math.log(DT_MIN), math.log(DT_MAX)),
        'ssm_b_re': nrm(10, (N_A_LAYERS_2, N_GROUPS_2, SSM_STATE, SSM_GROUP), (2 * SSM_GROUP) ** -0.5),
        'ssm_b_im': nrm(11, (N_A_LAYERS_2, N_GROUPS_2, SSM_STATE, SSM_GROUP), (2 * SSM_GROUP) ** -0.5),
        'ssm_c_re': nrm(12, (N_A_LAYERS_2, N_GROUPS_2, SSM_GROUP, SSM_STATE), SSM_STATE ** -0.5),
        'ssm_c_im': nrm(13, (N_A_LAYERS_2, N_GROUPS_2, SSM_GROUP, SSM_STATE), SSM_STATE ** -0.5),
        'ssm_d': nrm(14, (N_A_LAYERS_2, D_MODEL), 1.0),
        'ssm_w_glu': nrm(15, (N_A_LAYERS_2, D_MODEL, 2 * D_MODEL), D_MODEL ** -0.5),
        'ssm_w_out': nrm(16, (N_A_LAYERS_2, D_MODEL, D_MODEL), D_MODEL ** -0.5 * DN_BETA),
        'kv_w_a': nrm(17, (D_MODEL, KV_LORA + QK_ROPE), D_MODEL ** -0.5),
        'kv_norm_g': 1.0 + nrm(18, (KV_LORA,), 0.02),
        'kv_w_b': nrm(19, (KV_LORA, N_HEADS * (QK_NOPE + V_HEAD)), KV_LORA ** -0.5),
        'q_w_a': nrm(20, (N_B_LAYERS_2, D_MODEL, Q_LORA), D_MODEL ** -0.5),
        'q_norm_g': 1.0 + nrm(21, (N_B_LAYERS_2, Q_LORA), 0.02),
        'q_w_b': nrm(22, (N_B_LAYERS_2, Q_LORA, N_HEADS * (QK_NOPE + QK_ROPE)), Q_LORA ** -0.5),
        'attn_w_o': nrm(23, (N_B_LAYERS_2, N_HEADS * V_HEAD, D_MODEL), (N_HEADS * V_HEAD) ** -0.5 * DN_BETA),
    }

def second_block(x, positions, ln_mix_g, ln_mix_b, ln_ffn_g, ln_ffn_b, w_ff1, w_ff2,
              ssm_lam_re, ssm_lam_im, ssm_log_dt, ssm_b_re, ssm_b_im, ssm_c_re, ssm_c_im,
              ssm_d, ssm_w_glu, ssm_w_out, kv_w_a, kv_norm_g, kv_w_b,
              q_w_a, q_norm_g, q_w_b, attn_w_o):
    cos, sin = rope_tables(positions)
    h = x
    k_nope = k_rope = v = None
    for layer in range(DEPTH):
        if layer < N_A_LAYERS_2:
            i = layer
            mix = s5_mixer(h, ssm_lam_re[i], ssm_lam_im[i], ssm_log_dt[i], ssm_b_re[i], ssm_b_im[i],
                           ssm_c_re[i], ssm_c_im[i], ssm_d[i], ssm_w_glu[i], ssm_w_out[i])
        else:
            if layer == N_A_LAYERS_2:
                k_nope, k_rope, v = mla_shared_kv(h, kv_w_a, kv_norm_g, kv_w_b, cos, sin)
            j = layer - N_A_LAYERS_2
            mix = mla_mixer(h, q_w_a[j], q_norm_g[j], q_w_b[j], attn_w_o[j], k_nope, k_rope, v, cos, sin)
        h = layer_norm_2(DN_ALPHA * h + mix, ln_mix_g[layer], ln_mix_b[layer])
        h = layer_norm_2(DN_ALPHA * h + sq_relu_mlp(h, w_ff1[layer], w_ff2[layer]), ln_ffn_g[layer], ln_ffn_b[layer])
    return h


def setup_inputs(seed=0):
    out = dict(first_inputs(seed))
    for name, value in second_inputs(seed + 1).items():
        if name != "x":
            out[name + "_2"] = value
    return out


def reference(
    x, meta_tokens, lru_w_in, lru_conv_w, lru_conv_b, lru_w_a, lru_b_a, lru_w_i, lru_b_i,
    lru_lambda, lru_w_out, sc_w_in, sc_conv_w, sc_w_out, moe_w_group, moe_b_group, moe_w_expert,
    moe_b_expert, moe_w_gate, moe_w_up, moe_w_down, ln_g, ln_b, positions_2, ln_mix_g_2,
    ln_mix_b_2, ln_ffn_g_2, ln_ffn_b_2, w_ff1_2, w_ff2_2, ssm_lam_re_2, ssm_lam_im_2,
    ssm_log_dt_2, ssm_b_re_2, ssm_b_im_2, ssm_c_re_2, ssm_c_im_2, ssm_d_2, ssm_w_glu_2,
    ssm_w_out_2, kv_w_a_2, kv_norm_g_2, kv_w_b_2, q_w_a_2, q_norm_g_2, q_w_b_2, attn_w_o_2,
):
    x = first_block(
        x, meta_tokens, lru_w_in, lru_conv_w, lru_conv_b, lru_w_a, lru_b_a, lru_w_i, lru_b_i,
        lru_lambda, lru_w_out, sc_w_in, sc_conv_w, sc_w_out, moe_w_group, moe_b_group,
        moe_w_expert, moe_b_expert, moe_w_gate, moe_w_up, moe_w_down, ln_g, ln_b,
    )
    return second_block(
        x, positions_2, ln_mix_g_2, ln_mix_b_2, ln_ffn_g_2, ln_ffn_b_2, w_ff1_2, w_ff2_2,
        ssm_lam_re_2, ssm_lam_im_2, ssm_log_dt_2, ssm_b_re_2, ssm_b_im_2, ssm_c_re_2,
        ssm_c_im_2, ssm_d_2, ssm_w_glu_2, ssm_w_out_2, kv_w_a_2, kv_norm_g_2, kv_w_b_2, q_w_a_2,
        q_norm_g_2, q_w_b_2, attn_w_o_2,
    )


_drawn_inputs = setup_inputs


def setup_inputs(seed=0):
    import zlib

    import numpy as np

    out = dict(_drawn_inputs(seed))
    spreads = {}
    factors = {'lru_conv_b': 3.752,
     'lru_b_a': 8.0,
     'lru_b_i': 8.0,
     'moe_b_group': 8.0,
     'moe_b_expert': 7.02,
     'ssm_lam_re_2': 64.0,
     'ssm_lam_im_2': 45.768,
     'ssm_log_dt_2': 46.848,
     'ssm_b_re_2': 63.936,
     'ssm_b_im_2': 64.0,
     'ssm_c_re_2': 64.0,
     'ssm_c_im_2': 64.0,
     'kv_norm_g_2': 8.0,
     'q_norm_g_2': 8.0}
    for name, (base, spread) in spreads.items():
        noise = np.random.default_rng([zlib.crc32(name.encode()), seed]).standard_normal(out[name].shape)
        drawn = base * np.exp(spread * noise) if base else spread * noise
        out[name] = __import__('jax').numpy.asarray(drawn.astype(out[name].dtype))
    for name, factor in factors.items():
        out[name] = (out[name] * factor).astype(out[name].dtype)
    return out
```

```python
from contextlib import ExitStack
import math

import numpy as np

import concourse.bass as bass
from concourse import mybir

F32 = mybir.dt.float32
I32 = mybir.dt.int32
U32 = mybir.dt.uint32
ALU = mybir.AluOpType
ACT = mybir.ActivationFunctionType
AX = mybir.AxisListType

P = 128
D = 1024
DC = D // P
NMETA = 16
SEQ = 256
T = NMETA + SEQ
BLOCKS = [(0, NMETA), (NMETA, P), (NMETA + P, P)]
ALPHA = 4.0 ** 0.25
LN_EPS = 1e-5
RMS_EPS = 1e-6
NG, EPG = 4, 8
NE = NG * EPG
DE = D // 2
CAP = 32
ROUND_ROWS = NE * CAP
MAX_ROUNDS = -(-T // CAP)
SLOT = 4096
NSLOT = 6
LH, LHD = 16, 64
CONV_A, CONV_B = 4, 3
SG, SC, SS = 64, 16, 64
ST = SG * SS // P
HEADS, NOPE, ROPE, VH = 8, 128, 64, 128
QL, KVL = 384, 256
SM_SCALE = (NOPE + ROPE) ** -0.5
DFF = 4 * D
BIG = 1.0e30
ROUNDER = 1.5 * 2.0 ** 23
TWO_PI = 2.0 * math.pi
PI2_A = 6.28125
PI2_B = float(np.float32(np.round((TWO_PI - PI2_A) * 2.0 ** 21) / 2.0 ** 21))
PI2_C = TWO_PI - PI2_A - PI2_B
PI_IN = 3.1415925


def first_and_second_block(nc, a, out):
    xs_dram = nc.dram_tensor("expert_rows_in", [MAX_ROUNDS * ROUND_ROWS, D], F32).ap()
    ys_dram = nc.dram_tensor("expert_rows_out", [MAX_ROUNDS * ROUND_ROWS, D], F32).ap()
    rot_dram = nc.dram_tensor("s5_rotations", [4, P, SLOT], F32).ap()
    bc_dram = nc.dram_tensor("s5_in_out_maps", [P, SLOT], F32).ap()

    ctx = ExitStack()
    with ctx:
        def sb(name, shape, dt=F32):
            return ctx.enter_context(nc.sbuf_tensor(name, shape, dt))

        ln_blocks = {"mix0": [0, 1, 2], "ffn0": [0, 1, 2], "mix1": [1, 2], "ffn1": [1, 2],
                     "s5": [1, 2], "mlp0": [1, 2], "mla": [1, 2], "mlp1": [1, 2]}
        ln_order = list(ln_blocks)
        shared, base = {}, {}

        def share(kind, counts):
            total = 0
            for name, n in counts:
                shared[name], base[name] = kind, total
                total += n

        for kind in ("var", "sd", "normed"):
            share(kind, [(f"{n}_{kind}", len(b)) for n, b in ln_blocks.items()])
        for kind in ("turned", "hT"):
            share(kind, [(f"x_{kind}", 6)] + [(f"{n}_{kind}", 2 * len(b)) for n, b in ln_blocks.items()])
        share("mixed", [(f"{n}_mixed", len(b)) for n, b in ln_blocks.items() if not n.startswith("ffn")])
        share("piece", [(f"{n}_piece", 7 if n.startswith("mlp") else 1) for n in ln_blocks if not n.startswith("ffn")])
        for kind in ("gate_up", "silu", "hid_ready", "hid_turned", "hidT_ready", "down", "y_ready", "xs_turned", "xT_ready"):
            share(kind, [(f"{kind}{l}", NE) for l in range(2)])
        for b in range(2):
            share(f"y_stored_{b}", [(f"y_stored{l}_{b}", 64 * (NE // 2)) for l in range(2)])
            share(f"xs_loaded_{b}", [(f"xs_loaded{l}_{b}", 16 * (NE // 2)) for l in range(2)])
        for kind in ("logits", "choice", "ranks", "glog", "gexp", "vdiff", "vexp", "slots_ready", "rounds_known"):
            share(kind, [(f"{kind}{l}", 1) for l in range(2)])
        for kind, each in (("masked", 1), ("scattered", 32), ("gathered", 32), ("rowb_free", 1)):
            share(kind, [(f"{kind}{l}", each * (3 - l)) for l in range(2)])
        for kind in ("ff_proj", "ff_relu", "ff_sq"):
            share(kind, [(f"{kind}{l}", DFF // P) for l in range(2)])
        share("dve_constants", [(n, 1) for n in ("par_ready", "lam", "soft", "p_half", "p_theta", "s5_coef", "s5_bb",
                                                 "s5_bb_done", "maps_ready", "angles")])
        share("act_constants", [("lam_exp", 1), ("p_dt", 1), ("p_tanh", 1), ("p_sin", 4), ("s5_ncre", 1), ("a_tab", 3),
                                ("latent_rms", 2), ("ckvT", 1), ("cqT_a", 2), ("cqT", 1)])
        share("pe_constants", [("par_turned", 1), ("s5_coef_turned", 1), ("s5_bb_turned", 1), ("ckv_turned", 1),
                               ("cq_turned", 1), ("qr_turned", 2), ("kr_turned", 1)])
        share("evacuated", [("lru_evac", 16), ("sc_cg_out", 8), ("s5_g", 8), ("glu_sig", 8)])
        share("left_ready", [("lru_z", 8), ("sc_z", 8), ("s5_y", 8), ("glu_done", 8), ("oT", 8)])
        share("gated", [("lru_conv", 8), ("sc_gated", 8), ("s5_rotated", ST)])
        share("projected", [("lru_proj", 16), ("sc_cg", 8), ("glu_proj", 8)])
        share("projected_2", [("lru_gated", 8), ("sc_v", 8), ("s5_bu", ST), ("scores", 2 * HEADS)])
        share("projected_3", [("sc_bg", 8), ("s5_summed", ST), ("weighed", HEADS)])

        sems = {}

        def S(name):
            name = shared.get(name, name)
            if name not in sems:
                sems[name] = nc.alloc_semaphore(name)
            return sems[name]

        def nth(name, count):
            return S(name), base.get(name, 0) + count

        ring = sb("ring", [P, NSLOT, SLOT])
        work = sb("work", [P, 16384])
        hres = sb("hres", [P, 3, D])
        hT = sb("hT", [P, DC, T])
        tmp_a = sb("tmp_a", [P, D])
        rowb = sb("rowb", [P, D])
        multi = sb("multi", [P, 3072])
        ident = sb("ident", [P, P])
        ones = sb("ones", [P, P])
        before = sb("before", [P, P])
        par = sb("par", [P, DC, 12])
        w_route = sb("w_route", [P, 2, DC, NG + NE])
        b_route = sb("b_route", [1, 2, NG + NE])
        iota_e = sb("iota_e", [P, NE])
        marks = sb("marks", [P, MAX_ROUNDS - 1])
        first_rows = sb("first_rows", [P, 1])
        even_odd = sb("even_odd", [P, 2])
        eps_t = sb("eps_t", [P, 3])
        stats = sb("stats", [P, 3, 12])
        mean_var = sb("mean_var", [P, 3, 4])
        gates = sb("gates", [P, 3, 2])
        slots_u = sb("slots_u", [P, 3, 2], U32)
        rounds_i = sb("rounds_i", [1, 2], I32)
        decay = sb("decay", [P, ST])
        phase = sb("phase", [P, 3, ST])
        int_p = sb("int_p", [P, 2], I32)
        ps = ctx.enter_context(nc.psum_tensor("ps", [P, 8, 512], F32))

        tmps = [tmp_a[:, :], multi[:, 2048:3072]]
        gain_bc, bias_bc = multi[:, 0:1024], multi[:, 1024:2048]
        xs_in = [multi[:, 256 * b:256 * b + 256] for b in range(2)]
        xT = [multi[:, 512 + 256 * b:768 + 256 * b].rearrange("p (k s) -> p k s", k=DC) for b in range(2)]
        silu = [multi[:, 1024 + 128 * b:1152 + 128 * b] for b in range(2)]
        hid = [multi[:, 1280 + 128 * b:1408 + 128 * b] for b in range(2)]
        hidT = [multi[:, 1536 + 128 * b:1664 + 128 * b] for b in range(2)]
        y_out = [multi[:, 1792 + 256 * b:2048 + 256 * b] for b in range(2)]

        loaded = [S(f"slot{s}_loaded") for s in range(NSLOT)]

        def cols(w, c0, n):
            return w[:, c0:c0 + n].rearrange("(k p) n -> p k n", p=P)

        def rows(w, r0, n):
            return w[r0:r0 + n, :].rearrange("(k p) n -> p k n", p=P)

        plan = []

        def add(name, source, over):
            plan.append((name, source, over))

        lw, lo = a["lru_w_in"][0], a["lru_w_out"][0]
        for i, (n, c0) in enumerate((("lru_x0", D), ("lru_x1", D + 512), ("lru_y0", 0), ("lru_y1", 512))):
            add(n, cols(lw, c0, 512), ("lru_proj", 4 * i + 4))

        def add_rows(prefix, w, pieces, stage, blocks):
            for j in range(pieces):
                over = (f"{stage}_mixed", blocks) if j == pieces - 1 else (f"{stage}_piece", j + 1)
                add(f"{prefix}{j}", rows(w, 512 * j, 512), over)

        add_rows("lru_out", lo, 2, "mix0", 3)
        add("experts0", None, None)
        sw, so = a["sc_w_in"][0], a["sc_w_out"][0]
        for hf in range(2):
            for n, c0 in (("cg", D), ("v", 2 * D), ("bg", 0)):
                add(f"sc_{n}{hf}", cols(sw, c0 + 512 * hf, 512), (f"sc_{n}", 4 * hf + 4))
        add_rows("sc_out", so, 2, "mix1", 2)
        add("experts1", None, None)
        add("s5_maps", bc_dram, ("s5_summed", ST))
        for t in range(4):
            add(f"s5_rot{t}", rot_dram[t], ("s5_q", 8 * t + 8))
        gw, go = a["ssm_w_glu_2"][0], a["ssm_w_out_2"][0]
        for hf in range(2):
            add(f"glu_v{hf}", cols(gw, 512 * hf, 512), ("glu_proj", 4 * hf + 4))
            add(f"glu_g{hf}", cols(gw, D + 512 * hf, 512), ("glu_proj", 4 * hf + 4))
        add_rows("s5_out", go, 2, "s5", 2)

        def add_mlp(layer):
            for j in range(8):
                add(f"ff1_{layer}_{j}", cols(a["w_ff1_2"][layer], 512 * j, 512), (f"ff_proj{layer}", 4 * j + 4))
            add_rows(f"ff2_{layer}_", a["w_ff2_2"][layer], 8, f"mlp{layer}", 2)

        add_mlp(0)
        add("kv_a", cols(a["kv_w_a_2"], 0, KVL + ROPE), ("latent", 2))
        add("q_a", cols(a["q_w_a_2"][0], 0, QL), ("latent", 4))
        add("kv_b", rows(a["kv_w_b_2"], 0, KVL), ("values", 4))
        for j in range(2):
            add(f"q_b{j}", cols(a["q_w_b_2"][0], 768 * j, 768), ("q_rope", 2))
        add_rows("attn_out", a["attn_w_o_2"][0], 2, "mla", 2)
        add_mlp(1)

        place, turn, at = {}, {}, 0
        expert_at = {}
        turns = [0] * NSLOT
        holder = [None] * NSLOT
        free_when = {}
        for name, _, over in plan:
            if name.startswith("experts"):
                six = [(at + j) % NSLOT for j in range(6)]
                order = []
                for b in range(2):
                    s = six[3 * b:3 * b + 3]
                    if s[0] + 1 == s[1]:
                        order.append((("gate", s[0]), ("up", s[1]), ("down", s[2])))
                    else:
                        order.append((("down", s[0]), ("gate", s[1]), ("up", s[2])))
                expert_at[name] = (order, list(turns))
                free_when[name] = list(holder)
                turns = [t + NE // 2 for t in turns]
                for b in range(2):
                    for kind, s in order[b]:
                        holder[s] = (("down" if kind == "down" else "gate_up") + name[-1], NE - 1 + b)
            else:
                s = at % NSLOT
                place[name], turn[name] = s, turns[s]
                free_when[name], holder[s] = holder[s], over
                turns[s] += 1
                at += 1

        def slot_wait(eng, name):
            eng.wait_ge(loaded[place[name]], 16 * (turn[name] + 1))

        def slot_view(name, k, n):
            return ring[:, place[name], 0:k * n].rearrange("p (k n) -> p k n", k=k)

        def region(start, *shape):
            n = 1
            for x in shape:
                n *= x
            v = work[:, start:start + n]
            if len(shape) == 2:
                return v.rearrange("p (a b) -> p a b", a=shape[0])
            if len(shape) == 3:
                return v.rearrange("p (a b c) -> p a b c", a=shape[0], b=shape[1])
            return v

        PAD_A = CONV_A - 1
        w_gates = region(0, 2, DC, LHD)
        lru_x = region(1024, DC, T + PAD_A)
        lru_c = region(3224, DC, T)
        lru_y = region(5400, DC, T)
        lru_r = region(7576, DC, T)
        lru_i = region(9752, DC, T)
        lru_q = region(11928, DC, T)
        soft = sb("soft", [P, 5, DC])
        TC = SEQ + CONV_B - 1
        sc_cg = [region(260 * b, TC) for b in range(2)]
        sc_cv = [region(520 + 260 * b, TC) for b in range(2)]
        sc_a = region(1040, SEQ)
        sc_z = region(1300, DC, SEQ)
        pre = work[:, 3348:3348 + 24 * 64].rearrange("p (a b) -> p a b", a=24)
        s5_br, s5_bi, s5_t0, s5_t1 = (region(4884 + 1024 * i, 1024) for i in range(4))
        s5_c = region(8980, 2, DC, SS)
        s5_cm = region(10004, 128)
        maps = region(8192 + 4096, 4, DC, P)
        rot = [region(4884 + 2048 * b, 4, 2, SEQ) for b in range(2)]
        rot_k = region(10132, SEQ)
        iota_t = region(11028, SEQ)
        s5_y = region(0, DC, SEQ)
        s5_g = region(2048, DC, SEQ)
        s5_ncre = region(4096, DC, P)
        s5_p1 = [region(5120 + 1024 * b, 2, SEQ) for b in range(2)]
        s5_p2 = [region(5632 + 1024 * b, 2, SEQ) for b in range(2)]
        s5_v = [region(7168 + 512 * b, 2, SEQ) for b in range(2)]
        s5_h = [region(8192 + 512 * b, 2, SEQ) for b in range(2)]
        s5_q1 = [region(9216 + 512 * b, 2, SEQ) for b in range(2)]
        s5_q2 = [region(10240 + 512 * b, 2, SEQ) for b in range(2)]
        s5_sig = [region(11264 + 256 * b, SEQ) for b in range(2)]
        ff = region(0, DFF // P, SEQ)
        qnT = region(0, HEADS, SEQ)
        knT = region(2048, HEADS, SEQ)
        val = region(4096, 2, HEADS * VH)
        qrT = region(6144, HEADS // 2, SEQ)
        krT = region(7168, SEQ)
        oT = region(7424, HEADS, SEQ)
        ckv = region(9472, 2, KVL + ROPE)
        cq = region(10112, 2, QL)
        ckvT = region(10880, KVL // P, SEQ)
        cqT = region(11392, QL // P, SEQ)
        cos_t = region(12160, 2, ROPE // 2)
        sin_t = region(12224, 2, ROPE // 2)
        ang = region(12288, 2, ROPE // 2)
        angk = region(12352, 2, ROPE // 2)
        qr_in = region(12416, HEADS, ROPE)
        qr_rot = region(12928, HEADS, ROPE)
        kr_rot = region(13440, 2, ROPE)
        prob = [region(13568 + 256 * b, SEQ) for b in range(2)]
        probT = [region(14080 + 256 * b, 2, P) for b in range(2)]
        sq_sum = region(14592, 64)
        rope_u = region(14656, 512)
        pos_i = sb("pos_i", [P, 2], I32)
        pos_f = sb("pos_f", [P, 2])
        inv_f = region(15168, ROPE // 2)
        g_kv = region(15200, KVL)
        g_q = region(15456, QL)
        qr_rot_b = [qr_rot, qr_in]
        kr2 = region(15840, 2, 2, ROPE)

        block = ctx.enter_context(nc.Block())

        ln_rows = {
            "mix0": (a["ln_g"][0, 0:1], a["ln_b"][0, 0:1]), "ffn0": (a["ln_g"][0, 1:2], a["ln_b"][0, 1:2]),
            "mix1": (a["ln_g"][1, 0:1], a["ln_b"][1, 0:1]), "ffn1": (a["ln_g"][1, 1:2], a["ln_b"][1, 1:2]),
            "s5": (a["ln_mix_g_2"][0:1], a["ln_mix_b_2"][0:1]), "mlp0": (a["ln_ffn_g_2"][0:1], a["ln_ffn_b_2"][0:1]),
            "mla": (a["ln_mix_g_2"][1:2], a["ln_mix_b_2"][1:2]), "mlp1": (a["ln_ffn_g_2"][1:2], a["ln_ffn_b_2"][1:2]),
        }

        def packed(ap):
            return ap.rearrange("t (p k) -> t k p", k=DC)

        def unpacked(ap):
            return ap.rearrange("t (k p) -> t p k", k=DC)

        def two(ap, k):
            return ap.rearrange("t (a b) -> t a b", b=k)

        @block.sync
        def _(sp):
            def slot_free(when):
                if when:
                    sp.wait_ge(*nth(when[0], when[1]))

            def load_experts(l, name):
                order, before_ = expert_at[name]
                w = {"gate": a["moe_w_gate"][l], "up": a["moe_w_up"][l], "down": a["moe_w_down"][l]}

                def load_pair(e, step, first):
                    for b in range(2):
                        for kind, s in order[b]:
                            src = w[kind][e + b]
                            if kind == "down":
                                src = src.rearrange("(q p) n -> p q n", p=P)
                                dst = ring[:, s, :].rearrange("p (q n) -> p q n", q=4)
                            else:
                                src = src.rearrange("(p k) n -> p (k n)", k=DC)
                                dst = ring[:, s, :]
                            if first:
                                slot_free(free_when[name][s])
                            else:
                                sp.wait_ge(*nth(("down" if kind == "down" else "gate_up") + str(l), step * 2 + (b - 1)))
                            sp.dma_start(dst, src).then_inc(loaded[s], 16)

                load_pair(0, 0, True)
                with sp.Fori(1, NE // 2) as step:
                    load_pair(step * 2, step, False)
                sp.wait_ge(*nth(f"rounds_known{l}", 1))
                rounds = sp.value_load(rounds_i[0:1, l:l + 1], min_val=1, max_val=MAX_ROUNDS)
                with sp.If(rounds > 1):
                    sp.wait_ge(*nth(f"down{l}", NE))
                    with sp.Fori(1, rounds) as r:
                        with sp.Fori(0, NE) as e:
                            n = (r - 1) * NE + e
                            sp.wait_ge(*nth(f"more_ready{l}", n + 1))
                            for kind, s in (("gate", 0), ("up", 1), ("down", 2)):
                                src = w[kind][e]
                                if kind == "down":
                                    src = src.rearrange("(q p) n -> p q n", p=P)
                                    dst = ring[:, s, :].rearrange("p (q n) -> p q n", q=4)
                                else:
                                    src = src.rearrange("(p k) n -> p (k n)", k=DC)
                                    dst = ring[:, s, :]
                                sp.dma_start(dst, src).then_inc(S(f"more_loaded{l}"), 16)
                        sp.wait_ge(*nth(f"more_used{l}", r * NE))
                        sp.sem_inc(S("more_rounds"), 1)
                sp.end_ifs()

            for name, src, _ in plan:
                if name in ("experts0", "experts1"):
                    load_experts(int(name[-1]), name)
                    continue
                s = place[name]
                slot_free(free_when[name])
                if name == "s5_maps":
                    sp.wait_ge(*nth("maps_stored", 16))
                if name.startswith("s5_rot"):
                    for b in range(2):
                        sp.wait_ge(*nth(f"rot_stored{b}", 16 * (int(name[-1]) + 1)))
                n = 1
                for x in src.shape[1:]:
                    n *= x
                dst = ring[:, s, 0:n]
                if len(src.shape) == 3:
                    dst = dst.rearrange("p (k n) -> p k n", k=src.shape[1])
                sp.dma_start(dst, src).then_inc(loaded[s], 16)
            for b in (1, 2):
                sp.wait_ge(*nth("mlp1_normed", b))
                t0 = BLOCKS[b][0] - NMETA
                sp.dma_start(out[0, t0:t0 + P, :], hres[:, b, :]).then_inc(S("stored"), 16)
            sp.wait_ge(*nth("stored", 32))

        @block.gpsimd
        def _(pool):
            step = [0]

            def link(ins):
                step[0] += 1
                ins.then_inc(S("pool_step"), 1)
                pool.wait_ge(*nth("pool_step", step[0]))

            for b, (t0, n) in enumerate(BLOCKS):
                src = a["meta_tokens"] if b == 0 else a["x"][0, t0 - NMETA:t0 - NMETA + n, :]
                pool.dma_start(hres[0:n, b, :], src).then_inc(S(f"x_loaded{b}"), 16)
            link(nc.gpsimd.memset(ident[:, :], 0.0))
            nc.gpsimd.affine_select(out=ident[:, :], in_=ident[:, :], compare_op=ALU.not_equal, fill=1.0,
                                    base=0, pattern=[[-1, P]], channel_multiplier=1).then_inc(S("ident"), 1)
            vec = [(a["lru_conv_w"][0], 4), (a["lru_conv_b"], 1), (a["lru_b_a"], 1), (a["lru_b_i"], 1),
                   (a["lru_lambda"], 1), (a["sc_conv_w"][0], 3), (a["ssm_d_2"], 1)]
            r = 0
            for src, n in vec:
                pool.dma_start(rowb[r:r + n, :], src).then_inc(S("vectors_loaded"), 16)
                r += n
            for i, w in enumerate((a["lru_w_a"][0], a["lru_w_i"][0])):
                for j in range(2):
                    pool.dma_start(w_gates[64 * j:64 * j + 64, i],
                                   w.rearrange("(m j) d e -> j d m e", j=2)[j]).then_inc(S("gates_loaded"), 16)
            for l in range(2):
                pool.dma_start(w_route[:, l, :, 0:NG],
                               a["moe_w_group"][l].rearrange("(p k) n -> p k n", k=DC)).then_inc(S("route_loaded"), 16)
                pool.dma_start(w_route[:, l, :, NG:NG + NE],
                               a["moe_w_expert"][l].rearrange("(p k) n -> p k n", k=DC)).then_inc(S("route_loaded"), 16)
                pool.dma_start(b_route[0:1, l, 0:NG], a["moe_b_group"][l:l + 1, :]).then_inc(S("route_loaded"), 16)
                pool.dma_start(b_route[0:1, l, NG:NG + NE],
                               a["moe_b_expert"][l:l + 1].rearrange("a g e -> a (g e)")).then_inc(S("route_loaded"), 16)
            link(nc.gpsimd.memset(ones[:, :], 1.0))
            nc.gpsimd.affine_select(out=before[:, :], in_=ones[:, :], compare_op=ALU.is_gt, fill=0.0,
                                    base=0, pattern=[[1, P]], channel_multiplier=-1).then_inc(S("consts"), 1)
            nc.gpsimd.affine_select(out=first_rows[:, :], in_=ones[:, 0:1], compare_op=ALU.is_gt, fill=0.0,
                                    base=NMETA, pattern=[[0, 1]], channel_multiplier=-1).then_inc(S("consts"), 1)
            nc.gpsimd.iota(iota_e[:, :], pattern=[[1, NE]], base=0, channel_multiplier=0,
                           allow_small_or_imprecise_dtypes=True).then_inc(S("consts"), 1)
            nc.gpsimd.iota(marks[:, :], pattern=[[CAP, MAX_ROUNDS - 1]], base=CAP, channel_multiplier=0,
                           allow_small_or_imprecise_dtypes=True).then_inc(S("consts"), 1)
            nc.gpsimd.iota(int_p[:, 0:1], pattern=[[0, 1]], base=0, channel_multiplier=1).then_inc(S("consts"), 1)

            def broadcast_rows(n):
                g, b = ln_rows[n]
                i = ln_order.index(n)
                if i > 0:
                    prev = ln_order[i - 1]
                    pool.wait_ge(*nth(f"{prev}_normed", len(ln_blocks[prev])))
                pool.dma_start(gain_bc[0:1, :], g).then_inc(S("rows_loaded"), 16)
                pool.dma_start(bias_bc[0:1, :], b).then_inc(S("rows_loaded"), 16)
                pool.wait_ge(*nth("rows_loaded", 32 * (i + 1)))
                nc.gpsimd.partition_broadcast(gain_bc, gain_bc[0:1, :], P).then_inc(S("rows_ready"), 1)
                nc.gpsimd.partition_broadcast(bias_bc, bias_bc[0:1, :], P).then_inc(S("rows_ready"), 1)

            def rows_of(dram, r0, n):
                return dram[bass.ds(r0, n), :]

            def moe(l):
                blocks = ln_blocks[f"ffn{l}"]
                nb = len(blocks)

                def scatter(signal):
                    for i, b in enumerate(blocks):
                        n = BLOCKS[b][1]
                        for k in range(2):
                            pool.indirect_dma_start(
                                out=xs_dram, out_offset=bass.IndirectOffsetOnAxis(ap=slots_u[0:n, i, k:k + 1], axis=0),
                                in_=hres[0:n, b, :], in_offset=None).then_inc(S(signal), 16)

                pool.wait_ge(*nth(f"slots_ready{l}", 1))
                if l == 0:
                    pool.wait_ge(*nth("rows_zeroed", 16 * 8))
                scatter(f"scattered{l}")

                def store(n, b, row0, sem_, ready):
                    pool.wait_ge(*nth(ready, n))
                    pool.sem_inc(S("pool_seen"), 1)
                    for q in range(4):
                        pool.dma_start(ys_dram[bass.ds(row0, CAP), 256 * q:256 * q + 256],
                                       y_out[b][32 * q:32 * q + 32, :]).then_inc(S(sem_), 16)

                with pool.Fori(0, NE // 2) as i:
                    for b in range(2):
                        store(i * 2 + (b + 1), b, i * (2 * CAP) + CAP * b, f"y_stored{l}_{b}", f"y_ready{l}")
                for b in range(2):
                    pool.wait_ge(*nth(f"y_stored{l}_{b}", 64 * (NE // 2)))
                rounds = pool.value_load(rounds_i[0:1, l:l + 1], min_val=1, max_val=MAX_ROUNDS)
                with pool.If(rounds > 1):
                    nc.gpsimd.memset(rowb[:, :], 0.0).then_inc(S(f"more_zero{l}"), 1)
                    pool.wait_ge(*nth(f"more_zero{l}", 1))
                    with pool.Fori(1, rounds) as r:
                        for c in range(ROUND_ROWS // P):
                            pool.dma_start(rows_of(xs_dram, r * ROUND_ROWS + c * P, P), rowb[:, :])\
                                .then_inc(S(f"more_zeroed{l}"), 16)
                        pool.wait_ge(*nth(f"more_zeroed{l}", r * (16 * (ROUND_ROWS // P))))
                    with pool.Fori(1, MAX_ROUNDS) as r:
                        for c in range(ROUND_ROWS // P):
                            pool.dma_start(rows_of(ys_dram, r * ROUND_ROWS + c * P, P), rowb[:, :])\
                                .then_inc(S(f"more_cleared{l}"), 16)
                        pool.wait_ge(*nth(f"more_cleared{l}", r * (16 * (ROUND_ROWS // P))))
                    scatter(f"more_scattered{l}")
                    pool.wait_ge(*nth(f"more_scattered{l}", 32 * nb))
                    with pool.Fori(1, rounds) as r:
                        with pool.Fori(0, NE) as e:
                            n = (r - 1) * NE + e
                            row0 = r * ROUND_ROWS + e * CAP
                            for q in range(1):
                                pool.dma_start(xs_in[0], rows_of(xs_dram, row0, CAP).rearrange("s (q c) -> (s q) c", q=4))\
                                    .then_inc(S(f"more_xs{l}"), 16)
                            pool.wait_ge(*nth(f"more_xs{l}", (n + 1) * 16))
                            nc.gpsimd.sem_inc(S(f"more_ready{l}"), 1)
                            store(n + 1, 0, row0, f"more_stored{l}", f"more_y{l}")
                            pool.wait_ge(*nth(f"more_stored{l}", (n + 1) * 64))
                pool.end_ifs()
                broadcast_rows(f"ffn{l}")

                def gather(table):
                    for i, b in enumerate(blocks):
                        n = BLOCKS[b][1]
                        if i >= 2:
                            pool.wait_ge(*nth(f"ffn{l}_normed", i - 1))
                        if i >= 1:
                            pool.wait_ge(*nth(f"rowb_free{l}", i))
                        for k, dst in enumerate((tmps[i % 2], rowb[:, :])):
                            pool.indirect_dma_start(
                                out=dst[0:n, :], out_offset=None, in_=table,
                                in_offset=bass.IndirectOffsetOnAxis(ap=slots_u[0:n, i, k:k + 1], axis=0))\
                                .then_inc(S(f"gathered{l}"), 16)

                with pool.If(rounds < 2):
                    gather(ys_dram[0:ROUND_ROWS, :])
                pool.end_ifs()
                with pool.If(rounds > 1):
                    gather(ys_dram)
                pool.end_ifs()

            broadcast_rows("mix0")
            pool.wait_ge(*nth("par_ready", 1))
            link(nc.gpsimd.memset(rowb[:, :], 0.0))
            for c in range(ROUND_ROWS // P):
                pool.dma_start(xs_dram[P * c:P * c + P, :], rowb[:, :]).then_inc(S("rows_zeroed"), 16)
            moe(0)
            pool.wait_ge(*nth("ffn0_normed", 3))
            for i, src in enumerate((a["ssm_lam_re_2"][0], a["ssm_lam_im_2"][0])):
                pool.dma_start(pre[0:SG, i, :], src).then_inc(S("s5_loaded"), 16)
            pool.dma_start(pre[0:SG, 2, 0:1], a["ssm_log_dt_2"][0].rearrange("(g o) -> g o", o=1)).then_inc(S("s5_loaded"), 16)
            for dst, src in ((s5_br, a["ssm_b_re_2"][0]), (s5_bi, a["ssm_b_im_2"][0])):
                pool.dma_start(dst[0:SS, :].rearrange("p (g c) -> p g c", c=SC),
                               src.rearrange("g p c -> p g c")).then_inc(S("s5_loaded"), 16)
            for i, src in enumerate((a["ssm_c_re_2"][0], a["ssm_c_im_2"][0])):
                pool.dma_start(s5_c[:, i], src.rearrange("(m q) c p -> (q c) m p", q=8)).then_inc(S("s5_loaded"), 16)
            nc.gpsimd.iota(iota_t, pattern=[[1, SEQ]], base=0, channel_multiplier=0,
                           allow_small_or_imprecise_dtypes=True).then_inc(S("iota_t"), 1)
            broadcast_rows("mix1")
            pool.wait_ge(*nth("maps_ready", 1))
            pool.dma_start(bc_dram, work[:, 12288:16384]).then_inc(S("maps_stored"), 16)
            for g in range(8):
                pool.wait_ge(*nth("rot_ready", 2 * (g + 1)))
                pool.dma_start(rot_dram[g // 2, :, 2048 * (g % 2):2048 * (g % 2) + 2048],
                               work[:, 4884 + 2048 * (g % 2):4884 + 2048 * (g % 2) + 2048]).then_inc(S(f"rot_stored{g % 2}"), 16)
            moe(1)
            broadcast_rows("s5")
            for s in range(ST):
                b = s % 2
                pool.wait_ge(*nth("s5_rotated", s + 1))
                if s >= 2:
                    pool.wait_ge(*nth("s5_scanned", s - 1))
                nc.gpsimd.tensor_tensor(s5_v[b][:, 0, :], s5_p1[b][:, 0, :], s5_p2[b][:, 1, :], ALU.add)
                nc.gpsimd.tensor_tensor(s5_v[b][:, 1, :], s5_p1[b][:, 1, :], s5_p2[b][:, 0, :], ALU.subtract)\
                    .then_inc(S("s5_v"), 1)
            broadcast_rows("mlp0")
            broadcast_rows("mla")
            for b in range(2):
                pool.dma_start(pos_i[:, b:b + 1], a["positions_2"][0, P * b:P * b + P].rearrange("(t o) -> t o", o=1))\
                    .then_inc(S("pos_loaded"), 16)
            pool.wait_ge(*nth("mlp0_normed", 2))
            for dst, src, n in ((inv_f, a["inv_freq"], ROPE // 2), (g_kv, a["kv_norm_g_2"], KVL), (g_q, a["q_norm_g_2"][0], QL)):
                pool.dma_start(dst[0:1, :], src.rearrange("(o n) -> o n", o=1)).then_inc(S("attn_rows"), 16)
            pool.wait_ge(*nth("attn_rows", 48))
            for dst in (inv_f, g_kv, g_q):
                nc.gpsimd.partition_broadcast(dst, dst[0:1, :], P).then_inc(S("attn_bc"), 1)
            broadcast_rows("mlp1")

        @block.tensor
        def _(pe):
            def transposes(n, blocks, hold, src=None, width=4):
                for i, b in enumerate(blocks):
                    m = BLOCKS[b][1]
                    pe.wait_ge(*nth(hold, i + 1)) if hold else pe.wait_ge(*nth(f"x_loaded{b}", 16))
                    for h in range(2):
                        j = 2 * i + h
                        if j >= 2:
                            pe.wait_ge(*nth(f"{n}_hT", j - 1))
                        for c in range(4):
                            mm = pe.transpose(ps[:, j % 2, c * P:c * P + m], hres[0:m, b, (4 * h + c) * P:(4 * h + c + 1) * P],
                                              ident[0:m, 0:m])
                        mm.then_inc(S(f"{n}_turned"), 1)

            def project(name, c, bank, t0, n, sem_):
                w = slot_view(name, DC, 512)
                for k in range(DC):
                    mm = pe.matmul(ps[:, bank, 0:n], w[:, k, P * c:P * c + P], hT[:, k, t0:t0 + n],
                                   start=(k == 0), stop=(k == DC - 1))
                mm.then_inc(S(sem_), 1)

            def rows_out(n, blocks, pieces, left, t_off):
                for p_, name in enumerate(pieces):
                    slot_wait(pe, name)
                    w = slot_view(name, 4, D)
                    for i, b in enumerate(blocks):
                        m = BLOCKS[b][1]
                        t0 = BLOCKS[b][0] - t_off
                        for k in range(4):
                            kk = 4 * p_ + k
                            for hf in range(2):
                                mm = pe.matmul(ps[0:m, 2 + 2 * b + hf, :], left[:, kk, t0:t0 + m],
                                               w[:, k, 512 * hf:512 * hf + 512],
                                               start=(kk == 0), stop=(kk == 4 * len(pieces) - 1))
                        if p_ == len(pieces) - 1:
                            mm.then_inc(S(f"{n}_mixed"), 1)
                    if p_ < len(pieces) - 1:
                        mm.then_inc(S(f"{n}_piece"), 1)

            def gate_up(eng, x, b, bank, g):
                gu = ring[:, g:g + 2, :].rearrange("p u (k n) -> p k u n", k=DC)
                for k in range(DC):
                    for q in range(4):
                        mm = pe.matmul(ps[32 * q:32 * q + 32, bank, 0:256].rearrange("p (u n) -> p u n", u=2),
                                       x[:, k, :], gu[:, k, :, P * q:P * q + P], start=(k == 0), stop=(k == DC - 1))
                return mm

            def down(hT_, bank, s):
                w = ring[:, s, :].rearrange("p (k n) -> p k n", k=4)
                for k in range(4):
                    for q in range(4):
                        mm = pe.matmul(ps[32 * q:32 * q + 32, bank, 0:256], hT_[:, 32 * k:32 * k + 32],
                                       w[:, k, 256 * q:256 * q + 256], start=(k == 0), stop=(k == 3))
                return mm

            def moe(l):
                blocks = ln_blocks[f"ffn{l}"]
                transposes(f"mix{l}", blocks, f"mix{l}_normed")
                pe.wait_ge(*nth(f"mix{l}_hT", 2 * len(blocks)))
                if l == 0:
                    pe.wait_ge(*nth("route_loaded", 16 * 8))
                    pe.wait_ge(*nth("consts", 5))
                for i, b in enumerate(blocks):
                    t0 = BLOCKS[b][0]
                    for k in range(DC):
                        pe.matmul(ps[:, 7, 36 * i:36 * i + 36], hT[:, k, t0:t0 + P], w_route[:, l, k, :],
                                  start=(k == 0 and i == 0), stop=False, skip_group_check=True)
                    mm = pe.matmul(ps[:, 7, 36 * i:36 * i + 36], ones[0:1, :], b_route[0:1, l, :],
                                   start=False, stop=(i == len(blocks) - 1), skip_group_check=True)
                mm.then_inc(S(f"logits{l}"), 1)
                pe.wait_ge(*nth(f"choice{l}", 1))
                nb = len(blocks)
                o = rowb[:, 800:800 + 32 * nb].rearrange("p (b e) -> p b e", b=nb)
                for i in range(nb):
                    for j in range(i + 1):
                        pe.matmul(ps[:, 6, 32 * i:32 * i + 32], (before if j == i else ones)[:, :], o[:, j, :],
                                  start=(i == 0 and j == 0), stop=False, skip_group_check=True)
                for j in range(nb):
                    mm = pe.matmul(ps[:, 6, 32 * nb:32 * nb + 32], ones[:, :], o[:, j, :], start=False,
                                   stop=(j == nb - 1), skip_group_check=True)
                mm.then_inc(S(f"ranks{l}"), 1)

                order, turns0 = expert_at[f"experts{l}"]

                def expert(n, st, b, first=False):
                    o_ = dict(order[b])
                    g, d_ = o_["gate"], o_["down"]
                    pe.wait_ge(*nth(f"xs_loaded{l}_{b}", (st + 1) * 16))
                    for h in range(2):
                        mm = pe.transpose(ps[:, b, P * h:P * h + P], xs_in[b][:, P * h:P * h + P], ident[:, :])
                    mm.then_inc(S(f"xs_turned{l}"), 1)
                    pe.wait_ge(*nth(f"xT_ready{l}", n + 1))
                    pe.wait_ge(loaded[g], (st + (turns0[g] + 1)) * 16)
                    pe.wait_ge(loaded[g + 1], (st + (turns0[g + 1] + 1)) * 16)
                    mm = gate_up(pe, xT[b], b, 2 + b, g)
                    mm.then_inc(S(f"gate_up{l}"), 1)
                    pe.wait_ge(*nth(f"hid_ready{l}", n + 1))
                    pe.transpose(ps[:, 6 + b, 0:P], hid[b], ident[:, :]).then_inc(S(f"hid_turned{l}"), 1)
                    pe.wait_ge(*nth(f"hidT_ready{l}", n + 1))
                    pe.wait_ge(loaded[d_], (st + (turns0[d_] + 1)) * 16)
                    if not first:
                        pe.wait_ge(*nth(f"y_ready{l}", n - 1))
                    mm = down(hidT[b], 4 + b, d_)
                    mm.then_inc(S(f"down{l}"), 1)

                for b in range(2):
                    expert(b, 0, b, first=True)
                with pe.Fori(1, NE // 2) as i:
                    for b in range(2):
                        expert(i * 2 + b, i, b)
                rounds = pe.value_load(rounds_i[0:1, l:l + 1], min_val=1, max_val=MAX_ROUNDS)
                with pe.If(rounds > 1):
                    pe.wait_ge(*nth(f"y_ready{l}", NE))
                    with pe.Fori(1, rounds) as r:
                        with pe.Fori(0, NE) as e:
                            n = (r - 1) * NE + e
                            pe.wait_ge(*nth(f"more_xs{l}", (n + 1) * 16))
                            for h in range(2):
                                mm = pe.transpose(ps[:, 0, P * h:P * h + P], xs_in[0][:, P * h:P * h + P], ident[:, :])
                            mm.then_inc(S(f"more_turned{l}"), 1)
                            pe.wait_ge(*nth(f"more_xT{l}", n + 1))
                            pe.wait_ge(*nth(f"more_loaded{l}", (n + 1) * 48))
                            gate_up(pe, xT[0], 0, 2, 0).then_inc(S(f"more_gate_up{l}"), 1)
                            pe.wait_ge(*nth(f"more_hid{l}", n + 1))
                            pe.transpose(ps[:, 6, 0:P], hid[0], ident[:, :]).then_inc(S(f"more_hid_turned{l}"), 1)
                            pe.wait_ge(*nth(f"more_hidT{l}", n + 1))
                            down(hidT[0], 4, 2).then_inc(S(f"more_used{l}"), 1)
                pe.end_ifs()

            pe.wait_ge(*nth("ident", 1))
            transposes("x", [0, 1, 2], None)
            pe.wait_ge(*nth("vectors_loaded", 16 * 7))
            for c in range(DC):
                mm = pe.transpose(ps[:, 7, 12 * c:12 * c + 12], rowb[0:12, P * c:P * c + P], ident[0:12, 0:12])
            mm.then_inc(S("par_turned"), 1)
            pe.wait_ge(*nth("x_hT", 6))

            def lru_gates(m):
                pe.wait_ge(*nth("lru_conv", m + 1))
                if m >= 2:
                    pe.wait_ge(*nth("lru_sig", m - 1))
                for i in range(2):
                    for j in range(2):
                        h = slice(64 * j, 64 * j + 64)
                        mm = pe.matmul(ps[h, (0 if i == 0 else 6) + m % 2, 0:T], w_gates[h, i, m, :], lru_c[h, m, :],
                                       start=True, stop=True)
                mm.then_inc(S("lru_gated"), 1)

            for j in range(16):
                if j >= 4:
                    pe.wait_ge(*nth("lru_evac", j - 3))
                name = ("lru_x0", "lru_x1", "lru_y0", "lru_y1")[j // 4]
                if j % 4 == 0:
                    slot_wait(pe, name)
                project(name, j % 4, 2 + j % 4, 0, T, "lru_proj")
                if j == 1:
                    pe.wait_ge(*nth("gates_loaded", 64))
                    pe.wait_ge(*nth("par_ready", 1))
                if 2 <= j < 10:
                    lru_gates(j - 2)
            pe.wait_ge(*nth("lru_evac", 16))
            pe.wait_ge(*nth("lru_sig", DC))
            pe.wait_ge(*nth("lru_z", DC))
            rows_out("mix0", [0, 1, 2], ["lru_out0", "lru_out1"], lru_y, 0)
            moe(0)
            transposes("ffn0", [0, 1, 2], "ffn0_normed")
            pe.wait_ge(*nth("ffn0_hT", 6))

            def prep_turns(m):
                if m == 2:
                    pe.wait_ge(*nth("s5_coef", 1))
                    for i in range(4):
                        mm = pe.transpose(ps[:, 0, SG * i:SG * i + SG], pre[0:SG, 16 + 2 * i:18 + 2 * i, :], ident[0:SG, 0:SG])
                    mm.then_inc(S("s5_coef_turned"), 1)
                if m == 4:
                    pe.wait_ge(*nth("s5_bb", 1))
                    for i, src in enumerate((s5_t0, s5_t1)):
                        for h in range(2):
                            for c in range(4):
                                mm = pe.transpose(ps[:, h, (4 * i + c) * SS:(4 * i + c + 1) * SS],
                                                  src[0:SS, P * (4 * h + c):P * (4 * h + c + 1)], ident[0:SS, 0:SS])
                    mm.then_inc(S("s5_bb_turned"), 1)
                if m in (5, 6):
                    for n in range(DC * (m - 5), DC * (m - 5) + DC):
                        pe.wait_ge(*nth("s5_cm", n + 1))
                        if n == 0:
                            pe.wait_ge(*nth("s5_bb_done", 1))
                        if n >= 2:
                            pe.wait_ge(*nth("s5_cm_done", n - 1))
                        pe.transpose(ps[:, n % 2, 0:P], cm[n % 2], ident[:, :]).then_inc(S("s5_cm_turned"), 1)

            cm = [s5_cm, region(10644, 128)]
            t_first = NMETA - (CONV_B - 1)
            for m in range(DC):
                for i, kind in enumerate(("cg", "v", "bg")):
                    j = 3 * m + i
                    name = f"sc_{kind}{m // 4}"
                    if m % 4 == 0:
                        slot_wait(pe, name)
                    if m >= 2:
                        pe.wait_ge(*nth("sc_z", m - 1))
                    bank = 2 + 3 * (m % 2) + i
                    t0, n = (t_first, TC) if kind != "bg" else (NMETA, SEQ)
                    project(name, m % 4, bank, t0, n, f"sc_{kind}")
                prep_turns(m)
            pe.wait_ge(*nth("sc_z", DC))
            rows_out("mix1", [1, 2], ["sc_out0", "sc_out1"], sc_z, NMETA)
            moe(1)
            transposes("ffn1", [1, 2], "ffn1_normed")
            pe.wait_ge(*nth("ffn1_hT", 4))
            slot_wait(pe, "s5_maps")
            mp = ring[:, place["s5_maps"], :].rearrange("p (i m n) -> p i m n", i=4, m=DC)

            def s5_in(s):
                m, j = s // 4, s % 4
                if s >= 4:
                    pe.wait_ge(*nth("s5_rotated", s - 3))
                r = slice(32 * j, 32 * j + 32)
                for i in range(2):
                    mm = pe.matmul(ps[:, s % 4, SEQ * i:SEQ * i + SEQ], mp[r, i, m, :], hT[r, m, NMETA:T],
                                   start=True, stop=True)
                mm.then_inc(S("s5_bu"), 1)

            def s5_out(s):
                m, j = s // 4, s % 4
                pe.wait_ge(*nth("s5_q", s + 1))
                if j == 0 and m >= 2:
                    pe.wait_ge(*nth("s5_y", m - 1))
                if s == 0:
                    pe.wait_ge(*nth("s5_ncre", 1))
                c = slice(32 * j, 32 * j + 32)
                b = s % 2
                o = ps[c, 4 + m % 2, 0:SEQ]
                pe.matmul(o, mp[:, 2, m, c], s5_q1[b][:, 0, :], start=True, stop=False)
                pe.matmul(o, s5_ncre[:, m, c], s5_q2[b][:, 1, :], start=False, stop=False)
                pe.matmul(o, mp[:, 3, m, c], s5_q1[b][:, 1, :], start=False, stop=False)
                mm = pe.matmul(o, mp[:, 3, m, c], s5_q2[b][:, 0, :], start=False, stop=True)
                mm.then_inc(S("s5_summed"), 1)
                return mm

            for s in range(ST + 2):
                if s < ST:
                    s5_in(s)
                if s >= 2:
                    s5_out(s - 2)
            pe.wait_ge(*nth("s5_g", DC))
            for m in range(DC):
                for i, kind in enumerate("vg"):
                    name = f"glu_{kind}{m // 4}"
                    if m % 4 == 0:
                        slot_wait(pe, name)
                    if m >= 2:
                        pe.wait_ge(*nth("glu_done", m - 1))
                    w = slot_view(name, DC, 512)
                    for k in range(DC):
                        mm = pe.matmul(ps[:, 2 * (m % 2) + i, 0:SEQ], w[:, k, P * (m % 4):P * (m % 4) + P], s5_g[:, k, :],
                                       start=(k == 0), stop=(k == DC - 1))
                mm.then_inc(S("glu_proj"), 1)
            pe.wait_ge(*nth("glu_done", DC))
            rows_out("s5", [1, 2], ["s5_out0", "s5_out1"], s5_y, NMETA)

            def mlp(layer, before_):
                transposes(before_, [1, 2], f"{before_}_normed")
                pe.wait_ge(*nth(f"{before_}_hT", 4))
                for c in range(DFF // P):
                    name = f"ff1_{layer}_{c // 4}"
                    if c % 4 == 0:
                        slot_wait(pe, name)
                    if c >= 4:
                        pe.wait_ge(*nth(f"ff_relu{layer}", c - 3))
                    project(name, c % 4, 2 + c % 4, NMETA, SEQ, f"ff_proj{layer}")
                pe.wait_ge(*nth(f"ff_sq{layer}", DFF // P))
                rows_out(f"mlp{layer}", [1, 2], [f"ff2_{layer}_{j}" for j in range(8)], ff, NMETA)

            mlp(0, "s5")
            transposes("mlp0", [1, 2], "mlp0_normed")
            pe.wait_ge(*nth("mlp0_hT", 4))
            for name, n, bank in (("kv_a", KVL + ROPE, 2), ("q_a", QL, 4)):
                slot_wait(pe, name)
                w = slot_view(name, DC, n)
                for b in range(2):
                    for k in range(DC):
                        mm = pe.matmul(ps[:, bank + b, 0:n], hT[:, k, NMETA + P * b:NMETA + P * b + P], w[:, k, :],
                                       start=(k == 0), stop=(k == DC - 1))
                    mm.then_inc(S("latent"), 1)
            pe.wait_ge(*nth("kv_normed", 2))
            for k in range(KVL // P):
                for b in range(2):
                    mm = pe.transpose(ps[:, 0, 256 * k + P * b:256 * k + P * b + P], ckv[:, b, P * k:P * k + P], ident[:, :])
            mm.then_inc(S("ckv_turned"), 1)
            pe.wait_ge(*nth("q_normed", 2))
            for k in range(2):
                for b in range(2):
                    mm = pe.transpose(ps[:, 1, 256 * k + P * b:256 * k + P * b + P], cq[:, b, P * k:P * k + P], ident[:, :])
            for b in range(2):
                mm = pe.transpose(ps[:, 6, P * b:P * b + P], cq[:, b, 2 * P:3 * P], ident[:, :])
            mm.then_inc(S("cq_turned"), 1)
            pe.wait_ge(*nth("ckvT", 1))
            slot_wait(pe, "kv_b")
            wkv = slot_view("kv_b", 2, HEADS * (NOPE + VH)).rearrange("p k (h n) -> p k h n", h=HEADS)
            for h in range(HEADS):
                for k in range(2):
                    mm = pe.matmul(ps[:, 2 + h // 2, SEQ * (h % 2):SEQ * (h % 2) + SEQ], wkv[:, k, h, 0:NOPE], ckvT[:, k, :],
                                   start=(k == 0), stop=(k == 1), skip_group_check=True)
                if h % 2:
                    mm.then_inc(S("keys"), 1)
            pe.wait_ge(*nth("cqT", 1))
            for b in range(2):
                for hh in range(2):
                    bank = (7, 0, 1, 6)[2 * b + hh]
                    for k in range(2):
                        mm = pe.matmul(ps[:, bank, :].rearrange("p (h n) -> p h n", h=4), ckvT[:, k, P * b:P * b + P],
                                       wkv[:, k, 4 * hh:4 * hh + 4, NOPE:NOPE + VH], start=(k == 0), stop=(k == 1))
                    mm.then_inc(S("values"), 1)
            for h in range(HEADS):
                name = f"q_b{h // 4}"
                if h % 4 == 0:
                    slot_wait(pe, name)
                w = slot_view(name, 3, 768).rearrange("p k (h n) -> p k h n", h=4)
                if h % 2 == 0:
                    pe.wait_ge(*nth("keys_out", h // 2 + 1))
                for k in range(3):
                    mm = pe.matmul(ps[:, 2 + h // 2, SEQ * (h % 2):SEQ * (h % 2) + SEQ], w[:, k, h % 4, 0:NOPE], cqT[:, k, :],
                                   start=(k == 0), stop=(k == 2), skip_group_check=True)
                if h % 2:
                    mm.then_inc(S("queries"), 1)
            for b in range(2):
                bank = (7, 0)[b]
                pe.wait_ge(*nth("values_out", b + 1))
                for hh in range(2):
                    w = slot_view(f"q_b{hh}", 3, 768).rearrange("p k (h n) -> p k h n", h=4)
                    for k in range(3):
                        mm = pe.matmul(ps[:, bank, 256 * hh:256 * hh + 256].rearrange("p (h n) -> p h n", h=4),
                                       cqT[:, k, P * b:P * b + P], w[:, k, :, NOPE:NOPE + ROPE],
                                       start=(k == 0), stop=(k == 2), skip_group_check=True)
                mm.then_inc(S("q_rope"), 1)
            for b in range(2):
                pe.wait_ge(*nth("q_rotated", b + 1))
                pe.wait_ge(*nth("values_out", 4))
                for g in range(4):
                    mm = pe.transpose(ps[:, (1, 6)[b], P * g:P * g + P], qr_rot_b[b].rearrange("p h n -> p (h n)")[:, P * g:P * g + P],
                                      ident[:, :])
                mm.then_inc(S("qr_turned"), 1)
            pe.wait_ge(*nth("k_rotated", 2))
            pe.wait_ge(*nth("q_rotated", 1))
            for b in range(2):
                mm = pe.transpose(ps[:, 7, P * b:P * b + P], kr2[:, b].rearrange("p a n -> p (a n)"), ident[:, :])
            mm.then_inc(S("kr_turned"), 1)
            pe.wait_ge(*nth("attn_left", 1))

            def scores(u):
                h, b = u // 2, u % 2
                if u >= 2:
                    pe.wait_ge(*nth("score_max", u - 1))
                n = P * (b + 1)
                r = slice(64 * (h % 2), 64 * (h % 2) + 64)
                pe.matmul(ps[:, 2 + u % 2, 0:n], qnT[:, h, P * b:P * b + P], knT[:, h, 0:n], start=True, stop=False)
                pe.matmul(ps[:, 2 + u % 2, 0:n], qrT[r, h // 2, P * b:P * b + P], krT[r, 0:n], start=False, stop=True)\
                    .then_inc(S("scores"), 1)

            def weigh(u):
                h, b = u // 2, u % 2
                pe.wait_ge(*nth("prob_normed", u + 1))
                if u >= 2:
                    pe.wait_ge(*nth("probT", u - 1))
                for c in range(b + 1):
                    mm = pe.transpose(ps[:, 4 + u % 2, P * c:P * c + P], prob[u % 2][:, P * c:P * c + P], ident[:, :])
                mm.then_inc(S("prob_turned"), 1)
                pe.wait_ge(*nth("probT", u + 1))
                if h >= 2 and b == 0:
                    pe.wait_ge(*nth("oT", h - 1))
                for c in range(b + 1):
                    mm = pe.matmul(ps[:, 6 + h % 2, P * b:P * b + P], val[:, c, VH * h:VH * h + VH], probT[u % 2][:, c, :],
                                   start=(c == 0), stop=(c == b), skip_group_check=True)
                if b == 1:
                    mm.then_inc(S("weighed"), 1)

            for u in range(2 * HEADS + 1):
                if u < 2 * HEADS:
                    scores(u)
                if u >= 1:
                    weigh(u - 1)
            pe.wait_ge(*nth("oT", HEADS))
            rows_out("mla", [1, 2], ["attn_out0", "attn_out1"], oT, NMETA)
            mlp(1, "mla")

        @block.scalar
        def _(act):
            A = nc.scalar.activation
            step = [0]

            def link(ins):
                step[0] += 1
                ins.then_inc(S("act_step"), 1)
                act.wait_ge(*nth("act_step", step[0]))

            def evac_turned(n, blocks):
                for i, b in enumerate(blocks):
                    t0, m = BLOCKS[b]
                    for h in range(2):
                        j = 2 * i + h
                        act.wait_ge(*nth(f"{n}_turned", j + 1))
                        A(hT[:, 4 * h:4 * h + 4, t0:t0 + m], ps[:, j % 2, :].rearrange("p (c n) -> p c n", c=4)[:, :, 0:m],
                          ACT.Copy).then_inc(S(f"{n}_hT"), 1)

            def deviations(n):
                for i, b in enumerate(ln_blocks[n]):
                    m = BLOCKS[b][1]
                    act.wait_ge(*nth(f"{n}_var", i + 1))
                    A(mean_var[0:m, i, 2:3], mean_var[0:m, i, 1:2], ACT.Sqrt, bias=eps_t[0:m, 0:1]).then_inc(S(f"{n}_sd"), 1)

            def moe(l):
                blocks = ln_blocks[f"ffn{l}"]
                deviations(f"mix{l}")
                evac_turned(f"mix{l}", blocks)
                nb = len(blocks)
                act.wait_ge(*nth(f"glog{l}", 1))
                rt = tmp_a[:, :]
                A(rt[:, 16:16 + 4 * nb], rt[:, 0:4 * nb], ACT.Exp).then_inc(S(f"gexp{l}"), 1)
                act.wait_ge(*nth(f"vdiff{l}", 1))
                A(rt[:, 36:36 + nb], rt[:, 32:32 + nb], ACT.Exp).then_inc(S(f"vexp{l}"), 1)
                act.wait_ge(*nth(f"scattered{l}", 32 * nb))
                act.wait_ge(*nth(f"mix{l}_normed", nb))

                def load_rows(row0, b):
                    act.dma_start(xs_in[b], xs_dram[bass.ds(row0, CAP), :].rearrange("s (q c) -> (s q) c", q=4))\
                        .then_inc(S(f"xs_loaded{l}_{b}"), 16)

                def expert(n, b):
                    act.wait_ge(*nth(f"gate_up{l}", n + 1))
                    A(silu[b], ps[:, 2 + b, 0:P], ACT.Silu).then_inc(S(f"silu{l}"), 1)
                    act.wait_ge(*nth(f"hid_turned{l}", n + 1))
                    A(hidT[b], ps[:, 6 + b, 0:P], ACT.Copy).then_inc(S(f"hidT_ready{l}"), 1)

                load_rows(0, 0)
                load_rows(CAP, 1)
                with act.Fori(0, NE // 2 - 1) as i:
                    for b in range(2):
                        expert(i * 2 + b, b)
                        load_rows(i * (2 * CAP) + (2 * CAP + CAP * b), b)
                for b in range(2):
                    expert(NE - 2 + b, b)
                rounds = act.value_load(rounds_i[0:1, l:l + 1], min_val=1, max_val=MAX_ROUNDS)
                with act.If(rounds > 1):
                    with act.Fori(1, rounds) as r:
                        with act.Fori(0, NE) as e:
                            n = (r - 1) * NE + e
                            act.wait_ge(*nth(f"more_gate_up{l}", n + 1))
                            A(silu[0], ps[:, 2, 0:P], ACT.Silu).then_inc(S(f"more_silu{l}"), 1)
                            act.wait_ge(*nth(f"more_hid_turned{l}", n + 1))
                            A(hidT[0], ps[:, 6, 0:P], ACT.Copy).then_inc(S(f"more_hidT{l}"), 1)
                act.end_ifs()
                deviations(f"ffn{l}")
                evac_turned(f"ffn{l}", blocks)

            evac_turned("x", [0, 1, 2])
            act.wait_ge(*nth("lam", 1))
            A(soft[:, 1, :], soft[:, 0, :], ACT.Exp, scale=-1.0).then_inc(S("lam_exp"), 1)

            def lru_gate_act(m):
                act.wait_ge(*nth("lru_gated", m + 1))
                A(lru_r[:, m, :], ps[:, m % 2, 0:T], ACT.Sigmoid, bias=par[:, m, 5:6]).then_inc(S("act_r"), 1)
                A(lru_i[:, m, :], ps[:, 6 + m % 2, 0:T], ACT.Sigmoid, bias=par[:, m, 6:7]).then_inc(S("lru_sig"), 1)
                act.wait_ge(*nth("act_r", m + 1))
                A(lru_r[:, m, :], lru_r[:, m, :], ACT.Tanh, scale=soft[:, 4, m:m + 1]).then_inc(S("lru_tanh"), 1)

            for j in range(DC):
                act.wait_ge(*nth("lru_proj", j + 1))
                A(lru_x[:, j, PAD_A:PAD_A + T], ps[:, 2 + j % 4, 0:T], ACT.Copy).then_inc(S("lru_evac"), 1)
                if j == 2:
                    act.wait_ge(*nth("soft", 1))
                if j >= 2:
                    lru_gate_act(j - 2)
            for j in range(DC, 2 * DC):
                act.wait_ge(*nth("lru_proj", j + 1))
                A(lru_y[:, j - DC, :], ps[:, 2 + j % 4, 0:T], ACT.Copy).then_inc(S("lru_evac"), 1)
                if j < DC + 2:
                    lru_gate_act(j - 2)
                if j == DC + 2:
                    act.wait_ge(*nth("lru_tanh", DC))
                    A(lru_q[:, :, :], lru_r[:, :, :], ACT.Sqrt).then_inc(S("lru_sqrt"), 1)
                if j >= DC + 3 and (j - DC) % 4 == 3:
                    c = slice(j - DC - 3, j - DC + 1)
                    act.wait_ge(*nth("lru_evac", j + 1))
                    A(lru_y[:, c, :], lru_y[:, c, :], ACT.Gelu_apprx_tanh).then_inc(S("lru_gelu"), 1)
            moe(0)
            def prep(m):
                if m == 0:
                    act.wait_ge(*nth("s5_loaded", 16 * 7))
                    A(pre[0:SG, 2, 1:2], pre[0:SG, 2, 0:1], ACT.Exp).then_inc(S("p_dt"), 1)
                    act.wait_ge(*nth("p_half", 1))
                    A(pre[0:SG, 4, :], pre[0:SG, 3, :], ACT.Tanh).then_inc(S("p_tanh"), 1)
                    act.wait_ge(*nth("p_theta", 1))
                    A(pre[0:SG, 8, :], pre[0:SG, 7, :], ACT.Sin, scale=0.5).then_inc(S("p_sin"), 1)
                    A(pre[0:SG, 9, :], pre[0:SG, 7, :], ACT.Sin).then_inc(S("p_sin"), 1)
                    A(pre[0:SG, 10, :], pre[0:SG, 7, :], ACT.Abs).then_inc(S("p_sin"), 1)
                    act.wait_ge(*nth("p_sin", 3))
                    A(pre[0:SG, 10, :], pre[0:SG, 10, :], ACT.Sin, scale=-1.0, bias=eps_t[0:SG, 1:2]).then_inc(S("p_sin"), 1)

            def rotations(g):
                b = g % 2
                act.wait_ge(*nth("rot_turns", g + 1))
                A(rot[b][:, :, 0, :], rot[b][:, :, 1, :], ACT.Abs).then_inc(S("rot_abs"), 1)
                act.wait_ge(*nth("rot_abs", g + 1))
                A(rot[b][:, :, 0, :], rot[b][:, :, 0, :], ACT.Sin, scale=-2 * PI_IN, bias=eps_t[:, 1:2]).then_inc(S("rot_ready"), 1)
                A(rot[b][:, :, 1, :], rot[b][:, :, 1, :], ACT.Sin, scale=2 * PI_IN).then_inc(S("rot_ready"), 1)

            groups = {4: [0, 1], 5: [2, 3], 6: [4, 5], 7: [6, 7]}
            for m in range(DC):
                act.wait_ge(*nth("sc_cg", m + 1))
                if m >= 2:
                    act.wait_ge(*nth("sc_gated", m - 1))
                A(sc_cg[m % 2], ps[:, 2 + 3 * (m % 2), 0:TC], ACT.Copy).then_inc(S("sc_cg_out"), 1)
                prep(m)
                for g in groups.get(m, []):
                    rotations(g)
            moe(1)
            slot_wait(act, "s5_maps")
            act.wait_ge(*nth("ffn1_normed", 2))
            mp = ring[:, place["s5_maps"], :].rearrange("p (i m n) -> p i m n", i=4, m=DC)
            A(s5_ncre, mp[:, 2], ACT.Copy, scale=-1.0).then_inc(S("s5_ncre"), 1)
            for m in range(DC):
                act.wait_ge(*nth("s5_y", m + 1))
                A(s5_g[:, m, :], s5_y[:, m, :], ACT.Gelu_apprx_tanh).then_inc(S("s5_g"), 1)
            for m in range(DC):
                act.wait_ge(*nth("glu_proj", m + 1))
                if m >= 2:
                    act.wait_ge(*nth("glu_done", m - 1))
                A(s5_sig[m % 2], ps[:, 2 * (m % 2) + 1, 0:SEQ], ACT.Sigmoid).then_inc(S("glu_sig"), 1)

            def mlp(layer, before_):
                deviations(before_)
                evac_turned(before_, [1, 2])
                for c in range(DFF // P):
                    act.wait_ge(*nth(f"ff_proj{layer}", c + 1))
                    A(ff[:, c, :], ps[:, 2 + c % 4, 0:SEQ], ACT.Relu).then_inc(S(f"ff_relu{layer}"), 1)

            mlp(0, "s5")
            deviations("mlp0")
            evac_turned("mlp0", [1, 2])
            act.wait_ge(*nth("angles", 1))
            A(sin_t, ang, ACT.Sin).then_inc(S("a_tab"), 1)
            A(angk, ang, ACT.Abs).then_inc(S("a_tab"), 1)
            act.wait_ge(*nth("a_tab", 2))
            A(cos_t, angk, ACT.Sin, scale=-1.0, bias=eps_t[:, 1:2]).then_inc(S("a_tab"), 1)
            for i, (bank, n, full, dst) in enumerate(((2, KVL, KVL + ROPE, ckv), (4, QL, QL, cq))):
                for b in range(2):
                    act.wait_ge(*nth("latent", 2 * i + b + 1))
                    A(dst[:, b, :], ps[:, bank + b, 0:full], ACT.Copy).then_inc(S("latent_out"), 1)
                    A(rope_u[:, 0:n], ps[:, bank + b, 0:n], ACT.Square, accum_out=sq_sum[:, 2 * i + b:2 * i + b + 1])\
                        .then_inc(S("latent_sq"), 1)
                    act.wait_ge(*nth("latent_sq", 2 * i + b + 1))
            for i, n in enumerate((KVL, QL)):
                A(sq_sum[:, 4 + 2 * i:6 + 2 * i], sq_sum[:, 2 * i:2 * i + 2], ACT.Sqrt, scale=1.0 / n, bias=eps_t[:, 2:3])\
                    .then_inc(S("latent_rms"), 1)
            act.wait_ge(*nth("ckv_turned", 1))
            A(ckvT, ps[:, 0, :].rearrange("p (k n) -> p k n", k=2), ACT.Copy).then_inc(S("ckvT"), 1)
            act.wait_ge(*nth("cq_turned", 1))
            A(cqT[:, 0:2, :], ps[:, 1, :].rearrange("p (k n) -> p k n", k=2), ACT.Copy).then_inc(S("cqT_a"), 1)
            A(cqT[:, 2, :], ps[:, 6, 0:256], ACT.Copy).then_inc(S("cqT_a"), 1)
            act.wait_ge(*nth("cqT_a", 2))
            act.sem_inc(S("cqT"), 1)
            for j in range(4):
                act.wait_ge(*nth("keys", j + 1))
                A(knT[:, 2 * j:2 * j + 2, :], ps[:, 2 + j, :].rearrange("p (h n) -> p h n", h=2), ACT.Copy).then_inc(S("keys_out"), 1)
            for j in range(4):
                act.wait_ge(*nth("queries", j + 1))
                A(qnT[:, 2 * j:2 * j + 2, :], ps[:, 2 + j, :].rearrange("p (h n) -> p h n", h=2), ACT.Copy).then_inc(S("queries_out"), 1)
            for b in range(2):
                act.wait_ge(*nth("qr_turned", b + 1))
                A(qrT[:, :, P * b:P * b + P], ps[:, (1, 6)[b], :].rearrange("p (g n) -> p g n", g=4), ACT.Copy)\
                    .then_inc(S("queries_out"), 1)
            act.wait_ge(*nth("kr_turned", 1))
            A(krT, ps[:, 7, 0:SEQ], ACT.Copy).then_inc(S("queries_out"), 1)
            act.wait_ge(*nth("queries_out", 7))
            act.sem_inc(S("attn_left"), 1)
            for u in range(2 * HEADS):
                n = P * (u % 2 + 1)
                act.wait_ge(*nth("score_max", u + 1))
                A(prob[u % 2][:, 0:n], prob[u % 2][:, 0:n], ACT.Exp, bias=sq_sum[:, 16 + u:17 + u], scale=1.0,
                  accum_out=sq_sum[:, 32 + u:33 + u]).then_inc(S("prob_exp"), 1)
                if u >= 1:
                    v = u - 1
                    act.wait_ge(*nth("prob_turned", v + 1))
                    A(probT[v % 2][:, 0:v % 2 + 1, :], ps[:, 4 + v % 2, 0:P * (v % 2 + 1)].rearrange("p (c n) -> p c n", n=P),
                      ACT.Copy).then_inc(S("probT"), 1)
            v = 2 * HEADS - 1
            act.wait_ge(*nth("prob_turned", v + 1))
            A(probT[v % 2][:, 0:2, :], ps[:, 4 + v % 2, 0:2 * P].rearrange("p (c n) -> p c n", n=P), ACT.Copy).then_inc(S("probT"), 1)
            mlp(1, "mla")
            deviations("mlp1")

        @block.vector
        def _(dve):
            V = nc.vector
            step = [0]

            def link(ins):
                step[0] += 1
                ins.then_inc(S("dve_step"), 1)
                dve.wait_ge(*nth("dve_step", step[0]))

            def norm(n, i, b, write):
                m = BLOCKS[b][1]
                x = tmps[i % 2][0:m, :]
                V.bn_stats(stats[0:m, i, 0:6], x[:, 0:512])
                link(V.bn_stats(stats[0:m, i, 6:12], x[:, 512:1024]))
                V.bn_aggr(mean_var[0:m, i, 0:2], stats[0:m, i, :]).then_inc(S(f"{n}_var"), 1)
                dve.wait_ge(*nth(f"{n}_sd", i + 1))
                link(V.reciprocal(mean_var[0:m, i, 3:4], mean_var[0:m, i, 2:3]))
                link(V.tensor_scalar(x, x, mean_var[0:m, i, 0:1], mean_var[0:m, i, 3:4], ALU.subtract, ALU.mult))
                if i == 0:
                    dve.wait_ge(*nth("rows_ready", 2 * (ln_order.index(n) + 1)))
                link(V.tensor_tensor(x, x, gain_bc[0:m, :], ALU.mult))
                src, dst, bias = write(x, hres[0:m, b, :], bias_bc[0:m, :])
                V.tensor_tensor(dst, src, bias, ALU.add).then_inc(S(f"{n}_normed"), 1)

            def plain(x, dst, bias):
                return x, dst, bias

            def to_packed(x, dst, bias):
                return packed(x), two(dst, P), packed(bias)

            def mix_norm(n, write=plain):
                for i, b in enumerate(ln_blocks[n]):
                    m = BLOCKS[b][1]
                    dve.wait_ge(*nth(f"{n}_mixed", i + 1))
                    link(V.scalar_tensor_tensor(out=tmps[i % 2][0:m, :], in0=hres[0:m, b, :], scalar=ALPHA,
                                                in1=ps[0:m, 2 + 2 * b:4 + 2 * b, :].rearrange("p a n -> p (a n)"),
                                                op0=ALU.mult, op1=ALU.add))
                    norm(n, i, b, write)

            def route(l):
                nb = len(ln_blocks[f"ffn{l}"])
                rt, rb = tmp_a[:, :], rowb[:, :]

                def v3(t, at, w):
                    return t[:, at:at + nb * w].rearrange("p (b w) -> p b w", b=nb)

                glog, gm = v3(rt, 0, 4), rt[:, 12:12 + nb]
                gexp, vdiff, vexp = v3(rt, 16, 4), rt[:, 32:32 + nb], rt[:, 36:36 + nb]
                gsum, gidx, pen = rt[:, 40:40 + nb], rt[:, 44:44 + nb], v3(rt, 48, 4)
                v1, v2, i1, i2 = (rt[:, 64 + 4 * j:64 + 4 * j + nb] for j in range(4))
                p1, p2, rk1, rk2 = (rt[:, 80 + 4 * j:80 + 4 * j + nb] for j in range(4))
                cmax, nround, fl = rt[:, 96:97], rt[:, 97:98], rt[:, 100:108]
                g4 = v3(rt, 112, 4)
                em, ind = v3(rb, 0, NE), v3(rb, 96, NE)
                o1, o2 = v3(rb, 192, NE), v3(rb, 288, NE)
                both = v3(rb, 800, NE)
                rank, cmp8 = v3(rb, 384, NE), v3(rb, 480, MAX_ROUNDS - 1)
                lo = ps[:, 7, 0:36 * nb].rearrange("p (b n) -> p b n", b=nb)

                def wide(x, w):
                    return x.unsqueeze(2).to_broadcast([P, nb, w])

                def iot(w):
                    return iota_e[:, 0:w].unsqueeze(1).to_broadcast([P, nb, w])

                def first_index(values, top, w, scratch, dst):
                    link(V.tensor_tensor(scratch, values, wide(top, w), ALU.is_lt))
                    link(V.scalar_tensor_tensor(out=scratch, in0=scratch, scalar=BIG, in1=iot(w), op0=ALU.mult, op1=ALU.add))
                    link(V.tensor_reduce(dst, scratch, AX.X, ALU.min))

                dve.wait_ge(*nth(f"logits{l}", 1))
                if l == 0:
                    dve.wait_ge(*nth("consts", 5))
                    dve.wait_ge(*nth("rows_zeroed", 16 * 8))
                V.tensor_copy(em, lo[:, :, NG:NG + NE])
                link(V.tensor_reduce(gm, lo[:, :, 0:NG], AX.X, ALU.max))
                V.tensor_tensor(glog, lo[:, :, 0:NG], wide(gm, NG), ALU.subtract).then_inc(S(f"glog{l}"), 1)
                link(V.tensor_copy(g4, lo[:, :, 0:NG]))
                first_index(g4, gm, NG, pen, gidx)
                link(V.tensor_tensor(pen, iot(NG), wide(gidx, NG), ALU.is_equal))
                link(V.tensor_scalar(pen, pen, 1.0, BIG, ALU.subtract, ALU.mult))
                em4 = em.rearrange("p b (g e) -> p b g e", g=NG)
                for j in range(nb):
                    V.tensor_tensor(em4[:, j], em4[:, j], pen[:, j].unsqueeze(2).to_broadcast([P, NG, EPG]), ALU.add)\
                        .then_inc(S(f"masked{l}"), 1)
                dve.wait_ge(*nth(f"masked{l}", nb))
                for v, ix, o, last in ((v1, i1, o1, False), (v2, i2, o2, True)):
                    link(V.tensor_reduce(v, em, AX.X, ALU.max))
                    first_index(em, v, NE, ind, ix)
                    link(V.tensor_tensor(o, iot(NE), wide(ix, NE), ALU.is_equal))
                    if not last:
                        link(V.scalar_tensor_tensor(out=em, in0=o, scalar=-3.0 * BIG, in1=em, op0=ALU.mult, op1=ALU.add))
                V.tensor_tensor(vdiff, v2, v1, ALU.subtract).then_inc(S(f"vdiff{l}"), 1)
                if nb == 3:
                    V.tensor_scalar(o1[:, 0], o1[:, 0], first_rows[:, 0:1], None, ALU.mult)
                    link(V.tensor_scalar(o2[:, 0], o2[:, 0], first_rows[:, 0:1], None, ALU.mult))
                V.tensor_tensor(both, o1, o2, ALU.add).then_inc(S(f"choice{l}"), 1)
                dve.wait_ge(*nth(f"gexp{l}", 1))
                link(V.tensor_reduce(gsum, gexp, AX.X, ALU.add))
                link(V.reciprocal(gsum, gsum))
                dve.wait_ge(*nth(f"vexp{l}", 1))
                link(V.tensor_scalar(p1, vexp, 1.0, None, ALU.add))
                link(V.reciprocal(p1, p1))
                link(V.tensor_tensor(p1, p1, gsum, ALU.mult))
                V.tensor_copy(gates[:, 0:nb, 0], p1)
                link(V.tensor_tensor(gates[:, 0:nb, 1], p1, vexp, ALU.mult))
                dve.wait_ge(*nth(f"ranks{l}", 1))
                link(V.tensor_copy(rank, ps[:, 6, 0:32 * nb].rearrange("p (b e) -> p b e", b=nb)))
                for k, (o, ix, rk) in enumerate(((o1, i1, rk1), (o2, i2, rk2))):
                    link(V.tensor_tensor(ind, o, rank, ALU.mult))
                    link(V.tensor_reduce(rk, ind, AX.X, ALU.add))
                    link(V.tensor_tensor(cmp8, wide(rk, MAX_ROUNDS - 1), marks[:, :].unsqueeze(1).to_broadcast([P, nb, MAX_ROUNDS - 1]),
                                         ALU.is_ge))
                    link(V.tensor_reduce(p2, cmp8, AX.X, ALU.add))
                    link(V.scalar_tensor_tensor(out=rk, in0=p2, scalar=float(ROUND_ROWS - CAP), in1=rk, op0=ALU.mult, op1=ALU.add))
                    link(V.scalar_tensor_tensor(out=rk, in0=ix, scalar=float(CAP), in1=rk, op0=ALU.mult, op1=ALU.add))
                    link(V.tensor_copy(slots_u[:, 0:nb, k], rk))
                link(V.tensor_reduce(cmax, ps[:, 6, 32 * nb:32 * nb + 32], AX.X, ALU.max))
                link(V.tensor_scalar(fl, marks[:, :], cmax, None, ALU.is_lt))
                link(V.tensor_reduce(nround, fl, AX.X, ALU.add))
                link(V.tensor_scalar(nround, nround, 1.0, None, ALU.add))
                V.tensor_copy(rounds_i[0:1, l:l + 1], nround[0:1, :]).then_inc(S(f"rounds_known{l}"), 1)
                dve.wait_ge(*nth(f"rounds_known{l}", 1))
                V.tensor_copy(cmax, nround).then_inc(S(f"slots_ready{l}"), 1)

            def moe(l):
                blocks = ln_blocks[f"ffn{l}"]
                mix_norm(f"mix{l}", to_packed)
                route(l)

                def expert(n, b, pre_, xb, gb, yb):
                    dve.wait_ge(*nth(f"{pre_[0]}{l}", n + 1))
                    V.tensor_copy(xT[b].rearrange("p (q h) s -> p h q s", h=2),
                                  ps[:, xb, 0:256].rearrange("p (h s q) -> p h q s", h=2, q=4)).then_inc(S(f"{pre_[1]}{l}"), 1)
                    dve.wait_ge(*nth(f"{pre_[2]}{l}", n + 1))
                    V.tensor_tensor(hid[b], silu[b], ps[:, gb, P:2 * P], ALU.mult).then_inc(S(f"{pre_[3]}{l}"), 1)

                names_ = ("xs_turned", "xT_ready", "silu", "hid_ready")

                def pair(i, first):
                    for b in range(2):
                        n = i * 2 + b
                        expert(n, b, names_, b, 2 + b, 4 + b)
                        dve.wait_ge(*nth(f"down{l}", n + 1))
                        if not first:
                            dve.wait_ge(*nth(f"y_stored{l}_{b}", i * 64))
                        V.tensor_copy(y_out[b], ps[:, 4 + b, 0:256]).then_inc(S(f"y_ready{l}"), 1)

                pair(0, True)
                with dve.Fori(1, NE // 2) as i:
                    pair(i, False)
                rounds = dve.value_load(rounds_i[0:1, l:l + 1], min_val=1, max_val=MAX_ROUNDS)
                with dve.If(rounds > 1):
                    with dve.Fori(1, rounds) as r:
                        with dve.Fori(0, NE) as e:
                            n = (r - 1) * NE + e
                            expert(n, 0, ("more_turned", "more_xT", "more_silu", "more_hid"), 0, 2, 4)
                            dve.wait_ge(*nth(f"more_used{l}", n + 1))
                            V.tensor_copy(y_out[0], ps[:, 4, 0:256]).then_inc(S(f"more_y{l}"), 1)
                dve.end_ifs()
                for i, b in enumerate(blocks):
                    m = BLOCKS[b][1]
                    x = tmps[i % 2][0:m, :]
                    dve.wait_ge(*nth(f"gathered{l}", 32 * (i + 1)))
                    link(V.tensor_scalar(x, x, gates[0:m, i, 0:1], None, ALU.mult))
                    V.scalar_tensor_tensor(out=x, in0=rowb[0:m, :], scalar=gates[0:m, i, 1:2], in1=x, op0=ALU.mult, op1=ALU.add)\
                        .then_inc(S(f"rowb_free{l}"), 1)
                    dve.wait_ge(*nth(f"rowb_free{l}", i + 1))
                    link(V.scalar_tensor_tensor(out=two(x, DC), in0=unpacked(hres[0:m, b, :]), scalar=ALPHA, in1=two(x, DC),
                                                op0=ALU.mult, op1=ALU.add))
                    norm(f"ffn{l}", i, b, plain)

            V.memset(eps_t[:, 0:1], LN_EPS)
            V.memset(eps_t[:, 1:2], math.pi / 2)
            V.memset(eps_t[:, 2:3], RMS_EPS)
            link(V.memset(lru_x[:, :, 0:PAD_A], 0.0))
            dve.wait_ge(*nth("par_turned", 1))
            V.tensor_copy(par[:, :, :], ps[:, 7, 0:12 * DC].rearrange("p (m v) -> p m v", v=12)).then_inc(S("par_ready"), 1)
            dve.wait_ge(*nth("par_ready", 1))
            lam = par[:, :, 7]
            V.tensor_scalar(soft[:, 3, :], lam, -1.0, 0.0, ALU.mult, ALU.max)
            link(V.tensor_scalar(soft[:, 0, :], lam, -1.0, None, ALU.mult))
            V.tensor_tensor(soft[:, 0, :], soft[:, 0, :], lam, ALU.max).then_inc(S("lam"), 1)
            dve.wait_ge(*nth("lam_exp", 1))
            link(V.tensor_scalar(soft[:, 0, :], soft[:, 1, :], 2.0, None, ALU.add))
            link(V.reciprocal(soft[:, 0, :], soft[:, 0, :]))
            link(V.tensor_tensor(soft[:, 0, :], soft[:, 0, :], soft[:, 1, :], ALU.mult))
            link(V.tensor_tensor(soft[:, 1, :], soft[:, 0, :], soft[:, 0, :], ALU.mult))
            link(V.tensor_scalar(soft[:, 2, :], soft[:, 1, :], 1.0 / 17, 1.0 / 15, ALU.mult, ALU.add))
            for c in (13, 11, 9, 7, 5, 3, 1):
                link(V.tensor_tensor(soft[:, 2, :], soft[:, 2, :], soft[:, 1, :], ALU.mult))
                link(V.tensor_scalar(soft[:, 2, :], soft[:, 2, :], 1.0 / c, None, ALU.add))
            link(V.tensor_tensor(soft[:, 2, :], soft[:, 2, :], soft[:, 0, :], ALU.mult))
            link(V.scalar_tensor_tensor(out=soft[:, 3, :], in0=soft[:, 2, :], scalar=2.0, in1=soft[:, 3, :], op0=ALU.mult, op1=ALU.add))
            V.tensor_scalar(soft[:, 4, :], soft[:, 3, :], 4.0, None, ALU.mult).then_inc(S("soft"), 1)

            def lru_decay(m):
                s, q = lru_r[:, m, :], lru_x[:, m, 0:T]
                dve.wait_ge(*nth("lru_tanh", m + 1))
                V.tensor_tensor(lru_i[:, m, :], lru_i[:, m, :], lru_c[:, m, :], ALU.mult)
                link(V.tensor_scalar(q, s, 1.0, None, ALU.add))
                link(V.reciprocal(q, q))

            def lru_scan(m):
                q, t = lru_x[:, m, 0:T], lru_q[:, m, :]
                link(V.tensor_tensor(t, t, q, ALU.mult))
                V.tensor_scalar(q, q, 2.0, -1.0, ALU.mult, ALU.add)
                link(V.scalar_tensor_tensor(out=t, in0=t, scalar=2.0, in1=lru_i[:, m, :], op0=ALU.mult, op1=ALU.mult))
                link(V.tensor_tensor_scan(lru_c[:, m, :], q, t, 0.0, ALU.mult, ALU.add))
                dve.wait_ge(*nth("lru_gelu", m // 4 + 1))
                V.tensor_tensor(lru_y[:, m, :], lru_y[:, m, :], lru_c[:, m, :], ALU.mult).then_inc(S("lru_z"), 1)

            for m in range(DC):
                dve.wait_ge(*nth("lru_evac", m + 1))
                link(V.tensor_scalar(lru_c[:, m, :], lru_x[:, m, 0:T], par[:, m, 0:1], par[:, m, 4:5], ALU.mult, ALU.add))
                for k in range(1, CONV_A):
                    ins = V.scalar_tensor_tensor(out=lru_c[:, m, :], in0=lru_x[:, m, k:k + T], scalar=par[:, m, k:k + 1],
                                                 in1=lru_c[:, m, :], op0=ALU.mult, op1=ALU.add)
                    if k < CONV_A - 1:
                        link(ins)
                ins.then_inc(S("lru_conv"), 1)
                dve.wait_ge(*nth("lru_conv", m + 1))
                if m >= 3:
                    lru_decay(m - 3)
            for m in range(DC - 3, DC):
                lru_decay(m)
            dve.wait_ge(*nth("lru_sqrt", 1))
            for m in range(DC):
                lru_scan(m)
            moe(0)

            lr, li = pre[0:SG, 0, :], pre[0:SG, 1, :]
            dt = pre[0:SG, 2, 1:2]

            def pr(i):
                return pre[0:SG, i, :]

            def prep_coef():
                dve.wait_ge(*nth("p_dt", 1))
                link(V.tensor_scalar(pr(3), lr, dt, None, ALU.mult))
                V.tensor_scalar(pr(3), pr(3), -0.5, None, ALU.mult).then_inc(S("p_half"), 1)
                link(V.tensor_scalar(pr(5), li, dt, None, ALU.mult))
                link(V.tensor_scalar(pr(6), pr(5), 1.0 / TWO_PI, ROUNDER, ALU.mult, ALU.add))
                link(V.tensor_scalar(pr(6), pr(6), ROUNDER, None, ALU.subtract))
                for c in (PI2_A, PI2_B, PI2_C):
                    link(V.scalar_tensor_tensor(out=pr(5), in0=pr(6), scalar=-c, in1=pr(5), op0=ALU.mult, op1=ALU.add))
                V.tensor_scalar(pr(7), pr(5), PI_IN, -PI_IN, ALU.min, ALU.max).then_inc(S("p_theta"), 1)
                dve.wait_ge(*nth("p_tanh", 1))
                link(V.tensor_scalar(pr(11), pr(4), 1.0, None, ALU.add))
                link(V.reciprocal(pr(11), pr(11)))
                V.tensor_scalar(pr(18), pr(11), 2.0, -1.0, ALU.mult, ALU.add)
                link(V.scalar_tensor_tensor(out=pr(12), in0=pr(4), scalar=-2.0, in1=pr(11), op0=ALU.mult, op1=ALU.mult))
                dve.wait_ge(*nth("p_sin", 4))
                link(V.tensor_tensor(pr(13), pr(12), pr(10), ALU.mult))
                link(V.tensor_tensor(pr(14), pr(8), pr(8), ALU.mult))
                link(V.scalar_tensor_tensor(out=pr(13), in0=pr(14), scalar=-2.0, in1=pr(13), op0=ALU.mult, op1=ALU.add))
                link(V.tensor_tensor(pr(14), pr(18), pr(9), ALU.mult))
                V.tensor_tensor(pr(11), lr, lr, ALU.mult)
                link(V.tensor_tensor(pr(12), li, li, ALU.mult))
                link(V.tensor_tensor(pr(11), pr(11), pr(12), ALU.add))
                link(V.reciprocal(pr(11), pr(11)))
                V.tensor_tensor(pr(12), pr(13), lr, ALU.mult)
                link(V.tensor_tensor(pr(15), pr(14), li, ALU.mult))
                link(V.tensor_tensor(pr(12), pr(12), pr(15), ALU.add))
                link(V.tensor_tensor(pr(20), pr(12), pr(11), ALU.mult))
                V.tensor_tensor(pr(12), pr(14), lr, ALU.mult)
                link(V.tensor_tensor(pr(15), pr(13), li, ALU.mult))
                link(V.tensor_tensor(pr(12), pr(12), pr(15), ALU.subtract))
                link(V.tensor_tensor(pr(22), pr(12), pr(11), ALU.mult))
                link(V.tensor_scalar(pr(16), pr(5), 1.0 / TWO_PI, None, ALU.mult))
                for i in (16, 18, 20, 22):
                    link(V.tensor_copy(pr(i + 1), pr(i)))
                link(V.tensor_copy(pr(17), pr(16)))
                V.tensor_copy(pr(15), pr(16)).then_inc(S("s5_coef"), 1)

            def prep_bb():
                dve.wait_ge(*nth("s5_coef_turned", 1))
                for h in range(2):
                    r = slice(64 * h, 64 * h + 64)
                    V.tensor_copy(phase[r, 0, :], ps[r, 0, h:SG:2])
                    ins = V.tensor_copy(decay[r, :], ps[r, 0, SG + h:2 * SG:2])
                link(ins)
                cre, cim = pre[0:SS, 3, :], pre[0:SS, 4, :]
                V.tensor_copy(cre, ps[0:SS, 0, 2 * SG:3 * SG])
                link(V.tensor_copy(cim, ps[0:SS, 0, 3 * SG:4 * SG]))
                link(V.tensor_scalar(phase[:, 1, :], phase[:, 0, :], ROUNDER / 4096.0, None, ALU.add))
                link(V.tensor_scalar(phase[:, 1, :], phase[:, 1, :], ROUNDER / 4096.0, None, ALU.subtract))
                link(V.tensor_tensor(phase[:, 2, :], phase[:, 0, :], phase[:, 1, :], ALU.subtract))

                def g3(t):
                    return t[0:SS, :].rearrange("p (g c) -> p g c", c=SC)

                def bc(t):
                    return t.unsqueeze(2).to_broadcast([SS, SG, SC])

                t2 = region(8980 + 1024, 1024)
                link(V.tensor_tensor(g3(t2), g3(s5_bi), bc(cim), ALU.mult))
                link(V.tensor_tensor(g3(s5_t0), g3(s5_br), bc(cre), ALU.mult))
                link(V.tensor_tensor(s5_t0[0:SS, :], s5_t0[0:SS, :], t2[0:SS, :], ALU.subtract))
                link(V.tensor_tensor(g3(t2), g3(s5_br), bc(cim), ALU.mult))
                link(V.tensor_tensor(g3(s5_t1), g3(s5_bi), bc(cre), ALU.mult))
                V.tensor_tensor(s5_t1[0:SS, :], s5_t1[0:SS, :], t2[0:SS, :], ALU.add).then_inc(S("s5_bb"), 1)
                link(V.tensor_scalar(int_p[:, 1:2], int_p[:, 0:1], SC, None, ALU.bitwise_and))
                link(V.tensor_scalar(even_odd[:, 0:1], int_p[:, 1:2], 0.0, None, ALU.is_equal))
                link(V.tensor_scalar(even_odd[:, 1:2], even_odd[:, 0:1], -1.0, 1.0, ALU.mult, ALU.add))

            cm = [s5_cm, region(10644, 128)]

            def prep_maps():
                dve.wait_ge(*nth("s5_bb_turned", 1))
                for i in range(2):
                    for h in range(2):
                        src = ps[:, h, 256 * i:256 * i + 256].rearrange("p (c n) -> p c n", c=4)
                        for eo in range(2):
                            ins = V.tensor_scalar(maps[:, i, 4 * h:4 * h + 4, SS * eo:SS * eo + SS], src, even_odd[:, eo:eo + 1], None,
                                                  ALU.mult)
                ins.then_inc(S("s5_bb_done"), 1)
                dve.wait_ge(*nth("s5_bb_done", 1))

                def back(n):
                    i, m = n // DC, n % DC
                    dve.wait_ge(*nth("s5_cm_turned", n + 1))
                    V.tensor_scalar(maps[:, 2 + i, m, :], ps[:, n % 2, 0:P], 1.0 if i == 0 else -1.0, None, ALU.mult)\
                        .then_inc(S("s5_cm_done"), 1)

                for n in range(2 * DC):
                    i, m = n // DC, n % DC
                    if n >= 2:
                        back(n - 2)
                    V.tensor_scalar(cm[n % 2][:, 0:SS], s5_c[:, i, m, :], even_odd[:, 0:1], None, ALU.mult)
                    V.tensor_scalar(cm[n % 2][:, SS:P], s5_c[:, i, m, :], even_odd[:, 1:2], None, ALU.mult)\
                        .then_inc(S("s5_cm"), 1)
                back(2 * DC - 2)
                back(2 * DC - 1)
                dve.wait_ge(*nth("s5_cm_done", 2 * DC))
                V.tensor_copy(int_p[:, 1:2], int_p[:, 0:1]).then_inc(S("maps_ready"), 1)

            def prep_turns(g):
                b = g % 2
                if g == 0:
                    dve.wait_ge(*nth("iota_t", 1))
                    dve.wait_ge(*nth("maps_ready", 1))
                if g >= 2:
                    dve.wait_ge(*nth(f"rot_stored{b}", 16 * (g // 2)))
                for j in range(4):
                    s = 4 * g + j
                    f = rot[b][:, j, 1, :]
                    link(V.tensor_scalar(rot_k, iota_t, phase[:, 0, s:s + 1], ROUNDER, ALU.mult, ALU.add))
                    link(V.tensor_scalar(rot_k, rot_k, ROUNDER, None, ALU.subtract))
                    link(V.scalar_tensor_tensor(out=f, in0=iota_t, scalar=phase[:, 1, s:s + 1], in1=rot_k, op0=ALU.mult, op1=ALU.subtract))
                    link(V.scalar_tensor_tensor(out=f, in0=iota_t, scalar=phase[:, 2, s:s + 1], in1=f, op0=ALU.mult, op1=ALU.add))
                    ins = V.tensor_scalar(f, f, 0.5, -0.5, ALU.min, ALU.max)
                    if j < 3:
                        link(ins)
                ins.then_inc(S("rot_turns"), 1)

            groups = {4: [0, 1], 5: [2, 3], 6: [4, 5], 7: [6, 7]}
            for m in range(DC):
                b = m % 2
                dve.wait_ge(*nth("sc_cg_out", m + 1))
                dve.wait_ge(*nth("sc_v", m + 1))
                V.tensor_tensor(sc_cv[b], sc_cg[b], ps[:, 3 + 3 * b, 0:TC], ALU.mult).then_inc(S("sc_gated"), 1)
                dve.wait_ge(*nth("sc_gated", m + 1))
                link(V.tensor_scalar(sc_a, sc_cv[b][:, 0:SEQ], par[:, m, 8:9], None, ALU.mult))
                for k in range(1, CONV_B):
                    link(V.scalar_tensor_tensor(out=sc_a, in0=sc_cv[b][:, k:k + SEQ], scalar=par[:, m, 8 + k:9 + k], in1=sc_a,
                                                op0=ALU.mult, op1=ALU.add))
                dve.wait_ge(*nth("sc_bg", m + 1))
                V.tensor_tensor(sc_z[:, m, :], sc_a, ps[:, 4 + 3 * b, 0:SEQ], ALU.mult).then_inc(S("sc_z"), 1)
                if m == 0:
                    prep_coef()
                if m == 2:
                    prep_bb()
                for g in groups.get(m, []):
                    if g == 0:
                        prep_maps()
                    prep_turns(g)
            moe(1)

            def s5_rotate(s):
                b = s % 2
                name = f"s5_rot{s // 8}"
                if s % 8 == 0:
                    slot_wait(dve, name)
                dve.wait_ge(*nth("s5_bu", s + 1))
                if s >= 2:
                    dve.wait_ge(*nth("s5_v", s - 1))
                cs = ring[:, place[name], 512 * (s % 8):512 * (s % 8) + 512].rearrange("p (i n) -> p i n", i=2)
                bu = ps[:, s % 4, :].rearrange("p (i n) -> p i n", i=2)
                V.tensor_tensor(s5_p1[b], bu, cs[:, 0:1, :].to_broadcast([P, 2, SEQ]), ALU.mult)
                V.tensor_tensor(s5_p2[b], bu, cs[:, 1:2, :].to_broadcast([P, 2, SEQ]), ALU.mult).then_inc(S("s5_rotated"), 1)

            def s5_scan(s):
                b = s % 2
                name = f"s5_rot{s // 8}"
                dve.wait_ge(*nth("s5_v", s + 1))
                am = decay[:, s:s + 1].to_broadcast([P, SEQ])
                V.tensor_tensor_scan(s5_h[b][:, 0, :], am, s5_v[b][:, 0, :], 0.0, ALU.mult, ALU.add)
                V.tensor_tensor_scan(s5_h[b][:, 1, :], am, s5_v[b][:, 1, :], 0.0, ALU.mult, ALU.add).then_inc(S("s5_scanned"), 1)
                dve.wait_ge(*nth("s5_scanned", s + 1))
                if s >= 2:
                    dve.wait_ge(*nth("s5_summed", s - 1))
                cs = ring[:, place[name], 512 * (s % 8):512 * (s % 8) + 512].rearrange("p (i n) -> p i n", i=2)
                V.tensor_tensor(s5_q1[b], s5_h[b], cs[:, 0:1, :].to_broadcast([P, 2, SEQ]), ALU.mult)
                ins = V.tensor_tensor(s5_q2[b], s5_h[b], cs[:, 1:2, :].to_broadcast([P, 2, SEQ]), ALU.mult)
                ins.then_inc(S("s5_q"), 1)

            def s5_skip(m):
                dve.wait_ge(*nth("s5_summed", 4 * m + 4))
                V.scalar_tensor_tensor(out=s5_y[:, m, :], in0=hT[:, m, NMETA:T], scalar=par[:, m, 11:12],
                                       in1=ps[:, 4 + m % 2, 0:SEQ], op0=ALU.mult, op1=ALU.add).then_inc(S("s5_y"), 1)

            for s in range(ST + 3):
                if s < ST:
                    s5_rotate(s)
                if 1 <= s <= ST:
                    s5_scan(s - 1)
                if s >= 6 and (s - 6) % 4 == 0:
                    s5_skip((s - 6) // 4)
            for m in range(DC):
                dve.wait_ge(*nth("glu_sig", m + 1))
                dve.wait_ge(*nth("s5_g", DC))
                V.tensor_tensor(s5_y[:, m, :], s5_sig[m % 2], ps[:, 2 * (m % 2), 0:SEQ], ALU.mult).then_inc(S("glu_done"), 1)
            mix_norm("s5")

            def mlp(layer):
                for c in range(DFF // P):
                    dve.wait_ge(*nth(f"ff_relu{layer}", c + 1))
                    V.tensor_tensor(ff[:, c, :], ff[:, c, :], ff[:, c, :], ALU.mult).then_inc(S(f"ff_sq{layer}"), 1)
                mix_norm(f"mlp{layer}")

            mlp(0)
            dve.wait_ge(*nth("pos_loaded", 32))
            dve.wait_ge(*nth("attn_bc", 3))
            link(V.tensor_copy(pos_f[:, :], pos_i[:, :]))
            for b in range(2):
                link(V.tensor_scalar(ang[:, b, :], inv_f, pos_f[:, b:b + 1], None, ALU.mult))
            link(V.tensor_scalar(angk, ang, 1.0 / TWO_PI, ROUNDER, ALU.mult, ALU.add))
            link(V.tensor_scalar(angk, angk, ROUNDER, None, ALU.subtract))
            for c in (PI2_A, PI2_B, PI2_C):
                link(V.scalar_tensor_tensor(out=ang, in0=angk, scalar=-c, in1=ang, op0=ALU.mult, op1=ALU.add))
            V.tensor_scalar(ang, ang, PI_IN, -PI_IN, ALU.min, ALU.max).then_inc(S("angles"), 1)

            def rotate(x, dst, nh, b):
                h = ROPE // 2
                c = cos_t[:, b:b + 1, :].to_broadcast([P, nh, h])
                s = sin_t[:, b:b + 1, :].to_broadcast([P, nh, h])
                u = [rope_u[:, 256 * i:256 * i + nh * h].rearrange("p (g n) -> p g n", g=nh) for i in range(2)]
                V.tensor_tensor(u[0], x[:, :, 0:h], c, ALU.mult)
                link(V.tensor_tensor(u[1], x[:, :, h:ROPE], s, ALU.mult))
                link(V.tensor_tensor(dst[:, :, 0:h], u[0], u[1], ALU.subtract))
                V.tensor_tensor(u[0], x[:, :, 0:h], s, ALU.mult)
                link(V.tensor_tensor(u[1], x[:, :, h:ROPE], c, ALU.mult))
                return V.tensor_tensor(dst[:, :, h:ROPE], u[0], u[1], ALU.add)

            dve.wait_ge(*nth("latent_rms", 2))
            dve.wait_ge(*nth("latent_out", 4))
            link(V.reciprocal(sq_sum[:, 8:12], sq_sum[:, 4:8]))
            for i, (x, n, g, sem_) in enumerate(((ckv, KVL, g_kv, "kv_normed"), (cq, QL, g_q, "q_normed"))):
                for b in range(2):
                    V.scalar_tensor_tensor(out=x[:, b, 0:n], in0=x[:, b, 0:n], scalar=sq_sum[:, 8 + 2 * i + b:9 + 2 * i + b],
                                           in1=g, op0=ALU.mult, op1=ALU.mult).then_inc(S(sem_), 1)
            dve.wait_ge(*nth("a_tab", 3))
            for b in range(2):
                link(rotate(ckv[:, b:b + 1, KVL:KVL + ROPE], kr2[:, b, 0:1, :], 1, b))
                V.tensor_copy(kr2[:, b, 1, :], kr2[:, b, 0, :]).then_inc(S("k_rotated"), 1)
            for j in range(4):
                dve.wait_ge(*nth("values", j + 1))
                b, hh = j // 2, j % 2
                V.tensor_copy(val[:, b, 512 * hh:512 * hh + 512], ps[:, (7, 0, 1, 6)[j], :]).then_inc(S("values_out"), 1)
            for b in range(2):
                dve.wait_ge(*nth("q_rope", b + 1))
                src = ps[:, (7, 0)[b], :].rearrange("p (h n) -> p h n", h=HEADS)
                rotate(src, qr_rot_b[b], HEADS, b).then_inc(S("q_rotated"), 1)
                dve.wait_ge(*nth("q_rotated", b + 1))
            dve.wait_ge(*nth("attn_left", 1))

            def mask_and_max(u):
                b = u % 2
                n = P * (b + 1)
                dve.wait_ge(*nth("scores", u + 1))
                if u >= 2:
                    dve.wait_ge(*nth("prob_turned", u - 1))
                x = prob[b]
                d_ = slice(P * b, P * b + P)
                if b == 1:
                    V.tensor_scalar(x[:, 0:P], ps[:, 2 + b, 0:P], SM_SCALE, None, ALU.mult)
                link(V.scalar_tensor_tensor(out=x[:, d_], in0=ps[:, 2 + b, d_], scalar=SM_SCALE, in1=causal, op0=ALU.mult, op1=ALU.add))
                V.tensor_reduce(sq_sum[:, 16 + u:17 + u], x[:, 0:n], AX.X, ALU.max, negate=True).then_inc(S("score_max"), 1)

            def normalise(u):
                b = u % 2
                n = P * (b + 1)
                dve.wait_ge(*nth("prob_exp", u + 1))
                link(V.reciprocal(sq_sum[:, 32 + u:33 + u], sq_sum[:, 32 + u:33 + u]))
                V.tensor_scalar(prob[b][:, 0:n], prob[b][:, 0:n], sq_sum[:, 32 + u:33 + u], None, ALU.mult).then_inc(S("prob_normed"), 1)

            causal = region(12416 + 512, P)
            link(V.tensor_scalar(causal, before[:, :], -BIG, None, ALU.mult))
            for u in range(2 * HEADS + 2):
                if u < 2 * HEADS:
                    mask_and_max(u)
                if 1 <= u <= 2 * HEADS:
                    normalise(u - 1)
                if u >= 3 and u % 2 == 1:
                    h = (u - 3) // 2
                    dve.wait_ge(*nth("weighed", h + 1))
                    V.tensor_copy(oT[:, h, :], ps[:, 6 + h % 2, 0:SEQ]).then_inc(S("oT"), 1)
            mix_norm("mla")
            mlp(1)



def kernel(**inputs):
    import numpy as _np
    import concourse.bacc as _bacc
    from concourse import mybir as _mybir
    from concourse.bass_utils import run_bass_kernel_spmd as _run

    nc = _bacc.Bacc("TRN2", target_bir_lowering=False, num_devices=1)
    arrays, args = {}, {}
    for name, value in inputs.items():
        v = _np.ascontiguousarray(value)
        arrays[f"in_{name}"] = v
        args[name] = nc.dram_tensor(f"in_{name}", v.shape, _mybir.dt.from_np(v.dtype), kind="ExternalInput").ap()
    freq = _np.array([10000.0 ** (-i / 32) for i in range(32)], _np.float32)
    arrays["const_inv_freq"] = freq
    args["inv_freq"] = nc.dram_tensor("const_inv_freq", freq.shape, F32, kind="ExternalInput").ap()
    out = nc.dram_tensor("out_0", (1, SEQ, D), F32, kind="ExternalOutput").ap()
    first_and_second_block(nc, args, out)
    r = _run(nc, [arrays], core_ids=[0])
    return r.results[0]["out_0"]
```

```python
from contextlib import ExitStack
import math

import numpy as np

import concourse.bass as bass
from concourse import mybir

F32 = mybir.dt.float32
I32 = mybir.dt.int32
U32 = mybir.dt.uint32
ALU = mybir.AluOpType
ACT = mybir.ActivationFunctionType
AX = mybir.AxisListType

P = 128
D = 1024
DC = D // P
NMETA = 16
SEQ = 256
T = NMETA + SEQ
BLOCKS = [(0, NMETA), (NMETA, P), (NMETA + P, P)]
ALPHA = 4.0 ** 0.25
LN_EPS = 1e-5
RMS_EPS = 1e-6
NG, EPG = 4, 8
NE = NG * EPG
DE = D // 2
CAP = 32
ROUND_ROWS = NE * CAP
MAX_ROUNDS = -(-T // CAP)
SLOT = 4096
NSLOT = 6
PREP_STEPS = 5
LH, LHD = 16, 64
CONV_A, CONV_B = 4, 3
SG, SC, SS = 64, 16, 64
ST = SG * SS // P
HEADS, NOPE, ROPE, VH = 8, 128, 64, 128
QL, KVL = 384, 256
SM_SCALE = (NOPE + ROPE) ** -0.5
DFF = 4 * D
BIG = 1.0e30
ROUNDER = 1.5 * 2.0 ** 23
TWO_PI = 2.0 * math.pi
PI2_A = 6.28125
PI2_B = float(np.float32(np.round((TWO_PI - PI2_A) * 2.0 ** 21) / 2.0 ** 21))
PI2_C = TWO_PI - PI2_A - PI2_B
PI_IN = 3.1415925


def first_and_second_block(nc, a, out):
    xs_dram = nc.dram_tensor("expert_rows_in", [MAX_ROUNDS * ROUND_ROWS, D], F32).ap()
    ys_dram = nc.dram_tensor("expert_rows_out", [MAX_ROUNDS * ROUND_ROWS, D], F32).ap()
    rot_dram = nc.dram_tensor("s5_rotations", [4, P, SLOT], F32).ap()

    ctx = ExitStack()
    with ctx:
        def sb(name, shape, dt=F32):
            return ctx.enter_context(nc.sbuf_tensor(name, shape, dt))

        ln_blocks = {"mix0": [0, 1, 2], "ffn0": [0, 1, 2], "mix1": [1, 2], "ffn1": [1, 2],
                     "s5": [1, 2], "mlp0": [1, 2], "mla": [1, 2], "mlp1": [1, 2]}
        ln_order = list(ln_blocks)
        shared, base = {}, {}

        def share(kind, counts):
            total = 0
            for name, n in counts:
                shared[name], base[name] = kind, total
                total += n

        for kind in ("var", "sd", "normed"):
            share(kind, [(f"{n}_{kind}", len(b)) for n, b in ln_blocks.items()])
        for kind in ("turned", "hT"):
            share(kind, [(f"x_{kind}", 6)] + [(f"{n}_{kind}", 2 * len(b)) for n, b in ln_blocks.items()])
        share("mixed", [(f"{n}_mixed", len(b)) for n, b in ln_blocks.items() if not n.startswith("ffn")])
        share("piece", [(f"{n}_piece", 7 if n.startswith("mlp") else 1) for n in ln_blocks if not n.startswith("ffn")])
        for kind in ("gate_up", "silu", "hid_ready", "hid_turned", "hidT_ready", "down", "y_ready", "xs_turned", "xT_ready"):
            share(kind, [(f"{kind}{l}", NE) for l in range(2)])
        for b in range(2):
            share(f"y_stored_{b}", [(f"y_stored{l}_{b}", 16 * (NE // 2)) for l in range(2)])
            share(f"xs_loaded_{b}", [(f"xs_loaded{l}_{b}", 16 * (NE // 2)) for l in range(2)])
        for kind in ("logits", "choice", "ranks", "glog", "gexp", "vdiff", "vexp", "slots_ready", "rounds_known"):
            share(kind, [(f"{kind}{l}", 1) for l in range(2)])
        for kind, each in (("masked", 1), ("scattered", 32)):
            share(kind, [(f"{kind}{l}", each * (3 - l)) for l in range(2)])
        for i in range(3):
            share(f"gathered_{i}", [(f"gathered{l}_{i}", 32) for l in range(2)])
        for kind in ("ff_proj", "ff_relu", "ff_sq"):
            share(kind, [(f"{kind}{l}", DFF // P) for l in range(2)])
        share("dve_constants", [(n, 1) for n in ("par_ready", "lam", "soft", "p_half", "p_theta", "s5_coef", "s5_bb",
                                                 "maps_ready", "angles")])
        share("act_constants", [("lam_exp", 1), ("p_dt", 1), ("p_tanh", 1), ("p_sin", 4), ("s5_ncre", 1), ("a_tab", 3),
                                ("latent_rms", 2), ("ckvT", 1), ("cqT_a", 2), ("cqT", 1)])
        share("pe_constants", [("par_turned", 1), ("s5_coef_turned", 1), ("s5_bb_turned", 1), ("ckv_turned", 1),
                               ("cq_turned", 1), ("qr_turned", 2), ("kr_turned", 1)])
        share("evacuated", [("lru_evac", 16), ("sc_cg_out", 8), ("s5_g", 8), ("glu_sig", 8)])
        share("left_ready", [("lru_z", 8), ("sc_z", 8), ("s5_y", 8), ("glu_done", 8), ("oT", 8)])
        share("gated", [("lru_conv", 8), ("sc_gated", 8), ("s5_rotated", ST)])
        share("projected", [("lru_proj", 16), ("sc_cg", 8), ("glu_proj", 8)])
        share("projected_2", [("lru_gated", 8), ("sc_v", 8), ("s5_bu", ST), ("scores", 2 * HEADS)])
        share("projected_3", [("sc_bg", 8), ("s5_summed", ST), ("weighed", HEADS)])

        sems = {}

        def S(name):
            name = shared.get(name, name)
            if name not in sems:
                sems[name] = nc.alloc_semaphore(name)
            return sems[name]

        def nth(name, count):
            return S(name), base.get(name, 0) + count

        ring = sb("ring", [P, NSLOT, SLOT])
        work = sb("work", [P, 16384])
        hres = sb("hres", [P, 3, D])
        hT = sb("hT", [P, DC, T])
        tmp_a = sb("tmp_a", [P, D])
        rowb = sb("rowb", [P, D])
        multi = sb("multi", [P, 3072])
        ident = sb("ident", [P, P])
        ones = sb("ones", [P, P])
        before = sb("before", [P, P])
        par = sb("par", [P, DC, 12])
        w_route = sb("w_route", [P, 2, DC, NG + NE])
        b_route = sb("b_route", [1, 2, NG + NE])
        iota_e = sb("iota_e", [P, NE])
        marks = sb("marks", [P, MAX_ROUNDS - 1])
        first_rows = sb("first_rows", [P, 1])
        even_odd = sb("even_odd", [P, 2])
        eps_t = sb("eps_t", [P, 3])
        stats = sb("stats", [P, 3, 12])
        mean_var = sb("mean_var", [P, 3, 4])
        gates = sb("gates", [P, 3, 2])
        slots_u = sb("slots_u", [P, 3, 2], U32)
        rounds_i = sb("rounds_i", [1, 2], I32)
        decay = sb("decay", [P, ST])
        phase = sb("phase", [P, 3, ST])
        int_p = sb("int_p", [P, 2], I32)
        ps = ctx.enter_context(nc.psum_tensor("ps", [P, 8, 512], F32))

        tmps = [tmp_a[:, :], multi[:, 2048:3072]]
        gain_bc, bias_bc = multi[:, 0:1024], multi[:, 1024:2048]
        xs_in = [multi[:, 256 * b:256 * b + 256] for b in range(2)]
        xT = [multi[:, 512 + 256 * b:768 + 256 * b].rearrange("p (k s) -> p k s", k=DC) for b in range(2)]
        silu = [multi[:, 1024 + 128 * b:1152 + 128 * b] for b in range(2)]
        hid = [multi[:, 1280 + 128 * b:1408 + 128 * b] for b in range(2)]
        hidT = [multi[:, 1536 + 128 * b:1664 + 128 * b] for b in range(2)]
        y_out = [multi[:, 1792 + 256 * b:2048 + 256 * b] for b in range(2)]

        loaded = [S(f"slot{s}_loaded") for s in range(NSLOT)]

        def cols(w, c0, n):
            return w[:, c0:c0 + n].rearrange("(k p) n -> p k n", p=P)

        def rows(w, r0, n):
            return w[r0:r0 + n, :].rearrange("(k p) n -> p k n", p=P)

        plan = []

        def add(name, source, over):
            plan.append((name, source, over))

        lw, lo = a["lru_w_in"][0], a["lru_w_out"][0]
        for i, (n, c0) in enumerate((("lru_x0", D), ("lru_x1", D + 512), ("lru_y0", 0), ("lru_y1", 512))):
            add(n, cols(lw, c0, 512), ("lru_proj", 4 * i + 4))

        def add_rows(prefix, w, pieces, stage, blocks):
            for j in range(pieces):
                over = (f"{stage}_mixed", blocks) if j == pieces - 1 else (f"{stage}_piece", j + 1)
                add(f"{prefix}{j}", rows(w, 512 * j, 512), over)

        add_rows("lru_out", lo, 2, "mix0", 3)
        add("experts0", None, None)
        sw, so = a["sc_w_in"][0], a["sc_w_out"][0]
        for hf in range(2):
            for n, c0 in (("cg", D), ("v", 2 * D), ("bg", 0)):
                add(f"sc_{n}{hf}", cols(sw, c0 + 512 * hf, 512), (f"sc_{n}", 4 * hf + 4))
        add_rows("sc_out", so, 2, "mix1", 2)
        add("experts1", None, None)
        for t in range(4):
            add(f"s5_rot{t}", rot_dram[t], ("s5_summed", 8 * t + 8))
        gw, go = a["ssm_w_glu_2"][0], a["ssm_w_out_2"][0]
        for hf in range(2):
            add(f"glu_v{hf}", cols(gw, 512 * hf, 512), ("glu_proj", 4 * hf + 4))
            add(f"glu_g{hf}", cols(gw, D + 512 * hf, 512), ("glu_proj", 4 * hf + 4))
        add_rows("s5_out", go, 2, "s5", 2)

        def add_mlp(layer):
            for j in range(8):
                add(f"ff1_{layer}_{j}", cols(a["w_ff1_2"][layer], 512 * j, 512), (f"ff_proj{layer}", 4 * j + 4))
            add_rows(f"ff2_{layer}_", a["w_ff2_2"][layer], 8, f"mlp{layer}", 2)

        add_mlp(0)
        add("kv_a", cols(a["kv_w_a_2"], 0, KVL + ROPE), ("latent", 2))
        add("q_a", cols(a["q_w_a_2"][0], 0, QL), ("latent", 4))
        add("kv_b", rows(a["kv_w_b_2"], 0, KVL), ("values", 4))
        for j in range(2):
            add(f"q_b{j}", cols(a["q_w_b_2"][0], 768 * j, 768), ("q_rope", 2))
        add_rows("attn_out", a["attn_w_o_2"][0], 2, "mla", 2)
        add_mlp(1)

        place, turn, at = {}, {}, 0
        expert_at = {}
        turns = [0] * NSLOT
        holder = [None] * NSLOT
        free_when = {}
        for name, _, over in plan:
            if name.startswith("experts"):
                six = [(at + j) % NSLOT for j in range(6)]
                order = []
                for b in range(2):
                    s = six[3 * b:3 * b + 3]
                    if s[0] + 1 == s[1]:
                        order.append((("gate", s[0]), ("up", s[1]), ("down", s[2])))
                    else:
                        order.append((("down", s[0]), ("gate", s[1]), ("up", s[2])))
                expert_at[name] = (order, list(turns))
                free_when[name] = list(holder)
                turns = [t + NE // 2 for t in turns]
                for b in range(2):
                    for kind, s in order[b]:
                        holder[s] = (("down" if kind == "down" else "gate_up") + name[-1], NE - 1 + b)
            else:
                s = at % NSLOT
                place[name], turn[name] = s, turns[s]
                free_when[name], holder[s] = holder[s], over
                turns[s] += 1
                at += 1

        def slot_wait(eng, name):
            eng.wait_ge(loaded[place[name]], 16 * (turn[name] + 1))

        def slot_view(name, k, n):
            return ring[:, place[name], 0:k * n].rearrange("p (k n) -> p k n", k=k)

        def region(start, *shape):
            n = 1
            for x in shape:
                n *= x
            v = work[:, start:start + n]
            if len(shape) == 2:
                return v.rearrange("p (a b) -> p a b", a=shape[0])
            if len(shape) == 3:
                return v.rearrange("p (a b c) -> p a b c", a=shape[0], b=shape[1])
            return v

        PAD_A = CONV_A - 1
        w_gates = region(0, 2, DC, LHD)
        lru_x = region(1024, DC, T + PAD_A)
        lru_c = region(3224, DC, T)
        lru_y = region(5400, DC, T)
        lru_r = region(7576, DC, T)
        lru_i = region(9752, DC, T)
        lru_q = region(11928, DC, T)
        soft = sb("soft", [P, 5, DC])
        TC = SEQ + CONV_B - 1
        sc_cg = [region(260 * b, TC) for b in range(2)]
        sc_cv = [region(520 + 260 * b, TC) for b in range(2)]
        sc_a = region(1040, SEQ)
        sc_z = region(1300, DC, SEQ)
        early_rows = [region(1024 * i, 1024) for i in range(2)]
        pre = work[:, 3348:3348 + 24 * 64].rearrange("p (a b) -> p a b", a=24)
        s5_br, s5_bi, s5_t0, s5_t1 = (region(4884 + 1024 * i, 1024) for i in range(4))
        s5_c = region(8980, 2, DC, SS)
        expert_rows = [[region(4884 + 1024 * (2 * i + k), 1024) for k in range(2)] for i in range(3)]
        maps = region(8192 + 4096, 4, DC, P)
        rot = [region(4884 + 2048 * b, 4, 2, SEQ) for b in range(2)]
        s5_cm = [region(10004, P), region(10132, P)]
        s5_t2 = region(10260, 1024)
        rot_k = region(10260, 4, SEQ)
        iota_t = region(11284, SEQ)
        s5_y = region(0, DC, SEQ)
        s5_g = region(2048, DC, SEQ)
        s5_ncre = region(4096, DC, P)
        s5_p1 = [region(5120 + 1024 * b, 2, SEQ) for b in range(2)]
        s5_p2 = [region(5632 + 1024 * b, 2, SEQ) for b in range(2)]
        s5_v = [region(at_, 2, SEQ) for at_ in (7168, 7680, 11776)]
        s5_h = [region(8192 + 512 * b, 2, SEQ) for b in range(2)]
        s5_q1 = [t[:, 512 * b:512 * b + 512].rearrange("p (a n) -> p a n", a=2)
                 for t in (work[:, 9216:10240], rowb) for b in range(2)]
        s5_q2 = [t[:, 512 * b:512 * b + 512].rearrange("p (a n) -> p a n", a=2)
                 for t in (work[:, 10240:11264], tmp_a) for b in range(2)]
        s5_sig = [region(11264 + 256 * b, SEQ) for b in range(2)]
        ff = region(0, DFF // P, SEQ)
        qnT = region(0, HEADS, SEQ)
        knT = region(2048, HEADS, SEQ)
        val = region(4096, 2, HEADS * VH)
        qrT = region(6144, HEADS // 2, SEQ)
        krT = region(7168, SEQ)
        oT = region(7424, HEADS, SEQ)
        ckv = region(9472, 2, KVL + ROPE)
        cq = region(10112, 2, QL)
        ckvT = region(10880, KVL // P, SEQ)
        cqT = region(11392, QL // P, SEQ)
        cos_t = region(12160, 2, ROPE // 2)
        sin_t = region(12224, 2, ROPE // 2)
        ang = region(12288, 2, ROPE // 2)
        angk = region(12352, 2, ROPE // 2)
        qr_in = region(12416, HEADS, ROPE)
        qr_rot = region(12928, HEADS, ROPE)
        prob = [region(13568 + 256 * b, SEQ) for b in range(2)] + [region(12416 + 256 * b, SEQ) for b in range(2)]
        probT = [region(14080 + 256 * b, 2, P) for b in range(2)]
        sq_sum = region(14592, 64)
        rope_u = region(14656, 512)
        pos_i = sb("pos_i", [P, 2], I32)
        pos_f = sb("pos_f", [P, 2])
        inv_f = region(15168, ROPE // 2)
        g_kv = region(15200, KVL)
        g_q = region(15456, QL)
        qr_rot_b = [qr_rot, qr_in]
        kr2 = region(15840, 2, 2, ROPE)

        block = ctx.enter_context(nc.Block())

        ln_rows = {
            "mix0": (a["ln_g"][0, 0:1], a["ln_b"][0, 0:1]), "ffn0": (a["ln_g"][0, 1:2], a["ln_b"][0, 1:2]),
            "mix1": (a["ln_g"][1, 0:1], a["ln_b"][1, 0:1]), "ffn1": (a["ln_g"][1, 1:2], a["ln_b"][1, 1:2]),
            "s5": (a["ln_mix_g_2"][0:1], a["ln_mix_b_2"][0:1]), "mlp0": (a["ln_ffn_g_2"][0:1], a["ln_ffn_b_2"][0:1]),
            "mla": (a["ln_mix_g_2"][1:2], a["ln_mix_b_2"][1:2]), "mlp1": (a["ln_ffn_g_2"][1:2], a["ln_ffn_b_2"][1:2]),
        }

        def packed(ap):
            return ap.rearrange("t (p k) -> t k p", k=DC)

        def unpacked(ap):
            return ap.rearrange("t (k p) -> t p k", k=DC)

        def two(ap, k):
            return ap.rearrange("t (a b) -> t a b", b=k)

        @block.sync
        def _(sp):
            def slot_free(when):
                if when:
                    sp.wait_ge(*nth(when[0], when[1]))

            def load_experts(l, name):
                order, before_ = expert_at[name]
                w = {"gate": a["moe_w_gate"][l], "up": a["moe_w_up"][l], "down": a["moe_w_down"][l]}

                def load_pair(e, step, first):
                    for b in range(2):
                        for kind, s in order[b]:
                            src = w[kind][e + b]
                            if kind == "down":
                                src = src.rearrange("(q p) n -> p q n", p=P)
                                dst = ring[:, s, :].rearrange("p (q n) -> p q n", q=4)
                            else:
                                src = src.rearrange("(p k) n -> p (k n)", k=DC)
                                dst = ring[:, s, :]
                            if first:
                                slot_free(free_when[name][s])
                            else:
                                sp.wait_ge(*nth(("down" if kind == "down" else "gate_up") + str(l), step * 2 + (b - 1)))
                            sp.dma_start(dst, src).then_inc(loaded[s], 16)

                load_pair(0, 0, True)
                with sp.Fori(1, NE // 2) as step:
                    load_pair(step * 2, step, False)
                sp.wait_ge(*nth(f"rounds_known{l}", 1))
                rounds = sp.value_load(rounds_i[0:1, l:l + 1], min_val=1, max_val=MAX_ROUNDS)
                with sp.If(rounds > 1):
                    sp.wait_ge(*nth(f"down{l}", NE))
                    with sp.Fori(1, rounds) as r:
                        with sp.Fori(0, NE) as e:
                            n = (r - 1) * NE + e
                            sp.wait_ge(*nth(f"more_ready{l}", n + 1))
                            for kind, s in (("gate", 0), ("up", 1), ("down", 2)):
                                src = w[kind][e]
                                if kind == "down":
                                    src = src.rearrange("(q p) n -> p q n", p=P)
                                    dst = ring[:, s, :].rearrange("p (q n) -> p q n", q=4)
                                else:
                                    src = src.rearrange("(p k) n -> p (k n)", k=DC)
                                    dst = ring[:, s, :]
                                sp.dma_start(dst, src).then_inc(S(f"more_loaded{l}"), 16)
                        sp.wait_ge(*nth(f"more_used{l}", r * NE))
                        sp.sem_inc(S("more_rounds"), 1)
                sp.end_ifs()

            for b, (t0, n) in enumerate(BLOCKS):
                src = a["meta_tokens"] if b == 0 else a["x"][0, t0 - NMETA:t0 - NMETA + n, :]
                sp.dma_start(hres[0:n, b, :], src).then_inc(S(f"x_loaded{b}"), 16)
            vec = [(a["lru_conv_w"][0], 4), (a["lru_conv_b"], 1), (a["lru_b_a"], 1), (a["lru_b_i"], 1),
                   (a["lru_lambda"], 1), (a["sc_conv_w"][0], 3), (a["ssm_d_2"], 1)]
            r = 0
            for src, n in vec:
                sp.dma_start(rowb[r:r + n, :], src).then_inc(S("vectors_loaded"), 16)
                r += n
            for i, w in enumerate((a["lru_w_a"][0], a["lru_w_i"][0])):
                for j in range(2):
                    sp.dma_start(w_gates[64 * j:64 * j + 64, i],
                                   w.rearrange("(m j) d e -> j d m e", j=2)[j]).then_inc(S("gates_loaded"), 16)
            names = [entry[0] for entry in plan]
            after_experts = {names[names.index(f"experts{l}") + 3]: l for l in range(2)}
            for name, src, _ in plan:
                if name in ("experts0", "experts1"):
                    load_experts(int(name[-1]), name)
                    continue
                if name in after_experts:
                    layer = after_experts[name]
                    for i in range(len(ln_blocks[f"ffn{layer}"])):
                        sp.wait_ge(*nth(f"gathered{layer}_{i}", 32))
                s = place[name]
                slot_free(free_when[name])
                if name.startswith("s5_rot"):
                    for b in range(2):
                        sp.wait_ge(*nth(f"rot_stored{b}", 16 * (int(name[-1]) + 1)))
                n = 1
                for x in src.shape[1:]:
                    n *= x
                dst = ring[:, s, 0:n]
                if len(src.shape) == 3:
                    dst = dst.rearrange("p (k n) -> p k n", k=src.shape[1])
                sp.dma_start(dst, src).then_inc(loaded[s], 16)
            for b in (1, 2):
                sp.wait_ge(*nth("mlp1_normed", b))
                t0 = BLOCKS[b][0] - NMETA
                sp.dma_start(out[0, t0:t0 + P, :], hres[:, b, :]).then_inc(S("stored"), 16)
            sp.wait_ge(*nth("stored", 32))

        @block.gpsimd
        def _(pool):
            step = [0]

            def link(ins):
                step[0] += 1
                ins.then_inc(S("pool_step"), 1)
                pool.wait_ge(*nth("pool_step", step[0]))

            link(nc.gpsimd.memset(ident[:, :], 0.0))
            nc.gpsimd.affine_select(out=ident[:, :], in_=ident[:, :], compare_op=ALU.not_equal, fill=1.0,
                                    base=0, pattern=[[-1, P]], channel_multiplier=1).then_inc(S("ident"), 1)
            for l in range(2):
                pool.dma_start(w_route[:, l, :, 0:NG],
                               a["moe_w_group"][l].rearrange("(p k) n -> p k n", k=DC)).then_inc(S("route_loaded"), 16)
                pool.dma_start(w_route[:, l, :, NG:NG + NE],
                               a["moe_w_expert"][l].rearrange("(p k) n -> p k n", k=DC)).then_inc(S("route_loaded"), 16)
                pool.dma_start(b_route[0:1, l, 0:NG], a["moe_b_group"][l:l + 1, :]).then_inc(S("route_loaded"), 16)
                pool.dma_start(b_route[0:1, l, NG:NG + NE],
                               a["moe_b_expert"][l:l + 1].rearrange("a g e -> a (g e)")).then_inc(S("route_loaded"), 16)
            link(nc.gpsimd.memset(ones[:, :], 1.0))
            nc.gpsimd.affine_select(out=before[:, :], in_=ones[:, :], compare_op=ALU.is_gt, fill=0.0,
                                    base=0, pattern=[[1, P]], channel_multiplier=-1).then_inc(S("consts"), 1)
            nc.gpsimd.affine_select(out=first_rows[:, :], in_=ones[:, 0:1], compare_op=ALU.is_gt, fill=0.0,
                                    base=NMETA, pattern=[[0, 1]], channel_multiplier=-1).then_inc(S("consts"), 1)
            nc.gpsimd.iota(iota_e[:, :], pattern=[[1, NE]], base=0, channel_multiplier=0,
                           allow_small_or_imprecise_dtypes=True).then_inc(S("consts"), 1)
            nc.gpsimd.iota(marks[:, :], pattern=[[CAP, MAX_ROUNDS - 1]], base=CAP, channel_multiplier=0,
                           allow_small_or_imprecise_dtypes=True).then_inc(S("consts"), 1)
            nc.gpsimd.iota(int_p[:, 0:1], pattern=[[0, 1]], base=0, channel_multiplier=1).then_inc(S("consts"), 1)

            def broadcast_rows(n):
                g, b = ln_rows[n]
                i = ln_order.index(n)
                if i > 0:
                    prev = ln_order[i - 1]
                    pool.wait_ge(*nth(f"{prev}_normed", len(ln_blocks[prev])))
                rows_at = (gain_bc, bias_bc)
                if n.startswith("ffn"):
                    rows_at = early_rows
                else:
                    for dst, src in ((gain_bc, g), (bias_bc, b)):
                        pool.dma_start(dst[0:1, :], src).then_inc(S("rows_loaded"), 16)
                pool.wait_ge(*nth("rows_loaded", 32 * (i + 1)))
                for dst, src in zip((gain_bc, bias_bc), rows_at):
                    nc.gpsimd.partition_broadcast(dst, src[0:1, :], P).then_inc(S("rows_ready"), 1)

            def rows_of(dram, r0, n):
                return dram[bass.ds(r0, n), :]

            def load_s5():
                for i, src in enumerate((a["ssm_lam_re_2"][0], a["ssm_lam_im_2"][0])):
                    pool.dma_start(pre[0:SG, i, :], src).then_inc(S("s5_loaded"), 16)
                pool.dma_start(pre[0:SG, 2, 0:1], a["ssm_log_dt_2"][0].rearrange("(g o) -> g o", o=1)).then_inc(S("s5_loaded"), 16)
                for dst, src in ((s5_br, a["ssm_b_re_2"][0]), (s5_bi, a["ssm_b_im_2"][0])):
                    pool.dma_start(dst[0:SS, :].rearrange("p (g c) -> p g c", c=SC),
                                   src.rearrange("g p c -> p g c")).then_inc(S("s5_loaded"), 16)
                for i, src in enumerate((a["ssm_c_re_2"][0], a["ssm_c_im_2"][0])):
                    pool.dma_start(s5_c[:, i], src.rearrange("(m q) c p -> (q c) m p", q=8)).then_inc(S("s5_loaded"), 16)
                nc.gpsimd.iota(iota_t, pattern=[[1, SEQ]], base=0, channel_multiplier=0,
                               allow_small_or_imprecise_dtypes=True).then_inc(S("iota_t"), 1)

            def moe(l):
                blocks = ln_blocks[f"ffn{l}"]
                nb = len(blocks)

                def scatter(signal):
                    for i, b in enumerate(blocks):
                        n = BLOCKS[b][1]
                        for k in range(2):
                            pool.indirect_dma_start(
                                out=xs_dram, out_offset=bass.IndirectOffsetOnAxis(ap=slots_u[0:n, i, k:k + 1], axis=0),
                                in_=hres[0:n, b, :], in_offset=None).then_inc(S(signal), 16)

                pool.wait_ge(*nth(f"slots_ready{l}", 1))
                if l == 0:
                    pool.wait_ge(*nth("rows_zeroed", 16 * 8))
                scatter(f"scattered{l}")
                if l == 0:
                    load_s5()
                for dst, src in zip(early_rows, ln_rows[f"ffn{l}"]):
                    pool.dma_start(dst[0:1, :], src).then_inc(S("rows_loaded"), 16)

                def store(n, b, row0, sem_, ready):
                    pool.wait_ge(*nth(ready, n))
                    pool.sem_inc(S("pool_seen"), 1)
                    pool.dma_start(ys_dram[bass.ds(row0, CAP), :].rearrange("s (q c) -> q s c", q=4), y_out[b])\
                        .then_inc(S(sem_), 16)

                with pool.Fori(0, NE // 2) as i:
                    for b in range(2):
                        store(i * 2 + (b + 1), b, i * (2 * CAP) + CAP * b, f"y_stored{l}_{b}", f"y_ready{l}")
                for b in range(2):
                    pool.wait_ge(*nth(f"y_stored{l}_{b}", 16 * (NE // 2)))
                rounds = pool.value_load(rounds_i[0:1, l:l + 1], min_val=1, max_val=MAX_ROUNDS)
                with pool.If(rounds > 1):
                    nc.gpsimd.memset(rowb[:, :], 0.0).then_inc(S(f"more_zero{l}"), 1)
                    pool.wait_ge(*nth(f"more_zero{l}", 1))
                    with pool.Fori(1, rounds) as r:
                        for c in range(ROUND_ROWS // P):
                            pool.dma_start(rows_of(xs_dram, r * ROUND_ROWS + c * P, P), rowb[:, :])\
                                .then_inc(S(f"more_zeroed{l}"), 16)
                        pool.wait_ge(*nth(f"more_zeroed{l}", r * (16 * (ROUND_ROWS // P))))
                    with pool.Fori(1, MAX_ROUNDS) as r:
                        for c in range(ROUND_ROWS // P):
                            pool.dma_start(rows_of(ys_dram, r * ROUND_ROWS + c * P, P), rowb[:, :])\
                                .then_inc(S(f"more_cleared{l}"), 16)
                        pool.wait_ge(*nth(f"more_cleared{l}", r * (16 * (ROUND_ROWS // P))))
                    scatter(f"more_scattered{l}")
                    pool.wait_ge(*nth(f"more_scattered{l}", 32 * nb))
                    with pool.Fori(1, rounds) as r:
                        with pool.Fori(0, NE) as e:
                            n = (r - 1) * NE + e
                            row0 = r * ROUND_ROWS + e * CAP
                            pool.dma_start(xs_in[0], rows_of(xs_dram, row0, CAP).rearrange("s (q c) -> (s q) c", q=4))\
                                .then_inc(S(f"more_xs{l}"), 16)
                            pool.wait_ge(*nth(f"more_xs{l}", (n + 1) * 16))
                            nc.gpsimd.sem_inc(S(f"more_ready{l}"), 1)
                            store(n + 1, 0, row0, f"more_stored{l}", f"more_y{l}")
                            pool.wait_ge(*nth(f"more_stored{l}", (n + 1) * 16))
                pool.end_ifs()
                def gather(table):
                    for i, b in enumerate(blocks):
                        n = BLOCKS[b][1]
                        for k in range(2):
                            pool.indirect_dma_start(
                                out=expert_rows[i][k][0:n, :], out_offset=None, in_=table,
                                in_offset=bass.IndirectOffsetOnAxis(ap=slots_u[0:n, i, k:k + 1], axis=0))\
                                .then_inc(S(f"gathered{l}_{i}"), 16)

                with pool.If(rounds < 2):
                    gather(ys_dram[0:ROUND_ROWS, :])
                pool.end_ifs()
                with pool.If(rounds > 1):
                    gather(ys_dram)
                pool.end_ifs()
                broadcast_rows(f"ffn{l}")

            broadcast_rows("mix0")
            pool.wait_ge(*nth("par_ready", 1))
            link(nc.gpsimd.memset(rowb[:, :], 0.0))
            for c in range(ROUND_ROWS // P):
                pool.dma_start(xs_dram[P * c:P * c + P, :], rowb[:, :]).then_inc(S("rows_zeroed"), 16)
            moe(0)
            broadcast_rows("mix1")
            for g in range(8):
                pool.wait_ge(*nth("rot_ready", 2 * (g + 1)))
                pool.dma_start(rot_dram[g // 2, :, 2048 * (g % 2):2048 * (g % 2) + 2048],
                               work[:, 4884 + 2048 * (g % 2):4884 + 2048 * (g % 2) + 2048]).then_inc(S(f"rot_stored{g % 2}"), 16)
            moe(1)
            broadcast_rows("s5")
            def s5_by_sine(s):
                b = s % 2
                name = f"s5_rot{s // 8}"
                if s % 8 == 0:
                    slot_wait(pool, name)
                pool.wait_ge(*nth("s5_scanned", s + 1))
                if s >= 4:
                    pool.wait_ge(*nth("s5_summed", s - 3))
                sine = ring[:, place[name], 512 * (s % 8) + SEQ:512 * (s % 8) + 2 * SEQ].unsqueeze(1).to_broadcast([P, 2, SEQ])
                nc.gpsimd.tensor_tensor(s5_q2[s % 4], s5_h[b], sine, ALU.mult).then_inc(S("s5_q2"), 1)

            for s in range(ST + 2):
                if s < ST:
                    p1, p2, v = s5_p1[s % 2], s5_p2[s % 2], s5_v[s % 3]
                    pool.wait_ge(*nth("s5_rotated", s + 1))
                    if s >= 3:
                        pool.wait_ge(*nth("s5_scanned", s - 2))
                    nc.gpsimd.tensor_tensor(v[:, 0, :], p1[:, 0, :], p2[:, 1, :], ALU.add)
                    nc.gpsimd.tensor_tensor(v[:, 1, :], p1[:, 1, :], p2[:, 0, :], ALU.subtract).then_inc(S("s5_v"), 1)
                if s >= 2:
                    s5_by_sine(s - 2)
            broadcast_rows("mlp0")
            broadcast_rows("mla")
            for b in range(2):
                pool.dma_start(pos_i[:, b:b + 1], a["positions_2"][0, P * b:P * b + P].rearrange("(t o) -> t o", o=1))\
                    .then_inc(S("pos_loaded"), 16)
            pool.wait_ge(*nth("mlp0_normed", 2))
            for dst, src, n in ((inv_f, a["inv_freq"], ROPE // 2), (g_kv, a["kv_norm_g_2"], KVL), (g_q, a["q_norm_g_2"][0], QL)):
                pool.dma_start(dst[0:1, :], src.rearrange("(o n) -> o n", o=1)).then_inc(S("attn_rows"), 16)
            pool.wait_ge(*nth("attn_rows", 48))
            for dst in (inv_f, g_kv, g_q):
                nc.gpsimd.partition_broadcast(dst, dst[0:1, :], P).then_inc(S("attn_bc"), 1)
            broadcast_rows("mlp1")

        @block.tensor
        def _(pe):
            def transposes(n, blocks, hold):
                for i, b in enumerate(blocks):
                    m = BLOCKS[b][1]
                    pe.wait_ge(*nth(hold, i + 1)) if hold else pe.wait_ge(*nth(f"x_loaded{b}", 16))
                    for h in range(2):
                        j = 2 * i + h
                        if j >= 2:
                            pe.wait_ge(*nth(f"{n}_hT", j - 1))
                        for c in range(4):
                            mm = pe.transpose(ps[:, j % 2, c * P:c * P + m], hres[0:m, b, (4 * h + c) * P:(4 * h + c + 1) * P],
                                              ident[0:m, 0:m])
                        mm.then_inc(S(f"{n}_turned"), 1)

            def project(name, c, bank, t0, n, sem_):
                w = slot_view(name, DC, 512)
                for k in range(DC):
                    mm = pe.matmul(ps[:, bank, 0:n], w[:, k, P * c:P * c + P], hT[:, k, t0:t0 + n],
                                   start=(k == 0), stop=(k == DC - 1))
                mm.then_inc(S(sem_), 1)

            def rows_out(n, blocks, pieces, left, t_off):
                last = len(pieces) - 1

                def piece(p_, b):
                    m = BLOCKS[b][1]
                    t0 = BLOCKS[b][0] - t_off
                    w = slot_view(pieces[p_], 4, D)
                    for k in range(4):
                        kk = 4 * p_ + k
                        for hf in range(2):
                            mm = pe.matmul(ps[0:m, 2 + 2 * b + hf, :], left[:, kk, t0:t0 + m],
                                           w[:, k, 512 * hf:512 * hf + 512], start=(kk == 0), stop=(kk == 4 * last + 3))
                    return mm

                for p_ in range(last - 1):
                    slot_wait(pe, pieces[p_])
                    for b in blocks:
                        mm = piece(p_, b)
                    mm.then_inc(S(f"{n}_piece"), 1)
                for b in blocks:
                    slot_wait(pe, pieces[last - 1])
                    mm = piece(last - 1, b)
                    if b == blocks[-1]:
                        mm.then_inc(S(f"{n}_piece"), 1)
                    slot_wait(pe, pieces[last])
                    piece(last, b).then_inc(S(f"{n}_mixed"), 1)

            def gate_up(x, bank, g):
                gu = ring[:, g:g + 2, :].rearrange("p u (k n) -> p k u n", k=DC)
                for k in range(DC):
                    for q in range(4):
                        mm = pe.matmul(ps[32 * q:32 * q + 32, bank, 0:256].rearrange("p (u n) -> p u n", u=2),
                                       x[:, k, :], gu[:, k, :, P * q:P * q + P], start=(k == 0), stop=(k == DC - 1))
                return mm

            def down(hT_, bank, s):
                w = ring[:, s, :].rearrange("p (k n) -> p k n", k=4)
                for k in range(4):
                    for q in range(4):
                        mm = pe.matmul(ps[32 * q:32 * q + 32, bank, 0:256], hT_[:, 32 * k:32 * k + 32],
                                       w[:, k, 256 * q:256 * q + 256], start=(k == 0), stop=(k == 3))
                return mm

            def s5_constants(k):
                if k == 4:
                    pe.wait_ge(*nth("s5_coef", 1))
                    for i in range(4):
                        mm = pe.transpose(ps[:, 6, 256 + SG * i:256 + SG * i + SG], pre[0:SG, 16 + 2 * i:18 + 2 * i, :], ident[0:SG, 0:SG])
                    mm.then_inc(S("s5_coef_turned"), 1)
                if k == 5:
                    pe.wait_ge(*nth("s5_bb", 1))
                    for i, src in enumerate((s5_t0, s5_t1)):
                        for h in range(2):
                            for c in range(4):
                                mm = pe.transpose(ps[:, (0, 1, 6, 7)[2 * i + h], 256 + SS * c:256 + SS * c + SS],
                                                  src[0:SS, P * (4 * h + c):P * (4 * h + c + 1)], ident[0:SS, 0:SS])
                    mm.then_inc(S("s5_bb_turned"), 1)
                if k >= 6:
                    for n in range(4 * (k - 6), 4 * (k - 6) + 4):
                        pe.wait_ge(*nth("s5_cm", n + 1))
                        if n >= 2:
                            pe.wait_ge(*nth("s5_cm_done", n - 1))
                        pe.transpose(ps[:, 6 + n % 2, P:2 * P], s5_cm[n % 2], ident[:, :]).then_inc(S("s5_cm_turned"), 1)

            def moe(l):
                blocks = ln_blocks[f"ffn{l}"]
                transposes(f"mix{l}", blocks, f"mix{l}_normed")
                pe.wait_ge(*nth(f"mix{l}_hT", 2 * len(blocks)))
                if l == 0:
                    pe.wait_ge(*nth("route_loaded", 16 * 8))
                    pe.wait_ge(*nth("consts", 5))
                for i, b in enumerate(blocks):
                    t0 = BLOCKS[b][0]
                    for k in range(DC):
                        pe.matmul(ps[:, 7, 36 * i:36 * i + 36], hT[:, k, t0:t0 + P], w_route[:, l, k, :],
                                  start=(k == 0 and i == 0), stop=False, skip_group_check=True)
                    mm = pe.matmul(ps[:, 7, 36 * i:36 * i + 36], ones[0:1, :], b_route[0:1, l, :],
                                   start=False, stop=(i == len(blocks) - 1), skip_group_check=True)
                mm.then_inc(S(f"logits{l}"), 1)
                pe.wait_ge(*nth(f"choice{l}", 1))
                nb = len(blocks)
                o = rowb[:, 800:800 + 32 * nb].rearrange("p (b e) -> p b e", b=nb)
                for i in range(nb):
                    for j in range(i + 1):
                        pe.matmul(ps[:, 6, 32 * i:32 * i + 32], (before if j == i else ones)[:, :], o[:, j, :],
                                  start=(i == 0 and j == 0), stop=False, skip_group_check=True)
                for j in range(nb):
                    mm = pe.matmul(ps[:, 6, 32 * nb:32 * nb + 32], ones[:, :], o[:, j, :], start=False,
                                   stop=(j == nb - 1), skip_group_check=True)
                mm.then_inc(S(f"ranks{l}"), 1)

                order, turns0 = expert_at[f"experts{l}"]

                def expert(n, st, b, first=False):
                    o_ = dict(order[b])
                    g, d_ = o_["gate"], o_["down"]
                    pe.wait_ge(*nth(f"xs_loaded{l}_{b}", (st + 1) * 16))
                    for h in range(2):
                        mm = pe.transpose(ps[:, b, P * h:P * h + P], xs_in[b][:, P * h:P * h + P], ident[:, :])
                    mm.then_inc(S(f"xs_turned{l}"), 1)
                    pe.wait_ge(*nth(f"xT_ready{l}", n + 1))
                    pe.wait_ge(loaded[g], (st + (turns0[g] + 1)) * 16)
                    pe.wait_ge(loaded[g + 1], (st + (turns0[g + 1] + 1)) * 16)
                    mm = gate_up(xT[b], 2 + b, g)
                    mm.then_inc(S(f"gate_up{l}"), 1)
                    pe.wait_ge(*nth(f"hid_ready{l}", n + 1))
                    pe.transpose(ps[:, 6 + b, 0:P], hid[b], ident[:, :]).then_inc(S(f"hid_turned{l}"), 1)
                    pe.wait_ge(*nth(f"hidT_ready{l}", n + 1))
                    pe.wait_ge(loaded[d_], (st + (turns0[d_] + 1)) * 16)
                    if not first:
                        pe.wait_ge(*nth(f"y_ready{l}", n - 1))
                    mm = down(hidT[b], 4 + b, d_)
                    mm.then_inc(S(f"down{l}"), 1)

                for b in range(2):
                    expert(b, 0, b, first=True)
                if l == 0:
                    for st in range(1, PREP_STEPS):
                        for b in range(2):
                            expert(2 * st + b, st, b)
                            s5_constants(2 * st + b)
                with pe.Fori(PREP_STEPS if l == 0 else 1, NE // 2) as i:
                    for b in range(2):
                        expert(i * 2 + b, i, b)
                rounds = pe.value_load(rounds_i[0:1, l:l + 1], min_val=1, max_val=MAX_ROUNDS)
                with pe.If(rounds > 1):
                    pe.wait_ge(*nth(f"y_ready{l}", NE))
                    with pe.Fori(1, rounds) as r:
                        with pe.Fori(0, NE) as e:
                            n = (r - 1) * NE + e
                            pe.wait_ge(*nth(f"more_xs{l}", (n + 1) * 16))
                            for h in range(2):
                                mm = pe.transpose(ps[:, 0, P * h:P * h + P], xs_in[0][:, P * h:P * h + P], ident[:, :])
                            mm.then_inc(S(f"more_turned{l}"), 1)
                            pe.wait_ge(*nth(f"more_xT{l}", n + 1))
                            pe.wait_ge(*nth(f"more_loaded{l}", (n + 1) * 48))
                            gate_up(xT[0], 2, 0).then_inc(S(f"more_gate_up{l}"), 1)
                            pe.wait_ge(*nth(f"more_hid{l}", n + 1))
                            pe.transpose(ps[:, 6, 0:P], hid[0], ident[:, :]).then_inc(S(f"more_hid_turned{l}"), 1)
                            pe.wait_ge(*nth(f"more_hidT{l}", n + 1))
                            down(hidT[0], 4, 2).then_inc(S(f"more_used{l}"), 1)
                pe.end_ifs()

            pe.wait_ge(*nth("ident", 1))
            transposes("x", [0, 1, 2], None)
            pe.wait_ge(*nth("vectors_loaded", 16 * 7))
            for c in range(DC):
                mm = pe.transpose(ps[:, 7, 12 * c:12 * c + 12], rowb[0:12, P * c:P * c + P], ident[0:12, 0:12])
            mm.then_inc(S("par_turned"), 1)
            pe.wait_ge(*nth("x_hT", 6))

            def lru_gates(m):
                pe.wait_ge(*nth("lru_conv", m + 1))
                if m >= 2:
                    pe.wait_ge(*nth("lru_sig", m - 1))
                for i in range(2):
                    for j in range(2):
                        h = slice(64 * j, 64 * j + 64)
                        mm = pe.matmul(ps[h, (0 if i == 0 else 6) + m % 2, 0:T], w_gates[h, i, m, :], lru_c[h, m, :],
                                       start=True, stop=True)
                mm.then_inc(S("lru_gated"), 1)

            for j in range(16):
                if j >= 4:
                    pe.wait_ge(*nth("lru_evac", j - 3))
                name = ("lru_x0", "lru_x1", "lru_y0", "lru_y1")[j // 4]
                if j % 4 == 0:
                    slot_wait(pe, name)
                project(name, j % 4, 2 + j % 4, 0, T, "lru_proj")
                if j == 1:
                    pe.wait_ge(*nth("gates_loaded", 64))
                    pe.wait_ge(*nth("par_ready", 1))
                if 2 <= j < 10:
                    lru_gates(j - 2)
            pe.wait_ge(*nth("lru_evac", 16))
            pe.wait_ge(*nth("lru_sig", DC))
            pe.wait_ge(*nth("lru_z", DC))
            rows_out("mix0", [0, 1, 2], ["lru_out0", "lru_out1"], lru_y, 0)
            moe(0)
            transposes("ffn0", [0, 1, 2], "ffn0_normed")
            pe.wait_ge(*nth("ffn0_hT", 6))

            t_first = NMETA - (CONV_B - 1)
            for m in range(DC):
                for i, kind in enumerate(("cg", "v", "bg")):
                    j = 3 * m + i
                    name = f"sc_{kind}{m // 4}"
                    if m % 4 == 0:
                        slot_wait(pe, name)
                    if m >= 2:
                        pe.wait_ge(*nth("sc_z", m - 1))
                    bank = 2 + 3 * (m % 2) + i
                    t0, n = (t_first, TC) if kind != "bg" else (NMETA, SEQ)
                    project(name, m % 4, bank, t0, n, f"sc_{kind}")
            pe.wait_ge(*nth("sc_z", DC))
            rows_out("mix1", [1, 2], ["sc_out0", "sc_out1"], sc_z, NMETA)
            moe(1)
            transposes("ffn1", [1, 2], "ffn1_normed")
            pe.wait_ge(*nth("ffn1_hT", 4))
            pe.wait_ge(*nth("maps_ready", 1))
            mp = maps

            def s5_in(s0):
                for s in (s0, s0 + 1):
                    if s >= 4:
                        pe.wait_ge(*nth("s5_rotated", s - 3))
                for i in range(2):
                    for s in (s0, s0 + 1):
                        m, j = s // 4, s % 4
                        r = slice(32 * j, 32 * j + 32)
                        mm = pe.matmul(ps[:, s % 4, SEQ * i:SEQ * i + SEQ], mp[r, i, m, :], hT[r, m, NMETA:T],
                                       start=True, stop=True)
                        if i == 1:
                            mm.then_inc(S("s5_bu"), 1)

            def s5_out(s0):
                m = s0 // 4
                pe.wait_ge(*nth("s5_q", s0 + 2))
                pe.wait_ge(*nth("s5_q2", s0 + 2))
                if s0 % 4 == 0 and m >= 2:
                    pe.wait_ge(*nth("s5_y", m - 1))
                if s0 == 0:
                    pe.wait_ge(*nth("s5_ncre", 1))
                for term in range(4):
                    for s in (s0, s0 + 1):
                        c = slice(32 * (s % 4), 32 * (s % 4) + 32)
                        q1, q2 = s5_q1[s % 4], s5_q2[s % 4]
                        left, right = ((mp[:, 2, m, c], q1[:, 0, :]), (s5_ncre[:, m, c], q2[:, 1, :]),
                                       (mp[:, 3, m, c], q1[:, 1, :]), (mp[:, 3, m, c], q2[:, 0, :]))[term]
                        mm = pe.matmul(ps[c, 4 + m % 2, 0:SEQ], left, right, start=(term == 0), stop=(term == 3),
                                       skip_group_check=True)
                        if term == 3:
                            mm.then_inc(S("s5_summed"), 1)

            for s in range(0, ST + 4, 2):
                if s < ST:
                    s5_in(s)
                if s >= 4:
                    s5_out(s - 4)
            pe.wait_ge(*nth("s5_g", DC))
            for m in range(DC):
                for i, kind in enumerate("vg"):
                    name = f"glu_{kind}{m // 4}"
                    if m % 4 == 0:
                        slot_wait(pe, name)
                    if m >= 2:
                        pe.wait_ge(*nth("glu_done", m - 1))
                    w = slot_view(name, DC, 512)
                    for k in range(DC):
                        mm = pe.matmul(ps[:, 2 * (m % 2) + i, 0:SEQ], w[:, k, P * (m % 4):P * (m % 4) + P], s5_g[:, k, :],
                                       start=(k == 0), stop=(k == DC - 1))
                mm.then_inc(S("glu_proj"), 1)
            pe.wait_ge(*nth("glu_done", DC))
            rows_out("s5", [1, 2], ["s5_out0", "s5_out1"], s5_y, NMETA)

            def mlp(layer, before_):
                transposes(before_, [1, 2], f"{before_}_normed")
                pe.wait_ge(*nth(f"{before_}_hT", 4))
                for c in range(DFF // P):
                    name = f"ff1_{layer}_{c // 4}"
                    if c % 4 == 0:
                        slot_wait(pe, name)
                    if c >= 4:
                        pe.wait_ge(*nth(f"ff_relu{layer}", c - 3))
                    project(name, c % 4, 2 + c % 4, NMETA, SEQ, f"ff_proj{layer}")
                pe.wait_ge(*nth(f"ff_sq{layer}", DFF // P))
                rows_out(f"mlp{layer}", [1, 2], [f"ff2_{layer}_{j}" for j in range(8)], ff, NMETA)

            mlp(0, "s5")
            transposes("mlp0", [1, 2], "mlp0_normed")
            pe.wait_ge(*nth("mlp0_hT", 4))
            for name, n, bank in (("kv_a", KVL + ROPE, 2), ("q_a", QL, 4)):
                slot_wait(pe, name)
                w = slot_view(name, DC, n)
                for b in range(2):
                    for k in range(DC):
                        mm = pe.matmul(ps[:, bank + b, 0:n], hT[:, k, NMETA + P * b:NMETA + P * b + P], w[:, k, :],
                                       start=(k == 0), stop=(k == DC - 1))
                    mm.then_inc(S("latent"), 1)
            pe.wait_ge(*nth("kv_normed", 2))
            for k in range(KVL // P):
                for b in range(2):
                    mm = pe.transpose(ps[:, 0, 256 * k + P * b:256 * k + P * b + P], ckv[:, b, P * k:P * k + P], ident[:, :])
            mm.then_inc(S("ckv_turned"), 1)
            pe.wait_ge(*nth("q_normed", 2))
            for k in range(2):
                for b in range(2):
                    mm = pe.transpose(ps[:, 1, 256 * k + P * b:256 * k + P * b + P], cq[:, b, P * k:P * k + P], ident[:, :])
            for b in range(2):
                mm = pe.transpose(ps[:, 6, P * b:P * b + P], cq[:, b, 2 * P:3 * P], ident[:, :])
            mm.then_inc(S("cq_turned"), 1)
            pe.wait_ge(*nth("ckvT", 1))
            slot_wait(pe, "kv_b")
            wkv = slot_view("kv_b", 2, HEADS * (NOPE + VH)).rearrange("p k (h n) -> p k h n", h=HEADS)
            for h in range(HEADS):
                for k in range(2):
                    mm = pe.matmul(ps[:, 2 + h // 2, SEQ * (h % 2):SEQ * (h % 2) + SEQ], wkv[:, k, h, 0:NOPE], ckvT[:, k, :],
                                   start=(k == 0), stop=(k == 1), skip_group_check=True)
                if h % 2:
                    mm.then_inc(S("keys"), 1)
            pe.wait_ge(*nth("cqT", 1))
            for b in range(2):
                for hh in range(2):
                    bank = (7, 0, 1, 6)[2 * b + hh]
                    for k in range(2):
                        mm = pe.matmul(ps[:, bank, :].rearrange("p (h n) -> p h n", h=4), ckvT[:, k, P * b:P * b + P],
                                       wkv[:, k, 4 * hh:4 * hh + 4, NOPE:NOPE + VH], start=(k == 0), stop=(k == 1))
                    mm.then_inc(S("values"), 1)
            for h in range(HEADS):
                name = f"q_b{h // 4}"
                if h % 4 == 0:
                    slot_wait(pe, name)
                w = slot_view(name, 3, 768).rearrange("p k (h n) -> p k h n", h=4)
                if h % 2 == 0:
                    pe.wait_ge(*nth("keys_out", h // 2 + 1))
                for k in range(3):
                    mm = pe.matmul(ps[:, 2 + h // 2, SEQ * (h % 2):SEQ * (h % 2) + SEQ], w[:, k, h % 4, 0:NOPE], cqT[:, k, :],
                                   start=(k == 0), stop=(k == 2), skip_group_check=True)
                if h % 2:
                    mm.then_inc(S("queries"), 1)
            for b in range(2):
                bank = (7, 0)[b]
                pe.wait_ge(*nth("values_out", b + 1))
                for hh in range(2):
                    w = slot_view(f"q_b{hh}", 3, 768).rearrange("p k (h n) -> p k h n", h=4)
                    for k in range(3):
                        mm = pe.matmul(ps[:, bank, 256 * hh:256 * hh + 256].rearrange("p (h n) -> p h n", h=4),
                                       cqT[:, k, P * b:P * b + P], w[:, k, :, NOPE:NOPE + ROPE],
                                       start=(k == 0), stop=(k == 2), skip_group_check=True)
                mm.then_inc(S("q_rope"), 1)
            for b in range(2):
                pe.wait_ge(*nth("q_rotated", b + 1))
                pe.wait_ge(*nth("values_out", 4))
                for g in range(4):
                    mm = pe.transpose(ps[:, (1, 6)[b], P * g:P * g + P], qr_rot_b[b].rearrange("p h n -> p (h n)")[:, P * g:P * g + P],
                                      ident[:, :])
                mm.then_inc(S("qr_turned"), 1)
            pe.wait_ge(*nth("k_rotated", 2))
            pe.wait_ge(*nth("q_rotated", 1))
            for b in range(2):
                mm = pe.transpose(ps[:, 7, P * b:P * b + P], kr2[:, b].rearrange("p a n -> p (a n)"), ident[:, :])
            mm.then_inc(S("kr_turned"), 1)
            pe.wait_ge(*nth("attn_left", 1))

            def scores(u):
                h, b = u // 2, u % 2
                if u >= 4:
                    pe.wait_ge(*nth("score_max", u - 3))
                n = P * (b + 1)
                r = slice(64 * (h % 2), 64 * (h % 2) + 64)
                pe.matmul(ps[:, (2 + u % 4) % 4, 0:n], qnT[:, h, P * b:P * b + P], knT[:, h, 0:n], start=True, stop=False)
                pe.matmul(ps[:, (2 + u % 4) % 4, 0:n], qrT[r, h // 2, P * b:P * b + P], krT[r, 0:n], start=False, stop=True)\
                    .then_inc(S("scores"), 1)

            def turn(u):
                b = u % 2
                pe.wait_ge(*nth("prob_normed", u + 1))
                if u >= 2:
                    pe.wait_ge(*nth("probT", u - 1))
                for c in range(b + 1):
                    mm = pe.transpose(ps[:, 4 + b, P * c:P * c + P], prob[u % 4][:, P * c:P * c + P], ident[:, :])
                mm.then_inc(S("prob_turned"), 1)

            def weigh(u):
                h, b = u // 2, u % 2
                pe.wait_ge(*nth("probT", u + 1))
                if h >= 2 and b == 0:
                    pe.wait_ge(*nth("oT", h - 1))
                for c in range(b + 1):
                    mm = pe.matmul(ps[:, 6 + h % 2, P * b:P * b + P], val[:, c, VH * h:VH * h + VH], probT[b][:, c, :],
                                   start=(c == 0), stop=(c == b), skip_group_check=True)
                if b == 1:
                    mm.then_inc(S("weighed"), 1)

            for u in range(2 * HEADS + 4):
                if u < 2 * HEADS:
                    scores(u)
                if 3 <= u < 2 * HEADS + 3:
                    turn(u - 3)
                if u >= 4:
                    weigh(u - 4)
            pe.wait_ge(*nth("oT", HEADS))
            rows_out("mla", [1, 2], ["attn_out0", "attn_out1"], oT, NMETA)
            mlp(1, "mla")

        @block.scalar
        def _(act):
            A = nc.scalar.activation
            step = [0]

            def link(ins):
                step[0] += 1
                ins.then_inc(S("act_step"), 1)
                act.wait_ge(*nth("act_step", step[0]))

            def evac_turned(n, blocks):
                for i, b in enumerate(blocks):
                    t0, m = BLOCKS[b]
                    for h in range(2):
                        j = 2 * i + h
                        act.wait_ge(*nth(f"{n}_turned", j + 1))
                        A(hT[:, 4 * h:4 * h + 4, t0:t0 + m], ps[:, j % 2, :].rearrange("p (c n) -> p c n", c=4)[:, :, 0:m],
                          ACT.Copy).then_inc(S(f"{n}_hT"), 1)

            def deviations(n):
                for i, b in enumerate(ln_blocks[n]):
                    m = BLOCKS[b][1]
                    act.wait_ge(*nth(f"{n}_var", i + 1))
                    A(mean_var[0:m, i, 2:3], mean_var[0:m, i, 1:2], ACT.Sqrt, bias=eps_t[0:m, 0:1]).then_inc(S(f"{n}_sd"), 1)

            def s5_constants(k):
                if k == 2:
                    act.wait_ge(*nth("s5_loaded", 16 * 7))
                    A(pre[0:SG, 2, 1:2], pre[0:SG, 2, 0:1], ACT.Exp).then_inc(S("p_dt"), 1)
                    act.wait_ge(*nth("p_half", 1))
                    A(pre[0:SG, 4, :], pre[0:SG, 3, :], ACT.Tanh).then_inc(S("p_tanh"), 1)
                    act.wait_ge(*nth("p_theta", 1))
                    A(pre[0:SG, 8, :], pre[0:SG, 7, :], ACT.Sin, scale=0.5).then_inc(S("p_sin"), 1)
                    A(pre[0:SG, 9, :], pre[0:SG, 7, :], ACT.Sin).then_inc(S("p_sin"), 1)
                    A(pre[0:SG, 10, :], pre[0:SG, 7, :], ACT.Abs).then_inc(S("p_sin"), 1)
                    act.wait_ge(*nth("p_sin", 3))
                    A(pre[0:SG, 10, :], pre[0:SG, 10, :], ACT.Sin, scale=-1.0, bias=eps_t[0:SG, 1:2]).then_inc(S("p_sin"), 1)

            def moe(l):
                blocks = ln_blocks[f"ffn{l}"]
                deviations(f"mix{l}")
                evac_turned(f"mix{l}", blocks)
                nb = len(blocks)
                act.wait_ge(*nth(f"glog{l}", 1))
                rt = tmp_a[:, :]
                A(rt[:, 16:16 + 4 * nb], rt[:, 0:4 * nb], ACT.Exp).then_inc(S(f"gexp{l}"), 1)
                act.wait_ge(*nth(f"vdiff{l}", 1))
                A(rt[:, 36:36 + nb], rt[:, 32:32 + nb], ACT.Exp).then_inc(S(f"vexp{l}"), 1)
                act.wait_ge(*nth(f"scattered{l}", 32 * nb))
                act.wait_ge(*nth(f"mix{l}_normed", nb))

                def load_rows(row0, b):
                    act.dma_start(xs_in[b], xs_dram[bass.ds(row0, CAP), :].rearrange("s (q c) -> (s q) c", q=4))\
                        .then_inc(S(f"xs_loaded{l}_{b}"), 16)

                def expert(n, b):
                    act.wait_ge(*nth(f"gate_up{l}", n + 1))
                    A(silu[b], ps[:, 2 + b, 0:P], ACT.Silu).then_inc(S(f"silu{l}"), 1)
                    act.wait_ge(*nth(f"hid_turned{l}", n + 1))
                    A(hidT[b], ps[:, 6 + b, 0:P], ACT.Copy).then_inc(S(f"hidT_ready{l}"), 1)

                load_rows(0, 0)
                load_rows(CAP, 1)
                if l == 0:
                    for st in range(PREP_STEPS):
                        for b in range(2):
                            expert(2 * st + b, b)
                            load_rows((2 * st + 2 + b) * CAP, b)
                            s5_constants(2 * st + b)
                with act.Fori(PREP_STEPS if l == 0 else 0, NE // 2 - 1) as i:
                    for b in range(2):
                        expert(i * 2 + b, b)
                        load_rows(i * (2 * CAP) + (2 * CAP + CAP * b), b)
                for b in range(2):
                    expert(NE - 2 + b, b)
                rounds = act.value_load(rounds_i[0:1, l:l + 1], min_val=1, max_val=MAX_ROUNDS)
                with act.If(rounds > 1):
                    with act.Fori(1, rounds) as r:
                        with act.Fori(0, NE) as e:
                            n = (r - 1) * NE + e
                            act.wait_ge(*nth(f"more_gate_up{l}", n + 1))
                            A(silu[0], ps[:, 2, 0:P], ACT.Silu).then_inc(S(f"more_silu{l}"), 1)
                            act.wait_ge(*nth(f"more_hid_turned{l}", n + 1))
                            A(hidT[0], ps[:, 6, 0:P], ACT.Copy).then_inc(S(f"more_hidT{l}"), 1)
                act.end_ifs()
                deviations(f"ffn{l}")
                evac_turned(f"ffn{l}", blocks)

            evac_turned("x", [0, 1, 2])
            act.wait_ge(*nth("lam", 1))
            A(soft[:, 1, :], soft[:, 0, :], ACT.Exp, scale=-1.0).then_inc(S("lam_exp"), 1)

            def lru_gate_act(m):
                act.wait_ge(*nth("lru_gated", m + 1))
                A(lru_r[:, m, :], ps[:, m % 2, 0:T], ACT.Sigmoid, bias=par[:, m, 5:6]).then_inc(S("act_r"), 1)
                A(lru_i[:, m, :], ps[:, 6 + m % 2, 0:T], ACT.Sigmoid, bias=par[:, m, 6:7]).then_inc(S("lru_sig"), 1)
                act.wait_ge(*nth("act_r", m + 1))
                A(lru_r[:, m, :], lru_r[:, m, :], ACT.Tanh, scale=soft[:, 4, m:m + 1]).then_inc(S("lru_tanh"), 1)

            for j in range(DC):
                act.wait_ge(*nth("lru_proj", j + 1))
                A(lru_x[:, j, PAD_A:PAD_A + T], ps[:, 2 + j % 4, 0:T], ACT.Copy).then_inc(S("lru_evac"), 1)
                if j == 2:
                    act.wait_ge(*nth("soft", 1))
                if j >= 2:
                    lru_gate_act(j - 2)
            for j in range(DC, 2 * DC):
                act.wait_ge(*nth("lru_proj", j + 1))
                A(lru_y[:, j - DC, :], ps[:, 2 + j % 4, 0:T], ACT.Copy).then_inc(S("lru_evac"), 1)
                if j < DC + 2:
                    lru_gate_act(j - 2)
                if j == DC + 2:
                    act.wait_ge(*nth("lru_tanh", DC))
                    A(lru_q[:, :, :], lru_r[:, :, :], ACT.Sqrt).then_inc(S("lru_sqrt"), 1)
                if j >= DC + 3 and (j - DC) % 4 == 3:
                    c = slice(j - DC - 3, j - DC + 1)
                    act.wait_ge(*nth("lru_evac", j + 1))
                    A(lru_y[:, c, :], lru_y[:, c, :], ACT.Gelu_apprx_tanh).then_inc(S("lru_gelu"), 1)
            moe(0)
            def rotations(g):
                b = g % 2
                act.wait_ge(*nth("rot_turns", g + 1))
                A(rot[b][:, :, 0, :], rot[b][:, :, 1, :], ACT.Abs).then_inc(S("rot_abs"), 1)
                act.wait_ge(*nth("rot_abs", g + 1))
                A(rot[b][:, :, 0, :], rot[b][:, :, 0, :], ACT.Sin, scale=-2 * PI_IN, bias=eps_t[:, 1:2]).then_inc(S("rot_ready"), 1)
                A(rot[b][:, :, 1, :], rot[b][:, :, 1, :], ACT.Sin, scale=2 * PI_IN).then_inc(S("rot_ready"), 1)

            for m in range(DC):
                act.wait_ge(*nth("sc_cg", m + 1))
                if m >= 2:
                    act.wait_ge(*nth("sc_gated", m - 1))
                A(sc_cg[m % 2], ps[:, 2 + 3 * (m % 2), 0:TC], ACT.Copy).then_inc(S("sc_cg_out"), 1)
                if m >= 1:
                    rotations(m - 1)
            rotations(DC - 1)
            moe(1)
            act.wait_ge(*nth("maps_ready", 1))
            act.wait_ge(*nth("ffn1_normed", 2))
            A(s5_ncre, maps[:, 2], ACT.Copy, scale=-1.0).then_inc(S("s5_ncre"), 1)
            for m in range(DC):
                act.wait_ge(*nth("s5_y", m + 1))
                A(s5_g[:, m, :], s5_y[:, m, :], ACT.Gelu_apprx_tanh).then_inc(S("s5_g"), 1)
            for m in range(DC):
                act.wait_ge(*nth("glu_proj", m + 1))
                if m >= 2:
                    act.wait_ge(*nth("glu_done", m - 1))
                A(s5_sig[m % 2], ps[:, 2 * (m % 2) + 1, 0:SEQ], ACT.Sigmoid).then_inc(S("glu_sig"), 1)

            def mlp(layer, before_):
                deviations(before_)
                evac_turned(before_, [1, 2])
                for c in range(DFF // P):
                    act.wait_ge(*nth(f"ff_proj{layer}", c + 1))
                    A(ff[:, c, :], ps[:, 2 + c % 4, 0:SEQ], ACT.Relu).then_inc(S(f"ff_relu{layer}"), 1)

            mlp(0, "s5")
            deviations("mlp0")
            evac_turned("mlp0", [1, 2])
            act.wait_ge(*nth("angles", 1))
            A(sin_t, ang, ACT.Sin).then_inc(S("a_tab"), 1)
            A(angk, ang, ACT.Abs).then_inc(S("a_tab"), 1)
            act.wait_ge(*nth("a_tab", 2))
            A(cos_t, angk, ACT.Sin, scale=-1.0, bias=eps_t[:, 1:2]).then_inc(S("a_tab"), 1)
            for i, (bank, n, full, dst) in enumerate(((2, KVL, KVL + ROPE, ckv), (4, QL, QL, cq))):
                for b in range(2):
                    act.wait_ge(*nth("latent", 2 * i + b + 1))
                    A(dst[:, b, :], ps[:, bank + b, 0:full], ACT.Copy).then_inc(S("latent_out"), 1)
                    A(rope_u[:, 0:n], ps[:, bank + b, 0:n], ACT.Square, accum_out=sq_sum[:, 2 * i + b:2 * i + b + 1])\
                        .then_inc(S("latent_sq"), 1)
                    act.wait_ge(*nth("latent_sq", 2 * i + b + 1))
            for i, n in enumerate((KVL, QL)):
                A(sq_sum[:, 4 + 2 * i:6 + 2 * i], sq_sum[:, 2 * i:2 * i + 2], ACT.Sqrt, scale=1.0 / n, bias=eps_t[:, 2:3])\
                    .then_inc(S("latent_rms"), 1)
            act.wait_ge(*nth("ckv_turned", 1))
            A(ckvT, ps[:, 0, :].rearrange("p (k n) -> p k n", k=2), ACT.Copy).then_inc(S("ckvT"), 1)
            act.wait_ge(*nth("cq_turned", 1))
            A(cqT[:, 0:2, :], ps[:, 1, :].rearrange("p (k n) -> p k n", k=2), ACT.Copy).then_inc(S("cqT_a"), 1)
            A(cqT[:, 2, :], ps[:, 6, 0:256], ACT.Copy).then_inc(S("cqT_a"), 1)
            act.wait_ge(*nth("cqT_a", 2))
            act.sem_inc(S("cqT"), 1)
            for j in range(4):
                act.wait_ge(*nth("keys", j + 1))
                A(knT[:, 2 * j:2 * j + 2, :], ps[:, 2 + j, :].rearrange("p (h n) -> p h n", h=2), ACT.Copy).then_inc(S("keys_out"), 1)
            for j in range(4):
                act.wait_ge(*nth("queries", j + 1))
                A(qnT[:, 2 * j:2 * j + 2, :], ps[:, 2 + j, :].rearrange("p (h n) -> p h n", h=2), ACT.Copy).then_inc(S("queries_out"), 1)
            for b in range(2):
                act.wait_ge(*nth("qr_turned", b + 1))
                A(qrT[:, :, P * b:P * b + P], ps[:, (1, 6)[b], :].rearrange("p (g n) -> p g n", g=4), ACT.Copy)\
                    .then_inc(S("queries_out"), 1)
            act.wait_ge(*nth("kr_turned", 1))
            A(krT, ps[:, 7, 0:SEQ], ACT.Copy).then_inc(S("queries_out"), 1)
            act.wait_ge(*nth("queries_out", 7))
            act.sem_inc(S("attn_left"), 1)
            for u in range(2 * HEADS + 3):
                if u < 2 * HEADS:
                    n = P * (u % 2 + 1)
                    act.wait_ge(*nth("score_max", u + 1))
                    A(prob[u % 4][:, 0:n], prob[u % 4][:, 0:n], ACT.Exp, bias=sq_sum[:, 16 + u:17 + u], scale=1.0,
                      accum_out=sq_sum[:, 32 + u:33 + u]).then_inc(S("prob_exp"), 1)
                if u >= 3:
                    v = u - 3
                    act.wait_ge(*nth("prob_turned", v + 1))
                    A(probT[v % 2][:, 0:v % 2 + 1, :], ps[:, 4 + v % 2, 0:P * (v % 2 + 1)].rearrange("p (c n) -> p c n", n=P),
                      ACT.Copy).then_inc(S("probT"), 1)
            mlp(1, "mla")
            deviations("mlp1")

        @block.vector
        def _(dve):
            V = nc.vector
            step = [0]

            def link(ins):
                step[0] += 1
                ins.then_inc(S("dve_step"), 1)
                dve.wait_ge(*nth("dve_step", step[0]))

            def statistics(n, i, b):
                m = BLOCKS[b][1]
                x = tmps[i % 2][0:m, :]
                V.bn_stats(stats[0:m, i, 0:6], x[:, 0:512])
                link(V.bn_stats(stats[0:m, i, 6:12], x[:, 512:1024]))
                V.bn_aggr(mean_var[0:m, i, 0:2], stats[0:m, i, :]).then_inc(S(f"{n}_var"), 1)

            def normalised(n, i, b, write):
                m = BLOCKS[b][1]
                x = tmps[i % 2][0:m, :]
                if i == 0:
                    dve.wait_ge(*nth("rows_ready", 2 * (ln_order.index(n) + 1)))
                dve.wait_ge(*nth(f"{n}_var", i + 1))
                link(V.scalar_tensor_tensor(out=x, in0=x, scalar=mean_var[0:m, i, 0:1], in1=gain_bc[0:m, :],
                                            op0=ALU.subtract, op1=ALU.mult))
                dve.wait_ge(*nth(f"{n}_sd", i + 1))
                link(V.reciprocal(mean_var[0:m, i, 3:4], mean_var[0:m, i, 2:3]))
                src, dst, bias = write(x, hres[0:m, b, :], bias_bc[0:m, :])
                V.scalar_tensor_tensor(out=dst, in0=src, scalar=mean_var[0:m, i, 3:4], in1=bias, op0=ALU.mult, op1=ALU.add)\
                    .then_inc(S(f"{n}_normed"), 1)

            def plain(x, dst, bias):
                return x, dst, bias

            def to_packed(x, dst, bias):
                return packed(x), two(dst, P), packed(bias)

            def mix_norm(n, write=plain):
                blocks = ln_blocks[n]
                for i, b in enumerate(blocks):
                    m = BLOCKS[b][1]
                    dve.wait_ge(*nth(f"{n}_mixed", i + 1))
                    link(V.scalar_tensor_tensor(out=tmps[i % 2][0:m, :], in0=hres[0:m, b, :], scalar=ALPHA,
                                                in1=ps[0:m, 2 + 2 * b:4 + 2 * b, :].rearrange("p a n -> p (a n)"),
                                                op0=ALU.mult, op1=ALU.add))
                    statistics(n, i, b)
                    normalised(n, i, b, write)

            def route(l):
                nb = len(ln_blocks[f"ffn{l}"])
                rt, rb = tmp_a[:, :], rowb[:, :]

                def v3(t, at, w):
                    return t[:, at:at + nb * w].rearrange("p (b w) -> p b w", b=nb)

                glog, gm = v3(rt, 0, 4), rt[:, 12:12 + nb]
                gexp, vdiff, vexp = v3(rt, 16, 4), rt[:, 32:32 + nb], rt[:, 36:36 + nb]
                gsum, gidx, pen = rt[:, 40:40 + nb], rt[:, 44:44 + nb], v3(rt, 48, 4)
                v1, v2, i1, i2 = (rt[:, 64 + 4 * j:64 + 4 * j + nb] for j in range(4))
                p1, p2, rk1, rk2 = (rt[:, 80 + 4 * j:80 + 4 * j + nb] for j in range(4))
                cmax, nround, fl = rt[:, 96:97], rt[:, 97:98], rt[:, 100:108]
                g4 = v3(rt, 112, 4)
                em, ind = v3(rb, 0, NE), v3(rb, 96, NE)
                o1, o2 = v3(rb, 192, NE), v3(rb, 288, NE)
                both = v3(rb, 800, NE)
                rank, cmp8 = v3(rb, 384, NE), v3(rb, 480, MAX_ROUNDS - 1)
                lo = ps[:, 7, 0:36 * nb].rearrange("p (b n) -> p b n", b=nb)

                def wide(x, w):
                    return x.unsqueeze(2).to_broadcast([P, nb, w])

                def iot(w):
                    return iota_e[:, 0:w].unsqueeze(1).to_broadcast([P, nb, w])

                def first_index(values, top, w, scratch, dst):
                    link(V.tensor_tensor(scratch, values, wide(top, w), ALU.is_lt))
                    link(V.scalar_tensor_tensor(out=scratch, in0=scratch, scalar=BIG, in1=iot(w), op0=ALU.mult, op1=ALU.add))
                    link(V.tensor_reduce(dst, scratch, AX.X, ALU.min))

                dve.wait_ge(*nth(f"logits{l}", 1))
                if l == 0:
                    dve.wait_ge(*nth("consts", 5))
                    dve.wait_ge(*nth("rows_zeroed", 16 * 8))
                V.tensor_copy(em, lo[:, :, NG:NG + NE])
                link(V.tensor_reduce(gm, lo[:, :, 0:NG], AX.X, ALU.max))
                V.tensor_tensor(glog, lo[:, :, 0:NG], wide(gm, NG), ALU.subtract).then_inc(S(f"glog{l}"), 1)
                link(V.tensor_copy(g4, lo[:, :, 0:NG]))
                first_index(g4, gm, NG, pen, gidx)
                link(V.tensor_tensor(pen, iot(NG), wide(gidx, NG), ALU.is_equal))
                link(V.tensor_scalar(pen, pen, 1.0, BIG, ALU.subtract, ALU.mult))
                em4 = em.rearrange("p b (g e) -> p b g e", g=NG)
                for j in range(nb):
                    V.tensor_tensor(em4[:, j], em4[:, j], pen[:, j].unsqueeze(2).to_broadcast([P, NG, EPG]), ALU.add)\
                        .then_inc(S(f"masked{l}"), 1)
                dve.wait_ge(*nth(f"masked{l}", nb))
                for v, ix, o, last in ((v1, i1, o1, False), (v2, i2, o2, True)):
                    link(V.tensor_reduce(v, em, AX.X, ALU.max))
                    first_index(em, v, NE, ind, ix)
                    link(V.tensor_tensor(o, iot(NE), wide(ix, NE), ALU.is_equal))
                    if not last:
                        link(V.scalar_tensor_tensor(out=em, in0=o, scalar=-3.0 * BIG, in1=em, op0=ALU.mult, op1=ALU.add))
                V.tensor_tensor(vdiff, v2, v1, ALU.subtract).then_inc(S(f"vdiff{l}"), 1)
                if nb == 3:
                    V.tensor_scalar(o1[:, 0], o1[:, 0], first_rows[:, 0:1], None, ALU.mult)
                    link(V.tensor_scalar(o2[:, 0], o2[:, 0], first_rows[:, 0:1], None, ALU.mult))
                V.tensor_tensor(both, o1, o2, ALU.add).then_inc(S(f"choice{l}"), 1)
                dve.wait_ge(*nth(f"gexp{l}", 1))
                link(V.tensor_reduce(gsum, gexp, AX.X, ALU.add))
                link(V.reciprocal(gsum, gsum))
                dve.wait_ge(*nth(f"vexp{l}", 1))
                link(V.tensor_scalar(p1, vexp, 1.0, None, ALU.add))
                link(V.reciprocal(p1, p1))
                link(V.tensor_tensor(p1, p1, gsum, ALU.mult))
                V.tensor_copy(gates[:, 0:nb, 0], p1)
                link(V.tensor_tensor(gates[:, 0:nb, 1], p1, vexp, ALU.mult))
                dve.wait_ge(*nth(f"ranks{l}", 1))
                link(V.tensor_copy(rank, ps[:, 6, 0:32 * nb].rearrange("p (b e) -> p b e", b=nb)))
                for k, (o, ix, rk) in enumerate(((o1, i1, rk1), (o2, i2, rk2))):
                    link(V.tensor_tensor(ind, o, rank, ALU.mult))
                    link(V.tensor_reduce(rk, ind, AX.X, ALU.add))
                    link(V.tensor_tensor(cmp8, wide(rk, MAX_ROUNDS - 1), marks[:, :].unsqueeze(1).to_broadcast([P, nb, MAX_ROUNDS - 1]),
                                         ALU.is_ge))
                    link(V.tensor_reduce(p2, cmp8, AX.X, ALU.add))
                    link(V.scalar_tensor_tensor(out=rk, in0=p2, scalar=float(ROUND_ROWS - CAP), in1=rk, op0=ALU.mult, op1=ALU.add))
                    link(V.scalar_tensor_tensor(out=rk, in0=ix, scalar=float(CAP), in1=rk, op0=ALU.mult, op1=ALU.add))
                    ins = V.tensor_copy(slots_u[:, 0:nb, k], rk)
                    if k == 0:
                        link(ins)
                ins.then_inc(S(f"slots_ready{l}"), 1)
                link(V.tensor_reduce(cmax, ps[:, 6, 32 * nb:32 * nb + 32], AX.X, ALU.max))
                link(V.tensor_scalar(fl, marks[:, :], cmax, None, ALU.is_lt))
                link(V.tensor_reduce(nround, fl, AX.X, ALU.add))
                link(V.tensor_scalar(nround, nround, 1.0, None, ALU.add))
                V.tensor_copy(rounds_i[0:1, l:l + 1], nround[0:1, :]).then_inc(S(f"rounds_known{l}"), 1)

            lr, li = pre[0:SG, 0, :], pre[0:SG, 1, :]
            dt = pre[0:SG, 2, 1:2]

            def pr(i):
                return pre[0:SG, i, :]

            def prep_coef():
                dve.wait_ge(*nth("p_dt", 1))
                link(V.tensor_scalar(pr(3), lr, dt, None, ALU.mult))
                V.tensor_scalar(pr(3), pr(3), -0.5, None, ALU.mult).then_inc(S("p_half"), 1)
                link(V.tensor_scalar(pr(5), li, dt, None, ALU.mult))
                link(V.tensor_scalar(pr(6), pr(5), 1.0 / TWO_PI, ROUNDER, ALU.mult, ALU.add))
                link(V.tensor_scalar(pr(6), pr(6), ROUNDER, None, ALU.subtract))
                for c in (PI2_A, PI2_B, PI2_C):
                    link(V.scalar_tensor_tensor(out=pr(5), in0=pr(6), scalar=-c, in1=pr(5), op0=ALU.mult, op1=ALU.add))
                V.tensor_scalar(pr(7), pr(5), PI_IN, -PI_IN, ALU.min, ALU.max).then_inc(S("p_theta"), 1)
                dve.wait_ge(*nth("p_tanh", 1))
                link(V.tensor_scalar(pr(11), pr(4), 1.0, None, ALU.add))
                link(V.reciprocal(pr(11), pr(11)))
                V.tensor_scalar(pr(18), pr(11), 2.0, -1.0, ALU.mult, ALU.add)
                link(V.scalar_tensor_tensor(out=pr(12), in0=pr(4), scalar=-2.0, in1=pr(11), op0=ALU.mult, op1=ALU.mult))
                dve.wait_ge(*nth("p_sin", 4))
                link(V.tensor_tensor(pr(13), pr(12), pr(10), ALU.mult))
                link(V.tensor_tensor(pr(14), pr(8), pr(8), ALU.mult))
                link(V.scalar_tensor_tensor(out=pr(13), in0=pr(14), scalar=-2.0, in1=pr(13), op0=ALU.mult, op1=ALU.add))
                link(V.tensor_tensor(pr(14), pr(18), pr(9), ALU.mult))

            def prep_coef_2():
                V.tensor_tensor(pr(11), lr, lr, ALU.mult)
                link(V.tensor_tensor(pr(12), li, li, ALU.mult))
                link(V.tensor_tensor(pr(11), pr(11), pr(12), ALU.add))
                link(V.reciprocal(pr(11), pr(11)))
                V.tensor_tensor(pr(12), pr(13), lr, ALU.mult)
                link(V.tensor_tensor(pr(15), pr(14), li, ALU.mult))
                link(V.tensor_tensor(pr(12), pr(12), pr(15), ALU.add))
                link(V.tensor_tensor(pr(20), pr(12), pr(11), ALU.mult))
                V.tensor_tensor(pr(12), pr(14), lr, ALU.mult)
                link(V.tensor_tensor(pr(15), pr(13), li, ALU.mult))
                link(V.tensor_tensor(pr(12), pr(12), pr(15), ALU.subtract))
                link(V.tensor_tensor(pr(22), pr(12), pr(11), ALU.mult))
                link(V.tensor_scalar(pr(16), pr(5), 1.0 / TWO_PI, None, ALU.mult))
                for i in (16, 18, 20, 22):
                    link(V.tensor_copy(pr(i + 1), pr(i)))
                link(V.tensor_copy(pr(17), pr(16)))
                V.tensor_copy(pr(15), pr(16)).then_inc(S("s5_coef"), 1)

            def g3(t):
                return t[0:SS, :].rearrange("p (g c) -> p g c", c=SC)

            def bc(t):
                return t.unsqueeze(2).to_broadcast([SS, SG, SC])

            def prep_bb():
                dve.wait_ge(*nth("s5_coef_turned", 1))
                for h in range(2):
                    r = slice(64 * h, 64 * h + 64)
                    V.tensor_copy(phase[r, 0, :], ps[r, 6, 256 + h:256 + SG:2])
                    ins = V.tensor_copy(decay[r, :], ps[r, 6, 256 + SG + h:256 + 2 * SG:2])
                link(ins)
                cre, cim = pre[0:SS, 3, :], pre[0:SS, 4, :]
                V.tensor_copy(cre, ps[0:SS, 6, 256 + 2 * SG:256 + 3 * SG])
                link(V.tensor_copy(cim, ps[0:SS, 6, 256 + 3 * SG:256 + 4 * SG]))
                link(V.tensor_scalar(phase[:, 1, :], phase[:, 0, :], ROUNDER / 4096.0, None, ALU.add))
                link(V.tensor_scalar(phase[:, 1, :], phase[:, 1, :], ROUNDER / 4096.0, None, ALU.subtract))
                link(V.tensor_tensor(phase[:, 2, :], phase[:, 0, :], phase[:, 1, :], ALU.subtract))
                link(V.tensor_tensor(g3(s5_t2), g3(s5_bi), bc(cim), ALU.mult))
                link(V.tensor_tensor(g3(s5_t0), g3(s5_br), bc(cre), ALU.mult))
                link(V.tensor_tensor(s5_t0[0:SS, :], s5_t0[0:SS, :], s5_t2[0:SS, :], ALU.subtract))

            def prep_bb_2():
                cre, cim = pre[0:SS, 3, :], pre[0:SS, 4, :]
                link(V.tensor_tensor(g3(s5_t2), g3(s5_br), bc(cim), ALU.mult))
                link(V.tensor_tensor(g3(s5_t1), g3(s5_bi), bc(cre), ALU.mult))
                V.tensor_tensor(s5_t1[0:SS, :], s5_t1[0:SS, :], s5_t2[0:SS, :], ALU.add).then_inc(S("s5_bb"), 1)
                link(V.tensor_scalar(int_p[:, 1:2], int_p[:, 0:1], SC, None, ALU.bitwise_and))
                link(V.tensor_scalar(even_odd[:, 0:1], int_p[:, 1:2], 0.0, None, ALU.is_equal))
                link(V.tensor_scalar(even_odd[:, 1:2], even_odd[:, 0:1], -1.0, 1.0, ALU.mult, ALU.add))

            def prep_maps(k):
                if k == 0:
                    dve.wait_ge(*nth("s5_bb_turned", 1))
                    for i in range(2):
                        for h in range(2):
                            src = ps[:, (0, 1, 6, 7)[2 * i + h], 256:512].rearrange("p (c n) -> p c n", c=4)
                            for eo in range(2):
                                V.tensor_scalar(maps[:, i, 4 * h:4 * h + 4, SS * eo:SS * eo + SS], src, even_odd[:, eo:eo + 1], None,
                                                ALU.mult)
                for n0 in range(4 * k, 4 * k + 4, 2):
                    for n in (n0, n0 + 1):
                        i, m = n // DC, n % DC
                        V.tensor_scalar(s5_cm[n % 2][:, 0:SS], s5_c[:, i, m, :], even_odd[:, 0:1], None, ALU.mult)
                        V.tensor_scalar(s5_cm[n % 2][:, SS:P], s5_c[:, i, m, :], even_odd[:, 1:2], None, ALU.mult)\
                            .then_inc(S("s5_cm"), 1)
                    for n in (n0, n0 + 1):
                        i, m = n // DC, n % DC
                        dve.wait_ge(*nth("s5_cm_turned", n + 1))
                        V.tensor_scalar(maps[:, 2 + i, m, :], ps[:, 6 + n % 2, P:2 * P], 1.0 if i == 0 else -1.0, None, ALU.mult)\
                            .then_inc(S("s5_cm_done"), 1)
                if k == 3:
                    dve.wait_ge(*nth("s5_cm_done", 2 * DC))
                    V.tensor_copy(int_p[:, 1:2], int_p[:, 0:1]).then_inc(S("maps_ready"), 1)

            def s5_constants(k):
                if k == 2:
                    prep_coef()
                if k == 3:
                    prep_coef_2()
                if k == 4:
                    prep_bb()
                if k == 5:
                    prep_bb_2()
                if k >= 6:
                    prep_maps(k - 6)

            def moe(l):
                blocks = ln_blocks[f"ffn{l}"]
                mix_norm(f"mix{l}", to_packed)
                route(l)

                def expert(n, b, pre_, xb, gb, yb):
                    dve.wait_ge(*nth(f"{pre_[0]}{l}", n + 1))
                    V.tensor_copy(xT[b].rearrange("p (q h) s -> p h q s", h=2),
                                  ps[:, xb, 0:256].rearrange("p (h s q) -> p h q s", h=2, q=4)).then_inc(S(f"{pre_[1]}{l}"), 1)
                    dve.wait_ge(*nth(f"{pre_[2]}{l}", n + 1))
                    V.tensor_tensor(hid[b], silu[b], ps[:, gb, P:2 * P], ALU.mult).then_inc(S(f"{pre_[3]}{l}"), 1)

                names_ = ("xs_turned", "xT_ready", "silu", "hid_ready")

                def pair(i, first, beside=None):
                    for b in range(2):
                        n = i * 2 + b
                        expert(n, b, names_, b, 2 + b, 4 + b)
                        dve.wait_ge(*nth(f"down{l}", n + 1))
                        if not first:
                            dve.wait_ge(*nth(f"y_stored{l}_{b}", i * 16))
                        V.tensor_copy(y_out[b], ps[:, 4 + b, 0:256]).then_inc(S(f"y_ready{l}"), 1)
                        if beside:
                            beside(n)

                pair(0, True)
                if l == 0:
                    for st in range(1, PREP_STEPS):
                        pair(st, False, s5_constants)
                with dve.Fori(PREP_STEPS if l == 0 else 1, NE // 2) as i:
                    pair(i, False)
                rounds = dve.value_load(rounds_i[0:1, l:l + 1], min_val=1, max_val=MAX_ROUNDS)
                with dve.If(rounds > 1):
                    with dve.Fori(1, rounds) as r:
                        with dve.Fori(0, NE) as e:
                            n = (r - 1) * NE + e
                            expert(n, 0, ("more_turned", "more_xT", "more_silu", "more_hid"), 0, 2, 4)
                            dve.wait_ge(*nth(f"more_used{l}", n + 1))
                            V.tensor_copy(y_out[0], ps[:, 4, 0:256]).then_inc(S(f"more_y{l}"), 1)
                dve.end_ifs()
                nb = len(blocks)
                for i, b in enumerate(blocks):
                    m = BLOCKS[b][1]
                    x = tmps[i % 2][0:m, :]
                    dve.wait_ge(*nth(f"gathered{l}_{i}", 32))
                    y1, y2 = (t[0:m, :] for t in expert_rows[i])
                    if i >= 2:
                        dve.wait_ge(*nth(f"ffn{l}_normed", i - 1))
                    link(V.tensor_scalar(x, y1, gates[0:m, i, 0:1], None, ALU.mult))
                    link(V.scalar_tensor_tensor(out=x, in0=y2, scalar=gates[0:m, i, 1:2], in1=x, op0=ALU.mult, op1=ALU.add))
                    link(V.scalar_tensor_tensor(out=two(x, DC), in0=unpacked(hres[0:m, b, :]), scalar=ALPHA, in1=two(x, DC),
                                                op0=ALU.mult, op1=ALU.add))
                    statistics(f"ffn{l}", i, b)
                    if i >= 1:
                        normalised(f"ffn{l}", i - 1, blocks[i - 1], plain)
                normalised(f"ffn{l}", nb - 1, blocks[nb - 1], plain)

            V.memset(eps_t[:, 0:1], LN_EPS)
            V.memset(eps_t[:, 1:2], math.pi / 2)
            V.memset(eps_t[:, 2:3], RMS_EPS)
            link(V.memset(lru_x[:, :, 0:PAD_A], 0.0))
            dve.wait_ge(*nth("par_turned", 1))
            V.tensor_copy(par[:, :, :], ps[:, 7, 0:12 * DC].rearrange("p (m v) -> p m v", v=12)).then_inc(S("par_ready"), 1)
            dve.wait_ge(*nth("par_ready", 1))
            lam = par[:, :, 7]
            V.tensor_scalar(soft[:, 3, :], lam, -1.0, 0.0, ALU.mult, ALU.max)
            link(V.tensor_scalar(soft[:, 0, :], lam, -1.0, None, ALU.mult))
            V.tensor_tensor(soft[:, 0, :], soft[:, 0, :], lam, ALU.max).then_inc(S("lam"), 1)
            dve.wait_ge(*nth("lam_exp", 1))
            link(V.tensor_scalar(soft[:, 0, :], soft[:, 1, :], 2.0, None, ALU.add))
            link(V.reciprocal(soft[:, 0, :], soft[:, 0, :]))
            link(V.tensor_tensor(soft[:, 0, :], soft[:, 0, :], soft[:, 1, :], ALU.mult))
            link(V.tensor_tensor(soft[:, 1, :], soft[:, 0, :], soft[:, 0, :], ALU.mult))
            link(V.tensor_scalar(soft[:, 2, :], soft[:, 1, :], 1.0 / 17, 1.0 / 15, ALU.mult, ALU.add))
            for c in (13, 11, 9, 7, 5, 3, 1):
                link(V.tensor_tensor(soft[:, 2, :], soft[:, 2, :], soft[:, 1, :], ALU.mult))
                link(V.tensor_scalar(soft[:, 2, :], soft[:, 2, :], 1.0 / c, None, ALU.add))
            link(V.tensor_tensor(soft[:, 2, :], soft[:, 2, :], soft[:, 0, :], ALU.mult))
            link(V.scalar_tensor_tensor(out=soft[:, 3, :], in0=soft[:, 2, :], scalar=2.0, in1=soft[:, 3, :], op0=ALU.mult, op1=ALU.add))
            V.tensor_scalar(soft[:, 4, :], soft[:, 3, :], 4.0, None, ALU.mult).then_inc(S("soft"), 1)

            def lru_decay(m):
                s, q = lru_r[:, m, :], lru_x[:, m, 0:T]
                dve.wait_ge(*nth("lru_tanh", m + 1))
                V.tensor_tensor(lru_i[:, m, :], lru_i[:, m, :], lru_c[:, m, :], ALU.mult)
                link(V.tensor_scalar(q, s, 1.0, None, ALU.add))
                link(V.reciprocal(q, q))

            def lru_scan(m):
                q, t = lru_x[:, m, 0:T], lru_q[:, m, :]
                link(V.tensor_tensor(t, t, q, ALU.mult))
                V.tensor_scalar(q, q, 2.0, -1.0, ALU.mult, ALU.add)
                link(V.scalar_tensor_tensor(out=t, in0=t, scalar=2.0, in1=lru_i[:, m, :], op0=ALU.mult, op1=ALU.mult))
                link(V.tensor_tensor_scan(lru_c[:, m, :], q, t, 0.0, ALU.mult, ALU.add))
                dve.wait_ge(*nth("lru_gelu", m // 4 + 1))
                V.tensor_tensor(lru_y[:, m, :], lru_y[:, m, :], lru_c[:, m, :], ALU.mult).then_inc(S("lru_z"), 1)

            for m in range(DC):
                dve.wait_ge(*nth("lru_evac", m + 1))
                link(V.tensor_scalar(lru_c[:, m, :], lru_x[:, m, 0:T], par[:, m, 0:1], par[:, m, 4:5], ALU.mult, ALU.add))
                for k in range(1, CONV_A):
                    ins = V.scalar_tensor_tensor(out=lru_c[:, m, :], in0=lru_x[:, m, k:k + T], scalar=par[:, m, k:k + 1],
                                                 in1=lru_c[:, m, :], op0=ALU.mult, op1=ALU.add)
                    if k < CONV_A - 1:
                        link(ins)
                ins.then_inc(S("lru_conv"), 1)
                dve.wait_ge(*nth("lru_conv", m + 1))
                if m >= 3:
                    lru_decay(m - 3)
            for m in range(DC - 3, DC):
                lru_decay(m)
            dve.wait_ge(*nth("lru_sqrt", 1))
            for m in range(DC):
                lru_scan(m)
            moe(0)

            def prep_turns(g):
                b = g % 2
                if g == 0:
                    dve.wait_ge(*nth("iota_t", 1))
                if g >= 2:
                    dve.wait_ge(*nth(f"rot_stored{b}", 16 * (g // 2)))
                f = rot[b][:, :, 1, :]
                for j in range(4):
                    ins = V.tensor_scalar(rot_k[:, j, :], iota_t, phase[:, 0, 4 * g + j:4 * g + j + 1], ROUNDER, ALU.mult, ALU.add)
                link(ins)
                link(V.tensor_scalar(rot_k, rot_k, ROUNDER, None, ALU.subtract))
                for j in range(4):
                    ins = V.scalar_tensor_tensor(out=f[:, j], in0=iota_t, scalar=phase[:, 1, 4 * g + j:4 * g + j + 1],
                                                 in1=rot_k[:, j, :], op0=ALU.mult, op1=ALU.subtract)
                link(ins)
                for j in range(4):
                    ins = V.scalar_tensor_tensor(out=f[:, j], in0=iota_t, scalar=phase[:, 2, 4 * g + j:4 * g + j + 1],
                                                 in1=f[:, j], op0=ALU.mult, op1=ALU.add)
                link(ins)
                V.tensor_scalar(f, f, 0.5, -0.5, ALU.min, ALU.max).then_inc(S("rot_turns"), 1)

            for m in range(DC):
                b = m % 2
                dve.wait_ge(*nth("sc_cg_out", m + 1))
                dve.wait_ge(*nth("sc_v", m + 1))
                V.tensor_tensor(sc_cv[b], sc_cg[b], ps[:, 3 + 3 * b, 0:TC], ALU.mult).then_inc(S("sc_gated"), 1)
                dve.wait_ge(*nth("sc_gated", m + 1))
                link(V.tensor_scalar(sc_a, sc_cv[b][:, 0:SEQ], par[:, m, 8:9], None, ALU.mult))
                for k in range(1, CONV_B):
                    link(V.scalar_tensor_tensor(out=sc_a, in0=sc_cv[b][:, k:k + SEQ], scalar=par[:, m, 8 + k:9 + k], in1=sc_a,
                                                op0=ALU.mult, op1=ALU.add))
                dve.wait_ge(*nth("sc_bg", m + 1))
                V.tensor_tensor(sc_z[:, m, :], sc_a, ps[:, 4 + 3 * b, 0:SEQ], ALU.mult).then_inc(S("sc_z"), 1)
                prep_turns(m)
            moe(1)

            def s5_rotate(s):
                b = s % 2
                name = f"s5_rot{s // 8}"
                if s % 8 == 0:
                    slot_wait(dve, name)
                dve.wait_ge(*nth("s5_bu", s + 1))
                if s >= 2:
                    dve.wait_ge(*nth("s5_v", s - 1))
                cs = ring[:, place[name], 512 * (s % 8):512 * (s % 8) + 512].rearrange("p (i n) -> p i n", i=2)
                bu = ps[:, s % 4, :].rearrange("p (i n) -> p i n", i=2)
                V.tensor_tensor(s5_p1[b], bu, cs[:, 0:1, :].to_broadcast([P, 2, SEQ]), ALU.mult)
                V.tensor_tensor(s5_p2[b], bu, cs[:, 1:2, :].to_broadcast([P, 2, SEQ]), ALU.mult).then_inc(S("s5_rotated"), 1)

            def s5_scan(s):
                b = s % 2
                name = f"s5_rot{s // 8}"
                dve.wait_ge(*nth("s5_v", s + 1))
                if s >= 2:
                    dve.wait_ge(*nth("s5_q2", s - 1))
                am = decay[:, s:s + 1].to_broadcast([P, SEQ])
                V.tensor_tensor_scan(s5_h[b][:, 0, :], am, s5_v[s % 3][:, 0, :], 0.0, ALU.mult, ALU.add)
                V.tensor_tensor_scan(s5_h[b][:, 1, :], am, s5_v[s % 3][:, 1, :], 0.0, ALU.mult, ALU.add).then_inc(S("s5_scanned"), 1)
                dve.wait_ge(*nth("s5_scanned", s + 1))
                if s >= 4:
                    dve.wait_ge(*nth("s5_summed", s - 3))
                cs = ring[:, place[name], 512 * (s % 8):512 * (s % 8) + 512].rearrange("p (i n) -> p i n", i=2)
                V.tensor_tensor(s5_q1[s % 4], s5_h[b], cs[:, 0:1, :].to_broadcast([P, 2, SEQ]), ALU.mult).then_inc(S("s5_q"), 1)

            def s5_skip(m):
                dve.wait_ge(*nth("s5_summed", 4 * m + 4))
                V.scalar_tensor_tensor(out=s5_y[:, m, :], in0=hT[:, m, NMETA:T], scalar=par[:, m, 11:12],
                                       in1=ps[:, 4 + m % 2, 0:SEQ], op0=ALU.mult, op1=ALU.add).then_inc(S("s5_y"), 1)

            for s in range(ST + 4):
                if s < ST:
                    s5_rotate(s)
                if 2 <= s < ST + 2:
                    s5_scan(s - 2)
                if s >= 7 and (s - 7) % 4 == 0:
                    s5_skip((s - 7) // 4)
            for m in range(DC):
                dve.wait_ge(*nth("glu_sig", m + 1))
                dve.wait_ge(*nth("s5_g", DC))
                V.tensor_tensor(s5_y[:, m, :], s5_sig[m % 2], ps[:, 2 * (m % 2), 0:SEQ], ALU.mult).then_inc(S("glu_done"), 1)
            mix_norm("s5")

            def mlp(layer):
                for c in range(DFF // P):
                    dve.wait_ge(*nth(f"ff_relu{layer}", c + 1))
                    V.tensor_tensor(ff[:, c, :], ff[:, c, :], ff[:, c, :], ALU.mult).then_inc(S(f"ff_sq{layer}"), 1)
                mix_norm(f"mlp{layer}")

            mlp(0)
            dve.wait_ge(*nth("pos_loaded", 32))
            dve.wait_ge(*nth("attn_bc", 3))
            link(V.tensor_copy(pos_f[:, :], pos_i[:, :]))
            for b in range(2):
                link(V.tensor_scalar(ang[:, b, :], inv_f, pos_f[:, b:b + 1], None, ALU.mult))
            link(V.tensor_scalar(angk, ang, 1.0 / TWO_PI, ROUNDER, ALU.mult, ALU.add))
            link(V.tensor_scalar(angk, angk, ROUNDER, None, ALU.subtract))
            for c in (PI2_A, PI2_B, PI2_C):
                link(V.scalar_tensor_tensor(out=ang, in0=angk, scalar=-c, in1=ang, op0=ALU.mult, op1=ALU.add))
            V.tensor_scalar(ang, ang, PI_IN, -PI_IN, ALU.min, ALU.max).then_inc(S("angles"), 1)

            def rotate(x, dst, nh, b):
                h = ROPE // 2
                c = cos_t[:, b:b + 1, :].to_broadcast([P, nh, h])
                s = sin_t[:, b:b + 1, :].to_broadcast([P, nh, h])
                u = [rope_u[:, 256 * i:256 * i + nh * h].rearrange("p (g n) -> p g n", g=nh) for i in range(2)]
                V.tensor_tensor(u[0], x[:, :, 0:h], c, ALU.mult)
                link(V.tensor_tensor(u[1], x[:, :, h:ROPE], s, ALU.mult))
                link(V.tensor_tensor(dst[:, :, 0:h], u[0], u[1], ALU.subtract))
                V.tensor_tensor(u[0], x[:, :, 0:h], s, ALU.mult)
                link(V.tensor_tensor(u[1], x[:, :, h:ROPE], c, ALU.mult))
                return V.tensor_tensor(dst[:, :, h:ROPE], u[0], u[1], ALU.add)

            dve.wait_ge(*nth("latent_rms", 2))
            dve.wait_ge(*nth("latent_out", 4))
            link(V.reciprocal(sq_sum[:, 8:12], sq_sum[:, 4:8]))
            for i, (x, n, g, sem_) in enumerate(((ckv, KVL, g_kv, "kv_normed"), (cq, QL, g_q, "q_normed"))):
                for b in range(2):
                    V.scalar_tensor_tensor(out=x[:, b, 0:n], in0=x[:, b, 0:n], scalar=sq_sum[:, 8 + 2 * i + b:9 + 2 * i + b],
                                           in1=g, op0=ALU.mult, op1=ALU.mult).then_inc(S(sem_), 1)
            dve.wait_ge(*nth("a_tab", 3))
            for b in range(2):
                link(rotate(ckv[:, b:b + 1, KVL:KVL + ROPE], kr2[:, b, 0:1, :], 1, b))
                V.tensor_copy(kr2[:, b, 1, :], kr2[:, b, 0, :]).then_inc(S("k_rotated"), 1)
            for j in range(4):
                dve.wait_ge(*nth("values", j + 1))
                b, hh = j // 2, j % 2
                V.tensor_copy(val[:, b, 512 * hh:512 * hh + 512], ps[:, (7, 0, 1, 6)[j], :]).then_inc(S("values_out"), 1)
            for b in range(2):
                dve.wait_ge(*nth("q_rope", b + 1))
                src = ps[:, (7, 0)[b], :].rearrange("p (h n) -> p h n", h=HEADS)
                rotate(src, qr_rot_b[b], HEADS, b).then_inc(S("q_rotated"), 1)
                dve.wait_ge(*nth("q_rotated", b + 1))
            dve.wait_ge(*nth("attn_left", 1))

            def mask_and_max(u):
                b = u % 2
                n = P * (b + 1)
                dve.wait_ge(*nth("scores", u + 1))
                if u >= 4:
                    dve.wait_ge(*nth("prob_turned", u - 3))
                x = prob[u % 4]
                sc = ps[:, (2 + u % 4) % 4, :]
                d_ = slice(P * b, P * b + P)
                if b == 1:
                    V.tensor_scalar(x[:, 0:P], sc[:, 0:P], SM_SCALE, None, ALU.mult)
                link(V.scalar_tensor_tensor(out=x[:, d_], in0=sc[:, d_], scalar=SM_SCALE, in1=causal, op0=ALU.mult, op1=ALU.add))
                V.tensor_reduce(sq_sum[:, 16 + u:17 + u], x[:, 0:n], AX.X, ALU.max, negate=True).then_inc(S("score_max"), 1)

            def normalise(u):
                b = u % 2
                n = P * (b + 1)
                dve.wait_ge(*nth("prob_exp", u + 1))
                link(V.reciprocal(sq_sum[:, 32 + u:33 + u], sq_sum[:, 32 + u:33 + u]))
                V.tensor_scalar(prob[u % 4][:, 0:n], prob[u % 4][:, 0:n], sq_sum[:, 32 + u:33 + u], None, ALU.mult).then_inc(S("prob_normed"), 1)

            causal = region(12416 + 512, P)
            link(V.tensor_scalar(causal, before[:, :], -BIG, None, ALU.mult))
            for u in range(2 * HEADS + 5):
                if u < 2 * HEADS:
                    mask_and_max(u)
                if 2 <= u < 2 * HEADS + 2:
                    normalise(u - 2)
                if u >= 6 and u % 2 == 0:
                    h = (u - 6) // 2
                    dve.wait_ge(*nth("weighed", h + 1))
                    V.tensor_copy(oT[:, h, :], ps[:, 6 + h % 2, 0:SEQ]).then_inc(S("oT"), 1)
            mix_norm("mla")
            mlp(1)



def kernel(**inputs):
    import numpy as _np
    import concourse.bacc as _bacc
    from concourse import mybir as _mybir
    from concourse.bass_utils import run_bass_kernel_spmd as _run

    nc = _bacc.Bacc("TRN2", target_bir_lowering=False, num_devices=1)
    arrays, args = {}, {}
    for name, value in inputs.items():
        v = _np.ascontiguousarray(value)
        arrays[f"in_{name}"] = v
        args[name] = nc.dram_tensor(f"in_{name}", v.shape, _mybir.dt.from_np(v.dtype), kind="ExternalInput").ap()
    freq = _np.array([10000.0 ** (-i / 32) for i in range(32)], _np.float32)
    arrays["const_inv_freq"] = freq
    args["inv_freq"] = nc.dram_tensor("const_inv_freq", freq.shape, F32, kind="ExternalInput").ap()
    out = nc.dram_tensor("out_0", (1, SEQ, D), F32, kind="ExternalOutput").ap()
    first_and_second_block(nc, args, out)
    r = _run(nc, [arrays], core_ids=[0])
    return r.results[0]["out_0"]
```
